# Optimizing a Trainium2 kernel written in Bass

```python
import jax, jax.numpy as jnp
from jax import lax
import numpy as np

D_MODEL = 1024
BATCH = 1
SEQ = 512
DEPTH = 2

F_WIDTH = D_MODEL
F_GROUP_DIM = 128
F_GROUPS = F_WIDTH // F_GROUP_DIM
RET_HEADS = 4
RET_DK = D_MODEL // RET_HEADS
RET_DV = D_MODEL // RET_HEADS
RET_QK = RET_HEADS * RET_DK
RET_V = RET_HEADS * RET_DV
CHUNK = 128
ROPE_BASE = 10000.0
DECAY_OFFSET_FWD = 0.0
DECAY_OFFSET_BWD = 0.5
D_FF = 2816
CONV_WIDTH = 3
N_MOD = 6
EPS = 1e-6
IN_SIZES = (F_WIDTH, RET_QK, RET_QK, RET_V, RET_V, D_MODEL, D_MODEL)
D_IN = F_WIDTH + 2 * RET_QK + 2 * RET_V + 2 * D_MODEL


def rmsnorm(x, g):
    xf = x.astype(jnp.float32)
    y = xf * lax.rsqrt(jnp.mean(xf * xf, axis=-1, keepdims=True) + EPS)
    return (y * g.astype(jnp.float32)).astype(x.dtype)

def decay_logs(offset):
    expo = -(5.0 + offset) - jnp.arange(RET_HEADS, dtype=jnp.float32)
    return jnp.log1p(-jnp.exp2(expo))

def fourier_mix(u):
    B, S, _ = u.shape
    ug = u.astype(jnp.float32).reshape(B, S, F_GROUPS, F_GROUP_DIM)
    y = jnp.fft.fft2(ug, axes=(1, 3), norm='ortho').real
    return y.reshape(B, S, F_WIDTH).astype(u.dtype)

def rotary(t):
    S = t.shape[1]
    half = t.shape[-1] // 2
    inv_freq = ROPE_BASE ** (-jnp.arange(half, dtype=jnp.float32) / half)
    ang = jnp.arange(S, dtype=jnp.float32)[:, None] * inv_freq[None, :]
    cos = jnp.cos(ang)[None, :, None, :]
    sin = jnp.sin(ang)[None, :, None, :]
    t1, t2 = t[..., :half], t[..., half:]
    return jnp.concatenate([t1 * cos - t2 * sin, t1 * sin + t2 * cos], axis=-1)

def chunk_retention(q, k, v, log_gamma, strict):
    B, H, S, dk = q.shape
    dv = v.shape[-1]
    n_chunks = S // CHUNK
    qc = q.reshape(B, H, n_chunks, CHUNK, dk)
    kc = k.reshape(B, H, n_chunks, CHUNK, dk)
    vc = v.reshape(B, H, n_chunks, CHUNK, dv)
    j = jnp.arange(CHUNK, dtype=jnp.float32)
    diff = j[:, None] - j[None, :]
    keep = (diff > 0) if strict else (diff >= 0)
    dmask = jnp.where(keep[None], jnp.exp(log_gamma[:, None, None] * jnp.maximum(diff, 0.0)[None]), 0.0)
    scores = jnp.einsum('bhncd,bhnld->bhncl', qc, kc) * dmask[None, :, None]
    intra = jnp.einsum('bhncl,bhnle->bhnce', scores, vc)
    q_decay = jnp.exp(log_gamma[:, None] * (j + 1.0))[None, :, :, None]
    k_decay = jnp.exp(log_gamma[:, None] * (CHUNK - 1.0 - j))[None, :, :, None]
    chunk_decay = jnp.exp(log_gamma * CHUNK)[None, :, None, None]

    def step(state, xs):
        qi, ki, vi = xs
        cross = jnp.einsum('bhcd,bhde->bhce', qi, state) * q_decay
        state = state * chunk_decay + jnp.einsum('bhcd,bhce->bhde', ki * k_decay, vi)
        return state, cross

    state0 = jnp.zeros((B, H, dk, dv), jnp.float32)
    xs = (jnp.moveaxis(qc, 2, 0), jnp.moveaxis(kc, 2, 0), jnp.moveaxis(vc, 2, 0))
    _, cross = lax.scan(step, state0, xs)
    out = intra + jnp.moveaxis(cross, 0, 2)
    return out.reshape(B, H, S, dv)

def retention_branch(q, k, v, g):
    B, S, _ = q.shape
    dt = q.dtype
    qh = rotary(q.astype(jnp.float32).reshape(B, S, RET_HEADS, RET_DK)) * (RET_DK ** -0.5)
    kh = rotary(k.astype(jnp.float32).reshape(B, S, RET_HEADS, RET_DK))
    vh = v.astype(jnp.float32).reshape(B, S, RET_HEADS, RET_DV)
    qh = jnp.transpose(qh, (0, 2, 1, 3))
    kh = jnp.transpose(kh, (0, 2, 1, 3))
    vh = jnp.transpose(vh, (0, 2, 1, 3))
    fwd = chunk_retention(qh, kh, vh, decay_logs(DECAY_OFFSET_FWD), strict=False)
    bwd = jnp.flip(chunk_retention(jnp.flip(qh, axis=2), jnp.flip(kh, axis=2), jnp.flip(vh, axis=2),
                                   decay_logs(DECAY_OFFSET_BWD), strict=True), axis=2)
    y = jnp.transpose(fwd + bwd, (0, 2, 1, 3))
    mu = jnp.mean(y, axis=-1, keepdims=True)
    var = jnp.mean(jnp.square(y - mu), axis=-1, keepdims=True)
    y = (y - mu) * lax.rsqrt(var + EPS)
    y = y.reshape(B, S, RET_V) * jax.nn.silu(g.astype(jnp.float32))
    return y.astype(dt)

def token_mix(h, w_in, w_fourier, w_ret, w_out):
    proj = h @ w_in
    offsets = np.cumsum(IN_SIZES)[:-1].tolist()
    u_f, q, k, v, g, a_f, a_r = jnp.split(proj, offsets, axis=-1)
    y_f = fourier_mix(u_f) @ w_fourier
    y_r = retention_branch(q, k, v, g) @ w_ret
    merged = jax.nn.sigmoid(a_f) * y_f + jax.nn.sigmoid(a_r) * y_r
    return merged @ w_out

def conv_ffn(h, w_up, conv_w, conv_b, w_down):
    S = h.shape[1]
    u = h @ w_up
    pad = CONV_WIDTH // 2
    up = jnp.pad(u, ((0, 0), (pad, pad), (0, 0)))
    u = sum(up[:, i:i + S] * conv_w[i] for i in range(CONV_WIDTH)) + conv_b
    a, b = jnp.split(u, 2, axis=-1)
    return (jax.nn.gelu(a, approximate=False) * b) @ w_down

def first_inputs(seed: int = 0) -> dict:
    key = jax.random.key(seed)
    ks = jax.random.split(key, 15)

    def nrm(k, shape, scale):
        return jax.random.normal(k, shape, jnp.float32) * scale

    return {
        'x': nrm(ks[0], (BATCH, SEQ, D_MODEL), 1.0),
        'c': nrm(ks[1], (BATCH, D_MODEL), 1.0),
        'norm1_g': 1.0 + nrm(ks[2], (DEPTH, D_MODEL), 0.02),
        'norm2_g': 1.0 + nrm(ks[3], (DEPTH, D_MODEL), 0.02),
        'ada_w': nrm(ks[4], (DEPTH, D_MODEL, N_MOD * D_MODEL), 0.5 * D_MODEL ** -0.5),
        'ada_b': nrm(ks[5], (DEPTH, N_MOD * D_MODEL), 0.02),
        'w_in': nrm(ks[6], (DEPTH, D_MODEL, D_IN), D_MODEL ** -0.5),
        'w_fourier': nrm(ks[7], (DEPTH, F_WIDTH, D_MODEL), F_WIDTH ** -0.5),
        'w_ret': nrm(ks[8], (DEPTH, RET_V, D_MODEL), RET_V ** -0.5),
        'w_out': nrm(ks[9], (DEPTH, D_MODEL, D_MODEL), D_MODEL ** -0.5),
        'ffn_up': nrm(ks[10], (DEPTH, D_MODEL, 2 * D_FF), D_MODEL ** -0.5),
        'conv_w': nrm(ks[11], (DEPTH, CONV_WIDTH, 2 * D_FF), CONV_WIDTH ** -0.5),
        'conv_b': nrm(ks[12], (DEPTH, 2 * D_FF), 0.02),
        'ffn_down': nrm(ks[13], (DEPTH, D_FF, D_MODEL), D_FF ** -0.5),
        'final_g': 1.0 + nrm(ks[14], (D_MODEL,), 0.02),
    }

def first_block(x, c, norm1_g, norm2_g, ada_w, ada_b, w_in, w_fourier, w_ret, w_out,
              ffn_up, conv_w, conv_b, ffn_down, final_g):
    c_act = jax.nn.silu(c)
    for l in range(DEPTH):
        mod = (c_act @ ada_w[l] + ada_b[l])[:, None, :]
        sh1, sc1, g1, sh2, sc2, g2 = jnp.split(mod, N_MOD, axis=-1)
        h = rmsnorm(x, norm1_g[l]) * (1.0 + sc1) + sh1
        x = x + g1 * token_mix(h, w_in[l], w_fourier[l], w_ret[l], w_out[l])
        h = rmsnorm(x, norm2_g[l]) * (1.0 + sc2) + sh2
        x = x + g2 * conv_ffn(h, ffn_up[l], conv_w[l], conv_b[l], ffn_down[l])
    return rmsnorm(x, final_g)


DEPTH_2 = 1

CTX_LEN = 256
GRID_W = 64
N_MOD_2 = 9
M_HEADS = 4
M_HD = 128
M_W = M_HEADS * M_HD
CONV_W = 3
POOL_WINDOWS = (2, 4, 8, 16)
POOL_GROUPS = len(POOL_WINDOWS)
POOL_W = 512
POOL_GW = POOL_W // POOL_GROUPS
MIX_W = M_W + POOL_W
M_COLS = 3 * M_W + 4 * M_HEADS
IN_COLS = M_COLS + POOL_W


def rmsnorm_2(x, g):
    xf = x.astype(jnp.float32)
    y = xf * lax.rsqrt(jnp.mean(xf * xf, axis=-1, keepdims=True) + EPS)
    return (y * g.astype(jnp.float32)).astype(x.dtype)

def ada_in(x, mod, j, g):
    return rmsnorm_2(x, g) * (1 + mod[:, 3 * j + 1, None]) + mod[:, 3 * j, None]

def ada_out(x, z, mod, j, g, res_w):
    return x + res_w * mod[:, 3 * j + 2, None] * rmsnorm_2(z, g)

def swiglu(y, w_in, w_out):
    a, b = jnp.split(y @ w_in, 2, axis=-1)
    return (jax.nn.silu(a) * b) @ w_out

def centred_mean(u, win, axis):
    n = u.shape[axis]
    lo, hi = win // 2, win - 1 - win // 2
    pad = [(0, 0)] * u.ndim
    pad[axis] = (lo + 1, hi)
    s = jnp.cumsum(jnp.pad(u.astype(jnp.float32), pad), axis=axis)
    tot = lax.slice_in_dim(s, win, win + n, axis=axis) - lax.slice_in_dim(s, 0, n, axis=axis)
    t = jnp.arange(n)
    cnt = (jnp.minimum(t + hi, n - 1) - jnp.maximum(t - lo, 0) + 1).astype(jnp.float32)
    shape = [1] * u.ndim
    shape[axis] = n
    return (tot / cnt.reshape(shape)).astype(u.dtype)

def pool_mixer(u, w_pool, pool_scale, on_grid):
    bsz, n, _ = u.shape
    outs = []
    for gi, win in enumerate(POOL_WINDOWS):
        ug = u[..., gi * POOL_GW:(gi + 1) * POOL_GW]
        if on_grid:
            rows = n // GRID_W
            ug2 = ug.reshape(bsz, rows, GRID_W, POOL_GW)
            pg = centred_mean(centred_mean(ug2, win, 2), win, 1).reshape(bsz, n, POOL_GW)
        else:
            pg = centred_mean(ug, win, 1)
        outs.append(pg - ug)
    d = jnp.stack(outs, axis=2)
    y = jnp.einsum('bngc,gcd->bngd', d, w_pool).reshape(bsz, n, POOL_W)
    return y * pool_scale

def short_conv(u, w, b):
    n = u.shape[1]
    h = CONV_W // 2
    up = jnp.pad(u, ((0, 0), (h, h), (0, 0)))
    out = b
    for j in range(CONV_W):
        out = out + up[:, j:j + n] * w[j]
    return out

def mlstm_inputs(p, conv_w, conv_b, w_q, w_k, i_bias, f_bias):
    bsz, n, _ = p.shape
    u = jax.nn.silu(short_conv(p[..., :M_W], conv_w, conv_b)).reshape(bsz, n, M_HEADS, M_HD)
    q = jnp.einsum('bnhd,hde->bhne', u, w_q).astype(jnp.float32)
    k = jnp.einsum('bnhd,hde->bhne', u, w_k).astype(jnp.float32)
    v = p[..., M_W:2 * M_W].reshape(bsz, n, M_HEADS, M_HD).transpose(0, 2, 1, 3).astype(jnp.float32)
    g0 = 3 * M_W
    ig = (p[..., g0:g0 + 2 * M_HEADS].reshape(bsz, n, 2, M_HEADS) + i_bias).astype(jnp.float32)
    fg = (p[..., g0 + 2 * M_HEADS:M_COLS].reshape(bsz, n, 2, M_HEADS) + f_bias).astype(jnp.float32)
    return q, k, v, ig.transpose(2, 0, 3, 1), fg.transpose(2, 0, 3, 1)

def mlstm_chunkwise(q, k, v, i_pre, f_pre):
    bsz, nh, t_len, dk = q.shape
    nc = t_len // CHUNK
    q = q.reshape(bsz, nh, nc, CHUNK, dk)
    k = k.reshape(bsz, nh, nc, CHUNK, dk) * (dk ** -0.5)
    v = v.reshape(bsz, nh, nc, CHUNK, dk)
    ip = i_pre.reshape(bsz, nh, nc, CHUNK)
    b = jnp.cumsum(jax.nn.log_sigmoid(f_pre).reshape(bsz, nh, nc, CHUNK), axis=-1)
    g = b[..., -1]
    a = g[..., None] - b + ip
    m_loc = jnp.max(a, axis=-1)
    wk = jnp.exp(a - m_loc[..., None])[..., None] * k
    ckv = jnp.einsum('bhclk,bhclv->bhckv', wk, v)
    cn = jnp.sum(wk, axis=3)

    def step(carry, inp):
        c_st, n_st, m_st = carry
        g_c, m_c, ckv_c, cn_c = inp
        m_new = jnp.maximum(g_c + m_st, m_c)
        a_old = jnp.exp(g_c + m_st - m_new)
        a_new = jnp.exp(m_c - m_new)
        c_new = a_old[..., None, None] * c_st + a_new[..., None, None] * ckv_c
        n_new = a_old[..., None] * n_st + a_new[..., None] * cn_c
        return (c_new, n_new, m_new), (c_st, n_st, m_st)

    init = (jnp.zeros((bsz, nh, dk, dk), jnp.float32), jnp.zeros((bsz, nh, dk), jnp.float32),
            jnp.zeros((bsz, nh), jnp.float32))
    xs = (jnp.moveaxis(g, -1, 0), jnp.moveaxis(m_loc, -1, 0), jnp.moveaxis(ckv, 2, 0), jnp.moveaxis(cn, 2, 0))
    _, (c_in, n_in, m_in) = lax.scan(step, init, xs)
    c_in = jnp.moveaxis(c_in, 0, 2)
    n_in = jnp.moveaxis(n_in, 0, 2)
    m_in = jnp.moveaxis(m_in, 0, -1)
    mask = jnp.tril(jnp.ones((CHUNK, CHUNK), dtype=bool))
    dmat = jnp.where(mask, b[..., :, None] - b[..., None, :] + ip[..., None, :], -jnp.inf)
    inter = b + m_in[..., None]
    m_t = jnp.maximum(jnp.max(dmat, axis=-1), inter)
    s = jnp.einsum('bhctk,bhcsk->bhcts', q, k) * jnp.exp(dmat - m_t[..., None])
    w_inter = jnp.exp(inter - m_t)
    num = w_inter[..., None] * jnp.einsum('bhctk,bhckv->bhctv', q, c_in) + jnp.einsum('bhcts,bhcsv->bhctv', s, v)
    den = w_inter * jnp.einsum('bhctk,bhck->bhct', q, n_in) + jnp.sum(s, axis=-1)
    h = num / jnp.maximum(jnp.abs(den), jnp.exp(-m_t))[..., None]
    return h.reshape(bsz, nh, t_len, dk)

def mlstm_bidir(p_lat, p_ctx, conv_w, conv_b, w_q, w_k, i_bias, f_bias):
    ql, kl, vl, il, fl = mlstm_inputs(p_lat, conv_w, conv_b, w_q, w_k, i_bias, f_bias)
    qc, kc, vc, ic, fc = mlstm_inputs(p_ctx, conv_w, conv_b, w_q, w_k, i_bias, f_bias)
    lc = qc.shape[2]
    cat = lambda a, b: jnp.concatenate([a, b], axis=2)
    rev = lambda a: jnp.flip(a, axis=2)
    h_f = mlstm_chunkwise(cat(qc, ql), cat(kc, kl), cat(vc, vl), cat(ic[0], il[0]), cat(fc[0], fl[0]))
    h_b = mlstm_chunkwise(cat(rev(qc), rev(ql)), cat(rev(kc), rev(kl)), cat(rev(vc), rev(vl)),
                          cat(rev(ic[1]), rev(il[1])), cat(rev(fc[1]), rev(fl[1])))
    h_lat = h_f[:, :, lc:] + rev(h_b[:, :, lc:])
    h_ctx = h_f[:, :, :lc] + rev(h_b[:, :, :lc])
    return h_lat, h_ctx

def mlstm_out(h, o, g):
    bsz, _, n, _ = h.shape
    h = h.transpose(0, 2, 1, 3)
    h = h * lax.rsqrt(jnp.mean(h * h, axis=-1, keepdims=True) + EPS) * g.reshape(M_HEADS, M_HD).astype(jnp.float32)
    return (h.reshape(bsz, n, M_W) * jax.nn.sigmoid(o.astype(jnp.float32))).astype(o.dtype)

def second_inputs(seed: int = 0) -> dict:
    key = jax.random.key(seed)
    ks = jax.random.split(key, 24)
    nrm = lambda k, shape, s: jax.random.normal(k, shape, jnp.float32) * s
    f_base = jnp.linspace(3.0, 6.0, M_HEADS, dtype=jnp.float32)
    return {
        'x': nrm(ks[0], (BATCH, SEQ, D_MODEL), 1.0),
        'c': nrm(ks[1], (BATCH, D_MODEL), 1.0),
        'ctx': nrm(ks[2], (BATCH, CTX_LEN, D_MODEL), 1.0),
        'c_ctx': nrm(ks[3], (D_MODEL,), 1.0),
        'w_mod': nrm(ks[4], (DEPTH_2, D_MODEL, N_MOD_2 * D_MODEL), D_MODEL ** -0.5),
        'b_mod': nrm(ks[5], (DEPTH_2, N_MOD_2 * D_MODEL), 0.02),
        'norm_pre': 1.0 + nrm(ks[6], (DEPTH_2, 3, D_MODEL), 0.05),
        'norm_post': 1.0 + nrm(ks[7], (DEPTH_2, 3, D_MODEL), 0.05),
        'ffn_w_in': nrm(ks[8], (DEPTH_2, 2, D_MODEL, 2 * D_FF), D_MODEL ** -0.5),
        'ffn_w_out': nrm(ks[9], (DEPTH_2, 2, D_FF, D_MODEL), D_FF ** -0.5),
        'w_in': nrm(ks[10], (DEPTH_2, D_MODEL, IN_COLS), D_MODEL ** -0.5),
        'w_out': nrm(ks[11], (DEPTH_2, MIX_W, D_MODEL), MIX_W ** -0.5),
        'conv_w': nrm(ks[12], (DEPTH_2, CONV_W, M_W), CONV_W ** -0.5),
        'conv_b': nrm(ks[13], (DEPTH_2, M_W), 0.02),
        'w_q': nrm(ks[14], (DEPTH_2, M_HEADS, M_HD, M_HD), M_HD ** -0.5),
        'w_k': nrm(ks[15], (DEPTH_2, M_HEADS, M_HD, M_HD), M_HD ** -0.5),
        'i_bias': nrm(ks[16], (DEPTH_2, 2, M_HEADS), 0.1),
        'f_bias': f_base + nrm(ks[17], (DEPTH_2, 2, M_HEADS), 0.1),
        'head_norm': 1.0 + nrm(ks[18], (DEPTH_2, M_W), 0.05),
        'pool_w': nrm(ks[19], (DEPTH_2, POOL_GROUPS, POOL_GW, POOL_GW), POOL_GW ** -0.5),
        'pool_scale': 1.0 + nrm(ks[20], (DEPTH_2, POOL_W), 0.1),
    }

def second_block(x, c, ctx, c_ctx, w_mod, b_mod, norm_pre, norm_post, ffn_w_in, ffn_w_out, w_in, w_out,
              conv_w, conv_b, w_q, w_k, i_bias, f_bias, head_norm, pool_w, pool_scale):
    sc = jax.nn.silu(c)
    scc = jax.nn.silu(c_ctx)[None]
    xc = ctx
    for l in range(DEPTH_2):
        ctx_out = l < DEPTH_2 - 1
        mod = (sc @ w_mod[l] + b_mod[l]).reshape(-1, N_MOD_2, D_MODEL)
        modc = (scc @ w_mod[l] + b_mod[l]).reshape(1, N_MOD_2, D_MODEL)
        x = ada_out(x, swiglu(ada_in(x, mod, 0, norm_pre[l, 0]), ffn_w_in[l, 0], ffn_w_out[l, 0]),
                    mod, 0, norm_post[l, 0], 0.5)
        xc = ada_out(xc, swiglu(ada_in(xc, modc, 0, norm_pre[l, 0]), ffn_w_in[l, 0], ffn_w_out[l, 0]),
                     modc, 0, norm_post[l, 0], 0.5)
        p = ada_in(x, mod, 1, norm_pre[l, 1]) @ w_in[l]
        pc = ada_in(xc, modc, 1, norm_pre[l, 1]) @ (w_in[l] if ctx_out else w_in[l, :, :M_COLS])
        h_lat, h_ctx = mlstm_bidir(p[..., :M_COLS], pc[..., :M_COLS], conv_w[l], conv_b[l],
                                   w_q[l], w_k[l], i_bias[l], f_bias[l])
        mix = jnp.concatenate([mlstm_out(h_lat, p[..., 2 * M_W:3 * M_W], head_norm[l]),
                               pool_mixer(p[..., M_COLS:], pool_w[l], pool_scale[l], True)], axis=-1)
        x = ada_out(x, mix @ w_out[l], mod, 1, norm_post[l, 1], 1.0)
        if ctx_out:
            mixc = jnp.concatenate([mlstm_out(h_ctx, pc[..., 2 * M_W:3 * M_W], head_norm[l]),
                                    pool_mixer(pc[..., M_COLS:], pool_w[l], pool_scale[l], False)], axis=-1)
            xc = ada_out(xc, mixc @ w_out[l], modc, 1, norm_post[l, 1], 1.0)
        x = ada_out(x, swiglu(ada_in(x, mod, 2, norm_pre[l, 2]), ffn_w_in[l, 1], ffn_w_out[l, 1]),
                    mod, 2, norm_post[l, 2], 0.5)
        if ctx_out:
            xc = ada_out(xc, swiglu(ada_in(xc, modc, 2, norm_pre[l, 2]), ffn_w_in[l, 1], ffn_w_out[l, 1]),
                         modc, 2, norm_post[l, 2], 0.5)
    return x


def setup_inputs(seed=0):
    out = dict(first_inputs(seed))
    for name, value in second_inputs(seed + 1).items():
        if name != "x":
            out[name + "_2"] = value
    return out


def reference(
    x, c, norm1_g, norm2_g, ada_w, ada_b, w_in, w_fourier, w_ret, w_out, ffn_up, conv_w, conv_b,
    ffn_down, final_g, c_2, ctx_2, c_ctx_2, w_mod_2, b_mod_2, norm_pre_2, norm_post_2,
    ffn_w_in_2, ffn_w_out_2, w_in_2, w_out_2, conv_w_2, conv_b_2, w_q_2, w_k_2, i_bias_2,
    f_bias_2, head_norm_2, pool_w_2, pool_scale_2,
):
    x = first_block(
        x, c, norm1_g, norm2_g, ada_w, ada_b, w_in, w_fourier, w_ret, w_out, ffn_up, conv_w,
        conv_b, ffn_down, final_g,
    )
    return second_block(
        x, c_2, ctx_2, c_ctx_2, w_mod_2, b_mod_2, norm_pre_2, norm_post_2, ffn_w_in_2,
        ffn_w_out_2, w_in_2, w_out_2, conv_w_2, conv_b_2, w_q_2, w_k_2, i_bias_2, f_bias_2,
        head_norm_2, pool_w_2, pool_scale_2,
    )


_drawn_inputs = setup_inputs


def setup_inputs(seed=0):
    import zlib

    import numpy as np

    out = dict(_drawn_inputs(seed))
    spreads = {}
    factors = {'norm1_g': 6.387,
     'norm2_g': 5.009,
     'conv_b': 5.343,
     'conv_b_2': 3.691,
     'i_bias_2': 8.0,
     'head_norm_2': 4.978}
    for name, (base, spread) in spreads.items():
        noise = np.random.default_rng([zlib.crc32(name.encode()), seed]).standard_normal(out[name].shape)
        drawn = base * np.exp(spread * noise) if base else spread * noise
        out[name] = __import__('jax').numpy.asarray(drawn.astype(out[name].dtype))
    for name, factor in factors.items():
        out[name] = (out[name] * factor).astype(out[name].dtype)
    return out
```

```python
from contextlib import ExitStack

import numpy as np

import concourse.bass as bass
from concourse import mybir

F32 = mybir.dt.float32
F32R = mybir.dt.float32r
ALU = mybir.AluOpType
ACT = mybir.ActivationFunctionType

S = 512
C = 256
D = 1024
DT = 8
FF = 2816
NH = 4
EPS = 1e-6
GATE_ROWS = 36
NS = 4
NW = 3
AHEAD = 2
NSLOT = 19


class Queue:

    def __init__(self, sem):
        self.sem = sem
        self.count = 0
        self.ops = []
        self.seen = {}

    def wait(self, *tokens):
        for token in tokens:
            if token is None:
                continue
            sem, value = token
            if self.seen.get(id(sem), 0) < value:
                self.seen[id(sem)] = value
                self.ops.append(lambda e, s=sem, v=value: e.wait_ge(s, v))

    def do(self, fn, *waits):
        self.wait(*waits)
        self.count += 1
        self.ops.append(lambda e, f=fn, s=self.sem: f(e).then_inc(s, 1))
        return (self.sem, self.count)

    def quiet(self, fn, *waits):
        self.wait(*waits)
        self.ops.append(fn)

    def run(self, e):
        for op in self.ops:
            op(e)


PCOLS = {}
_at = 0
for _name, _n in [("c", 8), ("c2", 16), ("n1", 16), ("n2", 16), ("adab", 96), ("fing", 8), ("bmod", 144),
                  ("npre", 24), ("npost", 24), ("cw", 264), ("cb", 88), ("cw2", 12), ("cb2", 4),
                  ("hn", 4), ("ps", 4), ("ib", 1), ("fb", 1)]:
    PCOLS[_name] = _at
    _at += _n
NP = _at


def program(nc, ws, xT, cT, params, consts, sel_d, out, chunks, dry):
    nch = len(chunks)
    ctx = ExitStack()
    with ctx:
        def sem(name):
            return ctx.enter_context(nc.semaphore(name))

        def sb(name, shape, dt=F32, stack=None):
            return (stack or ctx).enter_context(nc.sbuf_tensor(name, shape, dt))

        pe, act, dve, pool, sp = (Queue(sem(f"s_{n}")) for n in ("pe", "act", "dve", "pool", "sp"))
        s_ws = [sem(f"s_ws{i}") for i in range(NS)]
        s_par, s_con, s_x, s_rope, s_out = (sem(n) for n in ("s_par", "s_con", "s_x", "s_rope", "s_out"))
        s_mk = [sem("s_mk0"), sem("s_mk1")]

        stage = sb("stage", [128, NS, 1024])
        WH = sb("WH", [128, NW, 1024], F32R)
        WL = sb("WL", [128, NW, 1024], F32R)
        HH = sb("HH", [128, DT, S], F32R)
        HL = sb("HL", [128, DT, S], F32R)
        GH = sb("GH", [128, NSLOT, S], F32R)
        GL = sb("GL", [128, NSLOT, S], F32R)
        GHf = GH[:, :, :].rearrange("p a b -> p (a b)")
        GLf = GL[:, :, :].rearrange("p a b -> p (a b)")
        X = sb("X", [128, DT, S])
        Z = sb("Z", [128, DT, S])
        SCR = sb("SCR", [128, 6, S])
        SSQ = sb("SSQ", [128, S])
        DG = sb("DG", [128, S])
        PAR = sb("PAR", [128, NP])
        MOD = sb("MOD", [128, 2, 48])
        MOD2 = sb("MOD2", [128, 72, 2])
        CS = sb("CS", [128, 8])
        CS2 = sb("CS2", [128, 8, 2])
        AB = sb("AB", [128, 8])
        V4 = sb("V4", [128, 8])
        HM = sb("HM", [128, 4])
        OC = sb("OC", [128, 3])
        IDN = sb("IDN", [128, 128])
        ONE = sb("ONE", [128, 128])
        VM = sb("VM", [128, 8])
        ONR = sb("ONR", [128, 128], F32R)

        PS = [ctx.enter_context(nc.psum_tensor(f"ps{i}", [128, S], F32)) for i in range(8)]
        STAT, MODP = PS[6], PS[7]

        def par(name, i, n=1):
            return PAR[:, PCOLS[name] + i:PCOLS[name] + i + n]

        class Ring:

            def __init__(self, n):
                self.idle = list(range(n))
                self.last = [()] * n

            def take(self):
                i = self.idle.pop(0)
                return i, self.last[i]

            def give(self, i, *tokens):
                assert i not in self.idle
                self.last[i] = tokens
                self.idle.append(i)

        banks = Ring(6)
        scr = Ring(6)

        class Stream:
            def __init__(self):
                self.n = -1
                self.used = 8
                self.loaded = 0
                self.ready = {}
                self.split_no = {}
                self.n_split = 0
                self.slot_free = [()] * NW
                self.stage_free = {}
                self.next = 0
                if not dry:
                    for i in range(min(NS, nch)):
                        self.load(i, ())

            def load(self, i, free):
                sp.wait(*free)
                sp.ops.append(lambda e, i=i: e.dma_start(stage[:, i % NS, :], ws[i]).then_inc(s_ws[i % NS], 16))
                self.loaded = i + 1

            def landed(self, i):
                return (s_ws[i % NS], 16 * (i // NS + 1))

            def freed(self, i, *tokens):
                self.stage_free[i] = tokens
                while self.loaded < nch and self.loaded - NS in self.stage_free:
                    self.load(self.loaded, self.stage_free.pop(self.loaded - NS))

            def prepare(self, upto):
                while self.next <= min(upto, nch - 1):
                    i = self.next
                    if chunks[i][0] != "raw" and self.slot_free[self.n_split % NW] is None:
                        assert i > self.n
                        break
                    self.next += 1
                    if chunks[i][0] == "raw":
                        self.ready[i] = self.landed(i)
                        continue
                    slot = self.n_split % NW
                    self.split_no[i] = slot
                    self.n_split += 1
                    src = stage[:, i % NS, :]
                    free = self.slot_free[slot]
                    self.slot_free[slot] = None
                    hi = act.do(lambda e, o=WH[:, slot, :], s=src: e.activation(o, s, ACT.Copy),
                                self.landed(i), *free)
                    lo = dve.do(lambda e, o=WL[:, slot, :], s=src, h=WH[:, slot, :].bitcast(F32):
                                e.tensor_tensor(o, s, h, ALU.subtract), self.landed(i), hi, *free)
                    self.ready[i] = lo
                    self.freed(i, lo)

            def start(self, kind):
                self.n += 1
                self.used = 0
                if dry:
                    chunks.append((kind, []))
                else:
                    self.prepare(self.n + AHEAD)
                    pe.wait(self.ready[self.n])

            def raw(self, specs):
                before = self.used
                self.start("raw")
                self.used = 8
                if dry:
                    chunks[-1][1].extend(specs)
                return stage[:, self.n % NS, :], self.n

            def block(self, specs):
                if self.used + len(specs) > 8:
                    self.start("split")
                    self.cur = self.n
                if dry:
                    chunks[self.cur][1].extend(specs)
                a = self.used * 128
                self.used += len(specs)
                b = self.used * 128
                if dry:
                    return WH[:, 0, a:b], WL[:, 0, a:b]
                slot = self.split_no[self.cur]
                return WH[:, slot, a:b], WL[:, slot, a:b]

            def done(self, token):
                if not dry:
                    self.slot_free[self.split_no[self.cur]] = (token,)

            def close(self):
                self.used = 8

        st = Stream()

        def mm3(o, wh, wl, mh, ml, start, stop, *waits):
            pe.quiet(lambda e: e.matmul(o, wh, mh, start=start, stop=False), *waits)
            pe.quiet(lambda e: e.matmul(o, wh, ml, start=False, stop=False))
            return pe.do(lambda e: e.matmul(o, wl, mh, start=False, stop=stop))

        def col_specs(name, l, k, n):
            return (name, l, k * 128, n * 128)

        mod_tok = {}
        mod_jobs = [("ada", 0, v) for v in range(6)] + [("ada", 1, v) for v in range(6)] \
            + [("mod", 0, v) for v in range(9)]
        mod_state = {"at": 0, "t": 0, "free": (), "run": False}

        def mod_step():
            if mod_state["at"] >= len(mod_jobs):
                return
            if st.used < 8:
                return
            which, l, v = mod_jobs[mod_state["at"]]
            t = mod_state["t"]
            w, n = st.raw([("ada_w" if which == "ada" else "w_mod", l, k * 128, (v * 8 + t) * 128) for k in range(8)])
            if t == 0:
                pe.wait(*mod_state["free"])
            for k in range(8):
                o = MODP[:, t:t + 1] if which == "ada" else MODP[:, 2 * t:2 * t + 2]
                m = CS[:, k:k + 1] if which == "ada" else CS2[:, k, :]
                fn = lambda e, o=o, k=k, m=m: e.matmul(o, w[:, k * 128:k * 128 + 128], m, start=(k == 0), stop=(k == 7))
                if k < 7:
                    pe.quiet(fn, cs_tok)
                else:
                    tok = pe.do(fn)
            if not dry:
                st.freed(n, tok)
            mod_state["t"] += 1
            if mod_state["t"] == 8:
                mod_state["t"] = 0
                mod_state["at"] += 1
                if which == "ada":
                    ev = dve.do(lambda e: e.tensor_tensor(MOD[:, l, v * 8:v * 8 + 8], MODP[:, 0:8],
                                                          par("adab", l * 48 + v * 8, 8), ALU.add), tok)
                else:
                    ev = dve.do(lambda e: e.tensor_tensor(
                        MOD2[:, v * 8:v * 8 + 8, :].rearrange("p a b -> p (a b)"), MODP[:, 0:16],
                        par("bmod", v * 16, 16), ALU.add), tok)
                mod_state["free"] = (ev,)
                mod_tok[(which, l, v)] = ev

        def need(*job):
            while job not in mod_tok:
                st.close()
                mod_step()
            return mod_tok[job]

        sp.ops.append(lambda e: e.dma_start(PAR[:, :], params).then_inc(s_par, 16))
        sp.ops.append(lambda e: e.dma_start(IDN[:, :], consts[:, 0:128]).then_inc(s_con, 16))
        for t in range(DT):
            sp.ops.append(lambda e, t=t: e.dma_start(X[:, t, :], xT[t]).then_inc(s_x, 16))
        par_ok, con_ok, x_ok = (s_par, 16), (s_con, 16), (s_x, 16 * DT)
        dve.do(lambda e: e.memset(ONE[:, :], 1.0))
        dve.do(lambda e: e.memset(OC[:, 0:1], 1.0 / 1024))
        dve.do(lambda e: e.memset(OC[:, 1:2], 1.0 / 256))
        dve.do(lambda e: e.memset(OC[:, 2:3], 1.0 / 128))
        dve.do(lambda e: e.memset(HM[:, :], -0.5))
        one_ok = dve.do(lambda e: e.memset(ONR[:, :].bitcast(F32), 1.0))
        cs1 = act.do(lambda e: e.activation(CS[:, :], par("c", 0, 8), ACT.Silu), par_ok)
        cs_tok = act.do(lambda e: e.activation(CS2[:, :, :].rearrange("p a b -> p (a b)"), par("c2", 0, 16), ACT.Silu))
        dve.wait(par_ok)
        pe.wait(one_ok)

        stat = {"free": ()}
        ssq = {"free": (), "ok": None}

        def take_scr(*qs):
            i, free = scr.take()
            for q in qs:
                q.wait(*free)
            return i, SCR[:, i, :]

        def take_bank():
            i, free = banks.take()
            pe.wait(*free)
            return i, PS[i]

        def split(src, hi, lo, *waits, bias=None, scale=None):
            if bias is None and scale is None:
                a = act.do(lambda e: e.activation(hi, src, ACT.Copy), *waits)
                return dve.do(lambda e: e.tensor_tensor(lo, src, hi.bitcast(F32), ALU.subtract), a, *waits)
            if scale is not None:
                a = act.do(lambda e: e.activation(hi, src, ACT.Copy, scale=scale), *waits)
                return dve.do(lambda e: e.scalar_tensor_tensor(out=lo, in0=src, scalar=scale, in1=hi.bitcast(F32),
                                                               op0=ALU.mult, op1=ALU.subtract), a, *waits)
            a = act.do(lambda e: e.activation(hi, src, ACT.Identity, bias=bias), *waits)
            return dve.do(lambda e: e.scalar_tensor_tensor(out=lo, in0=src, scalar=bias, in1=hi.bitcast(F32),
                                                           op0=ALU.add, op1=ALU.subtract), a, *waits)

        def add_ssq(src, n, first, *waits):
            if first:
                ssq["ok"] = act.do(lambda e: e.activation(SSQ[:, 0:n], src, ACT.Square), *waits, *ssq["free"])
                return ssq["ok"]
            i, t = take_scr(act)
            sq = act.do(lambda e: e.activation(t[:, 0:n], src, ACT.Square), *waits)
            ssq["ok"] = dve.do(lambda e: e.tensor_tensor(SSQ[:, 0:n], SSQ[:, 0:n], t[:, 0:n], ALU.add), sq, ssq["ok"])
            scr.give(i, ssq["ok"])
            return sq

        def rms(n, oc):
            nt = n // 128
            pe.wait(ssq["ok"], *stat["free"])
            for t in range(nt):
                fn = lambda e, t=t: e.matmul(STAT[:, t:t + 1], SSQ[:, t * 128:t * 128 + 128], OC[:, oc:oc + 1],
                                             start=True, stop=True)
                if t < nt - 1:
                    pe.quiet(fn)
                else:
                    sums = pe.do(fn)
            ssq["free"] = (sums,)
            e1 = dve.do(lambda e: e.tensor_scalar(V4[:, 0:nt], STAT[:, 0:nt], EPS, None, ALU.add), sums)
            r4 = pool.do(lambda e: e.tensor_tensor(V4[:, 4:4 + nt], V4[:, 0:nt], HM[:, 0:nt], ALU.pow), e1, one_ok)
            dve.wait(con_ok)
            for t in range(nt):
                dg = dve.do(lambda e, t=t: e.tensor_scalar(DG[:, t * 128:t * 128 + 128], IDN[:, :],
                                                           V4[:, 4 + t:5 + t], None, ALU.mult), r4)
            for t in range(nt):
                fn = lambda e, t=t: e.matmul(STAT[:, t * 128:t * 128 + 128], ONE[:, :], DG[:, t * 128:t * 128 + 128],
                                             start=True, stop=True)
                if t < nt - 1:
                    pe.quiet(fn, dg)
                else:
                    tok = pe.do(fn, dg)
            return tok

        def affine(src, dst, a_col, b_col, n, rtok, *waits):
            held = []
            last = None

            def low(i, tmp, t, hi):
                tok = dve.do(lambda e: e.scalar_tensor_tensor(out=dst(t)[1], in0=tmp, scalar=b_col(t), in1=dst(t)[0].bitcast(F32),
                                                              op0=ALU.add, op1=ALU.subtract), hi)
                scr.give(i, tok)
                return tok

            for t in range(DT):
                i, tmp = take_scr(dve)
                tmp = tmp[:, 0:n]
                m = dve.do(lambda e, t=t, tmp=tmp: e.scalar_tensor_tensor(out=tmp, in0=src(t), scalar=a_col(t), in1=STAT[:, 0:n],
                                                                          op0=ALU.mult, op1=ALU.mult), rtok, *waits)
                hi = act.do(lambda e, t=t, tmp=tmp: e.activation(dst(t)[0], tmp, ACT.Identity, bias=b_col(t)), m, *waits)
                if held:
                    low(*held.pop())
                held.append((i, tmp, t, hi))
            stat["free"] = (m,)
            return low(*held.pop())

        def lin(nk, spec, mov, n, o, *waits, bg=True):
            pe.wait(*waits)
            for k in range(nk):
                wh, wl = st.block([spec(k)])
                mh, ml = mov(k)
                tok = mm3(o, wh, wl, mh, ml, k == 0, k == nk - 1)
                st.done(tok)
            if bg:
                mod_step()
            return tok

        def slot(i, n=S):
            return GH[:, i, 0:n], GL[:, i, 0:n]

        def hx(n=S):
            return lambda k: (HH[:, k, 0:n], HL[:, k, 0:n])

        st1 = ctx.enter_context(ExitStack())
        MASK = sb("MASK", [128, 2, 896], stack=st1)
        ROPE = sb("ROPE", [128, 2, S], stack=st1)
        DFTF = SCR[:, 0, 0:256]
        CH = sb("CH", [128, 256], F32R, stack=st1)
        CL = sb("CL", [128, 256], F32R, stack=st1)
        SG = None

        state = {"x": x_ok, "h_free": (), "g_free": (), "z_free": (), "mask_n": 0}
        sp.ops.append(lambda e: e.dma_start(DFTF, consts[:, 128:384]).then_inc(s_con, 16))
        sp.ops.append(lambda e: e.dma_start(ROPE[:, :, :].rearrange("p a b -> p (a b)"), consts[:, 384:1408]).then_inc(s_rope, 16))
        i, _ = scr.take()
        dft_ok = split(DFTF, CH[:, :], CL[:, :], (s_con, 32))
        scr.give(i, dft_ok)
        mask_free = [(), ()]

        def load_mask(h):
            b = state["mask_n"] % 2
            state["mask_n"] += 1
            sp.wait(*mask_free[b])
            sp.ops.append(lambda e: e.dma_start(MASK[:, b, :], consts[:, 1408 + h * 896:1408 + (h + 1) * 896]).then_inc(s_mk[b], 16))
            return b, (s_mk[b], 16 * ((state["mask_n"] - 1) // 2 + 1))

        def first_ssq():
            for t in range(DT):
                add_ssq(X[:, t, :], S, t == 0, x_ok)

        def token_mix(l):
            need("ada", l, 0)
            mtok = need("ada", l, 1)
            ab = dve.do(lambda e: e.scalar_tensor_tensor(out=AB[:, :], in0=MOD[:, l, 8:16], scalar=1.0, in1=par("n1", l * 8, 8),
                                                         op0=ALU.add, op1=ALU.mult), mtok, *state.get("ab_free", ()))
            r = rms(S, 0)
            h_ok = affine(lambda t: X[:, t, :], lambda t: (HH[:, t, :], HL[:, t, :]), lambda t: AB[:, t:t + 1],
                          lambda t: MOD[:, l, t:t + 1], S, r, ab, state["x"], mtok, *state["h_free"])
            state["ab_free"] = (h_ok,)
            pe.wait(h_ok)
            x_ready = state["x"]

            uf = [slice(16 * S + 640 * b, 16 * S + 640 * (b + 1)) for b in range(2)]
            uf_free = [tuple(state["g_free"]), tuple(state["g_free"])]
            zero = []
            for b in range(2):
                for T in (GHf, GLf):
                    z = T[:, uf[b]]
                    dve.do(lambda e, z=z: e.memset(z[:, 512:640].bitcast(F32), 0.0), *uf_free[b])
                    zero.append(dve.do(lambda e, z=z: e.memset(z[:, 256:257].bitcast(F32), 0.0)))
            folded = []
            dfts = []
            pend = []

            def channel_dft(g, b, tok):
                i, p = take_bank()
                pe.wait(tok, zero[-1], dft_ok)
                uh, ul = GHf[:, uf[b]], GLf[:, uf[b]]
                for t in range(4):
                    cc = slice(0, 128) if t < 2 else slice(128, 256)
                    o = p[:, t * 128:t * 128 + 128]
                    tok = mm3(o, uh[:, t * 128:t * 128 + 128], ul[:, t * 128:t * 128 + 128], CH[:, cc], CL[:, cc],
                              True, t != 2)
                    if t == 2:
                        tok = mm3(o, uh[:, 512:640], ul[:, 512:640], CH[:, 0:128], CL[:, 0:128], False, True)
                uf_free[b] = (tok,)
                ev = split(p[:, :], *slot(8 + g), tok, *state["g_free"])
                banks.give(i, ev)
                dfts.append(ev)

            for g in range(8):
                i, p = take_bank()
                tok = lin(8, lambda k, g=g: ("w_in", l, k * 128, g * 128), hx(), S, p[:, :])
                j, U = take_scr(act)
                cp = act.do(lambda e, U=U, p=p: e.activation(U, p[:, :], ACT.Copy), tok)
                banks.give(i, cp)
                b = g % 2
                m, W = take_scr(dve)
                dve.do(lambda e, U=U, W=W: e.tensor_tensor(W[:, 1:256], U[:, 1:256], U[:, 511:256:-1], ALU.add), cp)
                dve.do(lambda e, U=U, W=W: e.tensor_tensor(W[:, 257:512], U[:, 1:256], U[:, 511:256:-1], ALU.subtract))
                fo = dve.do(lambda e, U=U, W=W: e.tensor_copy(W[:, 0:512:256], U[:, 0:512:256]))
                uh, ul = GHf[:, uf[b]], GLf[:, uf[b]]

                def halves(dst, src, *w):
                    a = act.do(lambda e: e.activation(dst[0], src, ACT.Copy), *w)
                    return dve.do(lambda e: e.tensor_tensor(dst[1], src, dst[0].bitcast(F32), ALU.subtract), a)

                w = (fo, *uf_free[b], *zero)
                halves((uh[:, 0:256], ul[:, 0:256]), W[:, 0:256], *w)
                halves((uh[:, 257:512], ul[:, 257:512]), W[:, 257:512], *w)
                fd = halves((uh[:, 512:513], ul[:, 512:513]), W[:, 256:257], *w)
                scr.give(j, fo)
                scr.give(m, fd)
                if pend:
                    channel_dft(*pend.pop())
                pend.append((g, b, fd))
            st.close()
            gates = {}

            def gate(base, n):
                i, p = take_bank()
                tok = lin(8, lambda k: ("w_in", l, k * 128, (base + n) * 128), hx(), S, p[:, :])
                j, sg = take_scr(act)
                sk = act.do(lambda e: e.activation(sg, p[:, :], ACT.Sigmoid), tok)
                banks.give(i, sk)
                gates[n] = (j, sg, sk)

            channel_dft(*pend.pop())
            gate(40, 0)
            pe.wait(*dfts)
            st.close()
            tabs = []
            for q in range(2):
                a = st.block([("dft", 0, 2 * q * 128, c * 128) for c in range(4)])
                first = st.cur
                b = st.block([("dft", 0, (2 * q + 1) * 128, c * 128) for c in range(4)])
                tabs += [(a, st.cur), (b, st.cur)]
            f_ok = []
            for g in range(8):
                i, p = take_bank()
                for t in range(4):
                    (th, tl), _ = tabs[t]
                    tok = mm3(p[:, :], GH[:, 8 + g, t * 128:t * 128 + 128], GL[:, 8 + g, t * 128:t * 128 + 128], th, tl,
                              t == 0, t == 3)
                ev = split(p[:, :], *slot(g), tok, *state["g_free"])
                banks.give(i, ev)
                f_ok.append(ev)
            if not dry:
                for (_, cur) in tabs:
                    st.slot_free[st.split_no[cur]] = (tok,)
            st.close()
            m1_ok = []
            for n in range(8):
                if n:
                    gate(40, n)
                i, p = take_bank()
                tok = lin(8, lambda k, n=n: ("w_fourier", l, k * 128, n * 128), slot, S, p[:, :], *f_ok)
                j, sg, sk = gates[n]
                ev = dve.do(lambda e, n=n, p=p, sg=sg: e.tensor_tensor(Z[:, n, :], p[:, :], sg, ALU.mult), tok, sk, *state["z_free"])
                banks.give(i, ev)
                scr.give(j, ev)
                m1_ok.append(ev)
            fourier_read = tok

            g_free = (fourier_read,)
            qk_free = g_free
            v_free = g_free
            s_free = g_free
            qk_ok, v_ok, s_ok, sg_ok, r_ok = {}, {}, {}, {}, []
            masks = {0: load_mask(0)}
            sg_slot = {}

            def part_a(h):
                nonlocal qk_free
                toks = []
                for w, base in ((0, 8 + 2 * h), (1, 16 + 2 * h)):
                    b = []
                    for t in range(2):
                        i, p = take_bank()
                        tok = lin(8, lambda k, c=base + t: ("w_in", l, k * 128, c * 128), hx(), S, p[:, :])
                        b.append((i, p, tok))
                    (i0, p0, k0), (i1, p1, k1) = b
                    dve.wait((s_rope, 16))
                    for half in range(2):
                        ja, A = take_scr(dve)
                        jb, B = take_scr(dve)
                        ca, cb = (0, 1) if half == 0 else (1, 0)
                        dve.do(lambda e, A=A, p0=p0, ca=ca: e.tensor_tensor(A, p0[:, :], ROPE[:, ca, :], ALU.mult), k0)
                        mb = dve.do(lambda e, B=B, p1=p1, cb=cb: e.tensor_tensor(B, p1[:, :], ROPE[:, cb, :], ALU.mult), k1)
                        rr = dve.do(lambda e, A=A, B=B, half=half: e.tensor_tensor(A, A, B, ALU.subtract if half == 0 else ALU.add), mb)
                        ok = split(A, *slot(2 * w + half), rr, *qk_free)
                        scr.give(ja, ok)
                        scr.give(jb, rr)
                        toks.append(ok)
                    banks.give(i0, mb)
                    banks.give(i1, mb)
                qk_ok[h] = toks

            def part_b(h):
                st.close()
                ch = []
                for q in range(2):
                    for kk in range(4):
                        ch.append(st.block([("w_in", l, (q * 4 + kk) * 128, (24 + 2 * h + c) * 128) for c in range(2)]))
                        cur = st.cur
                    ch[-1] = ch[-1]
                    if q == 0:
                        first = st.cur
                v = []
                for q in range(2):
                    i, p = take_bank()
                    for t in (2 * q, 2 * q + 1):
                        for k in range(8):
                            wh, wl = ch[k]
                            sl = slice(t * 128, t * 128 + 128)
                            tok = mm3(p[:, (t % 2) * 256:(t % 2) * 256 + 256], HH[:, k, sl], HL[:, k, sl], wh, wl, k == 0, k == 7)
                    v.append((i, p, tok))
                if not dry:
                    st.slot_free[st.split_no[first]] = (tok,)
                    st.done(tok)
                st.close()
                toks = []
                for q in range(2):
                    i, p, tok = v[q]
                    j, junk = take_scr(act)
                    sms = []
                    for t in range(2):
                        sms.append(act.do(lambda e, p=p, t=t, q=q, junk=junk: e.activation(
                            junk[:, t * 256:t * 256 + 256], p[:, t * 256:t * 256 + 256], ACT.Copy,
                            accum_out=VM[:, 2 * q + t:2 * q + t + 1]), tok, *state.get("vm_free", ())))
                    nm = dve.do(lambda e, q=q: e.tensor_scalar(VM[:, 4 + 2 * q:6 + 2 * q], VM[:, 2 * q:2 * q + 2], -1.0 / 256, None, ALU.mult), sms[-1])
                    for t in range(2):
                        sl = slice(t * 256, t * 256 + 256)
                        hi = act.do(lambda e, p=p, q=q, t=t, sl=sl: e.activation(
                            GH[:, 4 + q, sl], p[:, sl], ACT.Identity, bias=VM[:, 4 + 2 * q + t:5 + 2 * q + t]), nm, *v_free)
                    for t in range(2):
                        sl = slice(t * 256, t * 256 + 256)
                        ok = dve.do(lambda e, p=p, q=q, t=t, sl=sl: e.scalar_tensor_tensor(
                            out=GL[:, 4 + q, sl], in0=p[:, sl], scalar=VM[:, 4 + 2 * q + t:5 + 2 * q + t],
                            in1=GH[:, 4 + q, sl].bitcast(F32), op0=ALU.add, op1=ALU.subtract), hi, *v_free)
                    banks.give(i, ok)
                    scr.give(j, ok)
                    toks.append(ok)
                state["vm_free"] = (ok,)
                v_ok[h] = toks
                mod_step()
                sg_ok[h] = []
                for t in range(2):
                    i, p = take_bank()
                    tok = lin(8, lambda k, t=t: ("w_in", l, k * 128, (32 + 2 * h + t) * 128), hx(), S, p[:, :])
                    j, sg = take_scr(act)
                    sk = act.do(lambda e, p=p, sg=sg: e.activation(sg, p[:, :], ACT.Silu), tok)
                    banks.give(i, sk)
                    sg_ok[h].append((j, sg, sk))

            def part_c(h):
                nonlocal s_free, qk_free
                mb, mtok = masks[h]
                if h + 1 < NH:
                    masks[h + 1] = load_mask(h + 1)
                pe.wait(*qk_ok[h])
                s_ok[h] = []
                for jt in range(4):
                    i, p = take_bank()
                    for t in range(2):
                        sl = slice(jt * 128, jt * 128 + 128)
                        tok = mm3(p[:, :], GH[:, 2 + t, sl], GL[:, 2 + t, sl], GH[:, t, :], GL[:, t, :], t == 0, t == 1)
                    j, T = take_scr(dve)
                    m = dve.do(lambda e, T=T, p=p, jt=jt, mb=mb: e.tensor_tensor(
                        T, p[:, :], MASK[:, mb, 384 - 128 * jt:896 - 128 * jt], ALU.mult), tok, mtok)
                    banks.give(i, m)
                    a = act.do(lambda e, T=T, jt=jt: e.activation(GH[:, 6 + jt, :], T, ACT.Copy), m, *s_free)
                    lo = pool.do(lambda e, T=T, jt=jt: e.tensor_tensor(GL[:, 6 + jt, :], T, GH[:, 6 + jt, :].bitcast(F32), ALU.subtract), m, a, *s_free)
                    scr.give(j, lo)
                    s_ok[h].append(lo)
                mask_free[mb] = (m,)
                qk_free = (tok,)

            def part_d(h):
                nonlocal v_free, s_free
                pe.wait(*v_ok[h])
                ys = []
                for t in range(2):
                    i, p = take_bank()
                    for jt in range(4):
                        a = (jt % 2) * 256 + t * 128
                        tok = mm3(p[:, :], GH[:, 4 + jt // 2, a:a + 128], GL[:, 4 + jt // 2, a:a + 128],
                                  GH[:, 6 + jt, :], GL[:, 6 + jt, :], jt == 0, jt == 3, s_ok[h][jt])
                    sq = add_ssq(p[:, :], S, t == 0, tok)
                    j, sg, sk = sg_ok[h][t]
                    yg = dve.do(lambda e, p=p, sg=sg: e.tensor_tensor(sg, p[:, :], sg, ALU.mult), sq, sk)
                    banks.give(i, yg)
                    ys.append((j, sg, yg))
                v_free = (tok,)
                s_free = (tok,)
                return h, ys

            def part_e(h, ys):
                r = rms(S, 1)
                for t in range(2):
                    j, sg, yg = ys[t]
                    m = dve.do(lambda e, sg=sg: e.tensor_tensor(sg, STAT[:, :], sg, ALU.mult), r, yg)
                    ok = split(sg, *slot(10 + 2 * h + t), m, fourier_read)
                    scr.give(j, ok)
                    r_ok.append(ok)
                stat["free"] = (m,)

            part_a(0)
            part_b(0)
            part_c(0)
            for h in range(NH):
                if h + 1 < NH:
                    part_a(h + 1)
                d = part_d(h)
                if h + 1 == NH:
                    gates.clear()
                    gate(48, 0)
                part_e(*d)
                if h + 1 < NH:
                    part_b(h + 1)
                    part_c(h + 1)

            gread = v_free + qk_free + s_free
            mg_ok = []
            for n in range(8):
                i, p = take_bank()
                if n:
                    gate(48, n)
                tok = lin(8, lambda k, n=n: ("w_ret", l, k * 128, n * 128), lambda k: slot(10 + k), S, p[:, :], *r_ok)
                j, sg, sk = gates[n]
                dve.do(lambda e, p=p, sg=sg: e.tensor_tensor(sg, p[:, :], sg, ALU.mult), tok, sk)
                ev = (dve.sem, dve.count)
                banks.give(i, ev)
                ad = dve.do(lambda e, sg=sg, n=n: e.tensor_tensor(sg, sg, Z[:, n, :], ALU.add), ev, m1_ok[n])
                ok = split(sg, *slot(n), ad, *gread)
                scr.give(j, ok)
                mg_ok.append(ok)
            state["h_free"] = (tok,)
            state["z_free"] = (ad,)
            gtok = need("ada", l, 2)
            for n in range(8):
                i, p = take_bank()
                tok = lin(8, lambda k, n=n: ("w_out", l, k * 128, n * 128), slot, S, p[:, :], *mg_ok)
                ev = dve.do(lambda e, n=n, p=p: e.scalar_tensor_tensor(
                    out=X[:, n, :], in0=p[:, :], scalar=MOD[:, l, 16 + n:17 + n], in1=X[:, n, :], op0=ALU.mult, op1=ALU.add),
                    tok, gtok, x_ready)
                banks.give(i, ev)
                add_ssq(X[:, n, :], S, n == 0, ev)
            state["x"] = ev
            state["g_free"] = (tok,)

        def conv_ffn(l):
            need("ada", l, 3)
            mtok = need("ada", l, 4)
            ab = dve.do(lambda e: e.scalar_tensor_tensor(out=AB[:, :], in0=MOD[:, l, 32:40], scalar=1.0, in1=par("n2", l * 8, 8),
                                                         op0=ALU.add, op1=ALU.mult), mtok, *state["ab_free"])
            r = rms(S, 0)
            h_ok = affine(lambda t: X[:, t, :], lambda t: (HH[:, t, :], HL[:, t, :]), lambda t: AB[:, t:t + 1],
                          lambda t: MOD[:, l, 24 + t:25 + t], S, r, ab, state["x"], mtok, *state["h_free"])
            state["ab_free"] = (h_ok,)
            pe.wait(h_ok)
            for half in range(2):
                hid = []
                for jj in range(11):
                    j0 = half * 11 + jj
                    t2 = []
                    for c in (j0, 22 + j0):
                        i, p = take_bank()
                        tok = lin(8, lambda k, c=c: ("ffn_up", l, k * 128, c * 128), hx(), S, p[:, :])
                        h_read = tok
                        m, T = take_scr(act)
                        cw = lambda tap, c=c: par("cw", (l * 3 + tap) * 44 + c)
                        a = act.do(lambda e, T=T, p=p, c=c, cw=cw: e.activation(T, p[:, :], ACT.Identity, scale=cw(1), bias=par("cb", l * 44 + c)), tok)
                        b1 = dve.do(lambda e, T=T, p=p, cw=cw: e.scalar_tensor_tensor(
                            out=T[:, 1:S], in0=p[:, 0:S - 1], scalar=cw(0), in1=T[:, 1:S], op0=ALU.mult, op1=ALU.add), a)
                        b2 = dve.do(lambda e, T=T, p=p, cw=cw: e.scalar_tensor_tensor(
                            out=T[:, 0:S - 1], in0=p[:, 1:S], scalar=cw(2), in1=T[:, 0:S - 1], op0=ALU.mult, op1=ALU.add), b1)
                        banks.give(i, b2)
                        if c == j0:
                            b2 = act.do(lambda e, T=T: e.activation(T, T, ACT.Gelu), b2)
                        t2.append((m, T, b2))
                    (m1, A, ka), (m2, B, kb) = t2
                    hm = dve.do(lambda e, A=A, B=B: e.tensor_tensor(B, A, B, ALU.mult), ka, kb)
                    ok = split(B, *slot(jj), hm, *state["g_free"])
                    scr.give(m1, hm)
                    scr.give(m2, ok)
                    hid.append(ok)
                if half == 1:
                    state["h_free"] = (h_read,)
                gtok = need("ada", l, 5)
                for n in range(8):
                    i, p = take_bank()
                    tok = lin(11, lambda k, n=n: ("ffn_down", l, (half * 11 + k) * 128, n * 128), slot, S, p[:, :], *hid)
                    ev = dve.do(lambda e, n=n, p=p: e.scalar_tensor_tensor(
                        out=X[:, n, :], in0=p[:, :], scalar=MOD[:, l, 40 + n:41 + n], in1=X[:, n, :], op0=ALU.mult, op1=ALU.add),
                        tok, gtok, state["x"])
                    banks.give(i, ev)
                    if half:
                        add_ssq(X[:, n, :], S, n == 0, ev)
                state["x"] = ev
                state["g_free"] = (tok,)

        if not dry:
            pass
        first_ssq()
        for l in range(2):
            token_mix(l)
            conv_ffn(l)
        r = rms(S, 0)
        for t in range(DT):
            ev = dve.do(lambda e, t=t: e.scalar_tensor_tensor(out=X[:, t, :], in0=X[:, t, :], scalar=par("fing", t), in1=STAT[:, :],
                                                              op0=ALU.mult, op1=ALU.mult), r, state["x"], ssq["ok"])
        stat["free"] = (ev,)
        state["x"] = ev
        st1.close()

        GT = sb("GT", [GATE_ROWS, 4, 768])
        SEL = sb("SEL", [GATE_ROWS, 8, 128])
        TRI = sb("TRI", [128, 2, 128])
        GC = sb("GC", [128, 6, GATE_ROWS])
        RC = sb("RC", [128, 8])
        old = ((pe.sem, pe.count), (dve.sem, dve.count), (act.sem, act.count))
        sp.wait(*old)
        sp.ops.append(lambda e: e.dma_start(SEL[:, :, :].rearrange("p a b -> p (a b)"), sel_d).then_inc(s_rope, 16))
        sp.ops.append(lambda e: e.dma_start(TRI[:, :, :].rearrange("p a b -> p (a b)"), consts[:, 4992:5248]).then_inc(s_rope, 16))
        sp.wait(*state["z_free"])
        for t in range(DT):
            sp.ops.append(lambda e, t=t: e.dma_start(Z[:, t, 256:512], cT[t]).then_inc(s_x, 16))
        sel_ok = (s_rope, 48)
        xc_ok = (s_x, 32 * DT)

        def ada_norm(j, col, src, dst, n, *waits):
            need("mod", 0, 3 * j)
            mtok = need("mod", 0, 3 * j + 1)
            ab = dve.do(lambda e: e.scalar_tensor_tensor(out=AB[:, :], in0=MOD2[:, 24 * j + 8:24 * j + 16, col], scalar=1.0,
                                                         in1=par("npre", j * 8, 8), op0=ALU.add, op1=ALU.mult), mtok, *state["ab_free"])
            r = rms(n, 0)
            ok = affine(src, dst, lambda t: AB[:, t:t + 1], lambda t: MOD2[:, 24 * j + t, col:col + 1], n, r, ab, mtok, *waits)
            state["ab_free"] = (ok,)
            return ok

        def swiglu(f, n, zt, *waits):
            for half in range(2):
                hid = []
                for jj in range(11):
                    j0 = half * 11 + jj
                    i0, p0 = take_bank()
                    tok = lin(8, lambda k: ("ffn_w_in", f, k * 128, j0 * 128), hx(n), n, p0[:, 0:n])
                    m, T = take_scr(act)
                    T = T[:, 0:n]
                    a = act.do(lambda e, T=T, p0=p0: e.activation(T, p0[:, 0:n], ACT.Silu), tok)
                    banks.give(i0, a)
                    i1, p1 = take_bank()
                    tok = lin(8, lambda k: ("ffn_w_in", f, k * 128, (22 + j0) * 128), hx(n), n, p1[:, 0:n])
                    h_read = tok
                    hm = dve.do(lambda e, T=T, p1=p1: e.tensor_tensor(T, p1[:, 0:n], T, ALU.mult), tok, a)
                    banks.give(i1, hm)
                    ok = split(T, *slot(jj, n), hm, *state["g_free"])
                    scr.give(m, ok)
                    hid.append(ok)
                if half == 1:
                    state["h_free"] = (h_read,)
                for nn in range(8):
                    i, p = take_bank()
                    tok = lin(11, lambda k, nn=nn: ("ffn_w_out", f, (half * 11 + k) * 128, nn * 128), lambda k: slot(k, n), n,
                              p[:, 0:n], *hid)
                    z = zt(nn)
                    if half == 0:
                        ev = act.do(lambda e, z=z, p=p: e.activation(z, p[:, 0:n], ACT.Copy), tok, *waits)
                    else:
                        ev = dve.do(lambda e, z=z, p=p: e.tensor_tensor(z, p[:, 0:n], z, ALU.add), tok, z_prev)
                        add_ssq(z, n, nn == 0, ev)
                    banks.give(i, ev)
                z_prev = ev
                state["g_free"] = (tok,)
            return ev

        def ada_out(j, col, res_w, zt, xt, n, z_ok, x_tok):
            mtok = need("mod", 0, 3 * j + 2)
            rc = dve.do(lambda e: e.scalar_tensor_tensor(out=RC[:, :], in0=MOD2[:, 24 * j + 16:24 * j + 24, col], scalar=res_w,
                                                         in1=par("npost", j * 8, 8), op0=ALU.mult, op1=ALU.mult), mtok)
            r = rms(n, 0)
            for t in range(DT):
                i, T = take_scr(dve)
                T = T[:, 0:n]
                m = dve.do(lambda e, t=t, T=T: e.scalar_tensor_tensor(out=T, in0=zt(t), scalar=RC[:, t:t + 1], in1=STAT[:, 0:n],
                                                                      op0=ALU.mult, op1=ALU.mult), r, rc, z_ok)
                ev = dve.do(lambda e, t=t, T=T: e.tensor_tensor(xt(t), xt(t), T, ALU.add), m, x_tok)
                scr.give(i, ev)
                add_ssq(xt(t), n, t == 0, ev)
            stat["free"] = (m,)
            return ev

        zc = lambda t: Z[:, t, 0:256]
        xc = lambda t: Z[:, t, 256:512]
        zx = lambda t: Z[:, t, :]
        xx = lambda t: X[:, t, :]
        hcs = lambda t: (GH[:, 14 + t // 2, (t % 2) * 256:(t % 2) * 256 + 256], GL[:, 14 + t // 2, (t % 2) * 256:(t % 2) * 256 + 256])

        x_ssq_first = state["x"]
        for t in range(DT):
            add_ssq(xc(t), C, t == 0, xc_ok)
        h_ok = ada_norm(0, 1, xc, lambda t: (HH[:, t, 0:C], HL[:, t, 0:C]), C, xc_ok, *state["h_free"])
        pe.wait(h_ok)
        z_ok = swiglu(0, C, zc, *state["z_free"])
        c_ok = ada_out(0, 1, 0.5, zc, xc, C, z_ok, xc_ok)
        hc_ok = ada_norm(1, 1, xc, hcs, C, c_ok, *state["g_free"])

        for t in range(DT):
            add_ssq(xx(t), S, t == 0, x_ssq_first)
        h_ok = ada_norm(0, 0, xx, lambda t: (HH[:, t, :], HL[:, t, :]), S, state["x"], *state["h_free"])
        pe.wait(h_ok)
        z_ok = swiglu(0, S, zx, hc_ok)
        x_tok = ada_out(0, 0, 0.5, zx, xx, S, z_ok, state["x"])
        h_ok = ada_norm(1, 0, xx, lambda t: (HH[:, t, :], HL[:, t, :]), S, x_tok, *state["h_free"])
        pe.wait(h_ok, hc_ok)
        g_free = state["g_free"]
        UH, UL = GHf[:, 0:3072], GLf[:, 0:3072]
        lat, con = slice(256, 768), slice(0, 256)

        u_ok = []
        for h in range(NH):
            ix, px = take_bank()
            ic, pc = take_bank()
            for k in range(8):
                wh, wl = st.block([("w_in2", 0, k * 128, h * 128)])
                mm3(px[:, :], wh, wl, HH[:, k, :], HL[:, k, :], k == 0, k == 7)
                tok = mm3(pc[:, 0:C], wh, wl, *hcs(k), k == 0, k == 7)
                st.done(tok)
            mod_step()
            for p, i, n, cols in ((px, ix, S, lat), (pc, ic, C, con)):
                m, T = take_scr(act)
                cw = lambda tap, h=h: par("cw2", tap * 4 + h)
                a = act.do(lambda e, T=T, p=p, n=n, cw=cw, h=h: e.activation(
                    T[:, 0:n], p[:, 0:n], ACT.Identity, scale=cw(1), bias=par("cb2", h)), tok)
                b1 = dve.do(lambda e, T=T, p=p, n=n, cw=cw: e.scalar_tensor_tensor(
                    out=T[:, 1:n], in0=p[:, 0:n - 1], scalar=cw(0), in1=T[:, 1:n], op0=ALU.mult, op1=ALU.add), a)
                b2 = dve.do(lambda e, T=T, p=p, n=n, cw=cw: e.scalar_tensor_tensor(
                    out=T[:, 0:n - 1], in0=p[:, 1:n], scalar=cw(2), in1=T[:, 0:n - 1], op0=ALU.mult, op1=ALU.add), b1)
                banks.give(i, b2)
                sl = act.do(lambda e, T=T, n=n: e.activation(T[:, 0:n], T[:, 0:n], ACT.Silu), b2)
                a0 = h * 768 + cols.start
                ok = split(T[:, 0:n], UH[:, a0:a0 + n], UL[:, a0:a0 + n], sl, *g_free)
                scr.give(m, ok)
                u_ok.append(ok)

        st.close()
        bs = []
        for c in range(6):
            bs.append(take_bank())
        for k in range(8):
            wh, wl = st.block([("w_in2", 0, k * 128, 512 + q * 128) for q in range(4)])
            for c in range(6):
                if c < 2:
                    a, b = (x[:, c * 128:c * 128 + 128] for x in hcs(k))
                else:
                    a, b = HH[:, k, (c - 2) * 128:(c - 1) * 128], HL[:, k, (c - 2) * 128:(c - 1) * 128]
                tok = mm3(bs[c][1][:, :], a, b, wh, wl, k == 0, k == 7)
            st.done(tok)
        v_ok = []
        for c in range(6):
            i, p = bs[c]
            ok = split(p[:, :], *slot(6 + c), tok, *g_free)
            banks.give(i, ok)
            v_ok.append(ok)
        mod_step()

        ix, px = take_bank()
        ic, pc = take_bank()
        for k in range(8):
            wh, wl = st.block([("gate", 0, k * 128, 0)])
            mm3(px[:, :], wh, wl, HH[:, k, :], HL[:, k, :], k == 0, k == 7)
            tok = mm3(pc[:, 0:C], wh, wl, *hcs(k), k == 0, k == 7)
            st.done(tok)
        hc_read = tok
        T0, T1, T2, T3 = (GT[:, i, :] for i in range(4))
        for T, base in ((T0, 0), (T1, 64)):
            for p, c0, n in ((px, 256, S), (pc, 0, C)):
                dve.do(lambda e, T=T, p=p, c0=c0, n=n, base=base: e.tensor_copy(T[0:32, c0:c0 + n], p[base:base + 32, 0:n]), tok, *old)
                cpy = dve.do(lambda e, T=T, p=p, c0=c0, n=n, base=base: e.tensor_copy(
                    T[32:36, c0:c0 + n], p[base + 32:base + 36, n - 1::-1] if n == S else p[base + 32:base + 36, C - 1::-1]))
        banks.give(ix, cpy)
        banks.give(ic, cpy)
        ib, fb = PAR[0:36, PCOLS["ib"]:PCOLS["ib"] + 1], PAR[0:36, PCOLS["fb"]:PCOLS["fb"] + 1]
        dve.do(lambda e: e.tensor_scalar(T0, T0, ib, None, ALU.add), cpy)
        d1 = dve.do(lambda e: e.tensor_scalar(T1, T1, fb, None, ALU.add), cpy)
        d0 = dve.do(lambda e: e.memset(T3, 1.0))
        a1 = act.do(lambda e: e.activation(T2, T1, ACT.Abs), d1)
        a2 = act.do(lambda e: e.activation(T2, T2, ACT.Exp, scale=-1.0), a1)
        a3 = act.do(lambda e: e.activation(T2, T2, ACT.Ln, bias=1.0), a2)
        d2 = dve.do(lambda e: e.scalar_tensor_tensor(out=T1, in0=T1, scalar=0.0, in1=T2, op0=ALU.min, op1=ALU.subtract), a3)
        d3 = dve.do(lambda e: e.tensor_tensor_scan(T2, T3, T1, 0.0, ALU.mult, ALU.add), d2, d0)
        d4 = dve.do(lambda e: e.tensor_tensor(T0, T0, T2, ALU.subtract), d3)
        d5 = dve.do(lambda e: e.tensor_tensor_scan(T1, T3, T0, 0.0, ALU.mult, ALU.max), d4)
        d6 = dve.do(lambda e: e.tensor_tensor(T2, T2, T1, ALU.add), d5)
        dve.do(lambda e: e.tensor_copy(T3[0:32, :], T0[0:32, :]), d6)
        dve.do(lambda e: e.tensor_copy(T3[32:36, 0:256], T0[32:36, 255::-1]))
        d7 = dve.do(lambda e: e.tensor_copy(T3[32:36, 256:768], T0[32:36, 767:255:-1]))
        dve.do(lambda e: e.tensor_copy(T0[0:32, 256:768], T1[0:32, 256:768]), d7)
        d8 = dve.do(lambda e: e.tensor_copy(T0[32:36, 256:768], T1[32:36, 767:255:-1]), d7)
        dve.do(lambda e: e.tensor_copy(T1[0:32, 256:768], T2[0:32, 256:768]), d8)
        d9 = dve.do(lambda e: e.tensor_copy(T1[32:36, 256:768], T2[32:36, 767:255:-1]), d8)

        so_ok = []
        for h in range(NH):
            i, p = take_bank()
            tok = lin(8, lambda k: ("w_in2", 0, k * 128, 1024 + h * 128), hx(), S, p[:, :])
            ok = act.do(lambda e, p=p, h=h: e.activation(Z[:, h, :], p[:, :], ACT.Sigmoid), tok, x_tok)
            banks.give(i, ok)
            so_ok.append(ok)

        pe.wait(*stat["free"], d7, con_ok)
        for c in range(6):
            fn = lambda e, c=c: e.transpose(STAT[:, c * 36:c * 36 + 36], T3[:, c * 128:c * 128 + 128], IDN[0:36, 0:36])
            if c < 5:
                pe.quiet(fn)
            else:
                tok = pe.do(fn)
        gc_ok = dve.do(lambda e: e.tensor_copy(GC[:, :, :].rearrange("p a b -> p (a b)"), STAT[:, 0:216]), tok, *old)
        stat["free"] = (gc_ok,)

        st.close()
        bs = [take_bank() for _ in range(4)]
        for k in range(8):
            wh, wl = st.block([("w_in2", 0, k * 128, 1552 + q * 128) for q in range(4)])
            for c in range(4):
                tok = mm3(bs[c][1][:, :], HH[:, k, c * 128:c * 128 + 128], HL[:, k, c * 128:c * 128 + 128], wh, wl, k == 0, k == 7)
            st.done(tok)
        h_read = tok
        pu_ok = []
        for c in range(4):
            i, p = bs[c]
            ok = split(p[:, :], *slot(14 + c), tok, hc_read)
            banks.give(i, ok)
            pu_ok.append(ok)
        mod_step()
        st.close()
        d_free = [g_free, g_free]
        mix_ok = {}
        pend = []

        def pool_out(g, ok):
            i, p = take_bank()
            wh, wl = st.block([("pool_w", g, 0, 0)])
            tok = mm3(p[:, :], wh, wl, *slot(12 + g % 2), True, True, ok)
            st.done(tok)
            d_free[g % 2] = (tok,)
            mix_ok[4 + g] = split(p[:, :], HH[:, 4 + g, :], HL[:, 4 + g, :], tok, h_read, scale=par("ps", g))
            banks.give(i, mix_ok[4 + g])

        pe.wait(*pu_ok)
        for g in range(4):
            i, p = take_bank()
            for t in range(4):
                ph, pl = st.block([("poolm", g, t * 128, q * 128) for q in range(4)])
                tok = mm3(p[:, :], GH[:, 14 + t, g * 128:g * 128 + 128], GL[:, 14 + t, g * 128:g * 128 + 128], ph, pl, t == 0, t == 3)
                st.done(tok)
            pu_read = tok
            ok = split(p[:, :], *slot(12 + g % 2), tok, *d_free[g % 2])
            banks.give(i, ok)
            if pend:
                pool_out(*pend.pop())
            pend.append((g, ok))
            mod_step()
        pool_out(*pend.pop())
        st.close()

        qk = st.block([("w_q" if i % 2 == 0 else "w_k", i // 2, 0, 0) for i in range(8)])
        qk_chunk = st.cur
        q_sl = slice(12 * S, 13 * S)
        q_free = d_free[0] + d_free[1]
        e_free = [(pu_read,)] * 4
        mb_free = ()
        pe.wait(*u_ok)
        e_n = 0
        scale = 128.0 ** -0.5
        kslot = lambda c: (GH[:, 18, c * 128:c * 128 + 128], GL[:, 18, c * 128:c * 128 + 128]) if c < 2 else \
            (GH[:, 13, (c - 2) * 128:(c - 1) * 128], GL[:, 13, (c - 2) * 128:(c - 1) * 128])
        acc_free = [tuple(banks.last[i]) for i in range(4)]
        s_free = [tuple(banks.last[4]), tuple(banks.last[5])]
        sn = 0
        pe.wait(sel_ok, d9)
        for h in range(NH):
            wq = [x[:, 2 * h * 128:2 * h * 128 + 128] for x in qk]
            wk = [x[:, (2 * h + 1) * 128:(2 * h + 1) * 128 + 128] for x in qk]
            a0 = h * 768
            mbs = []
            for d in range(2):
                for w, T in ((0, T0), (1, T1)):
                    pe.wait(*stat["free"])
                    tok = pe.do(lambda e, d=d, T=T, h=h: e.matmul(STAT[:, :], SEL[:, d * 4 + h, :], T[:, 256:768], start=True, stop=True))
                    dst = Z[:, 4 + 2 * d + w, :]
                    if w == 0:
                        ok = act.do(lambda e, dst=dst: e.activation(dst, STAT[:, :], ACT.Copy), tok, x_tok, *mb_free)
                    else:
                        ok = act.do(lambda e, dst=dst: e.activation(dst, STAT[:, :], ACT.Exp, scale=-1.0), tok, x_tok, *mb_free)
                    stat["free"] = (ok,)
                    mbs.append(ok)
            for which, w, cols, dst in ((0, wq, slice(a0 + 256, a0 + 768), slot(12)),
                                        (1, wk, slice(a0 + 256, a0 + 768), slot(13)),
                                        (2, wk, slice(a0, a0 + 256), slot(18, C))):
                b = sn % 2
                sn += 1
                n = cols.stop - cols.start
                P = PS[4 + b]
                tok = mm3(P[:, 0:n], w[0], w[1], UH[:, cols], UL[:, cols], True, True, *s_free[b])
                ok = split(P[:, 0:n], *dst, tok, *q_free, scale=None if which == 0 else scale)
                s_free[b] = (ok,)
            pe.wait(ok)
            if not dry:
                st.slot_free[st.split_no[qk_chunk]] = (tok,)
            NUM, DEN = (PS[0], PS[1]), (PS[2], PS[3])
            for i in range(4):
                pe.wait(*acc_free[i])
            for c in range(6):
                b = sn % 2
                sn += 1
                P = PS[4 + b]
                stok = mm3(P[:, :], *kslot(c), *slot(12), True, True, *s_free[b])
                q_read = stok
                for d in range(2):
                    j = c - 2
                    lo_c, hi_c = (0, S) if c < 2 else ((128 * j, S) if d == 0 else (0, 128 * (j + 1)))
                    n = hi_c - lo_c
                    m, T = take_scr(dve)
                    T = T[:, 0:n]
                    g1 = dve.do(lambda e, T=T, lo_c=lo_c, hi_c=hi_c, c=c, d=d, h=h: e.tensor_scalar(
                        T, Z[:, 4 + 2 * d, lo_c:hi_c], GC[:, c, 32 * d + h:32 * d + h + 1], 0.0, ALU.subtract, ALU.max),
                        mbs[2 * d], gc_ok)
                    g2 = act.do(lambda e, T=T: e.activation(T, T, ACT.Exp, scale=-1.0), g1)
                    if c >= 2:
                        dd = slice(0, 128) if d == 0 else slice(n - 128, n)
                        g2 = dve.do(lambda e, T=T, dd=dd, d=d: e.tensor_tensor(T[:, dd], T[:, dd], TRI[:, d, :], ALU.mult), g2, sel_ok)
                    g3 = dve.do(lambda e, T=T, P=P, lo_c=lo_c, hi_c=hi_c: e.tensor_tensor(T, P[:, lo_c:hi_c], T, ALU.mult), g2, stok)
                    es = e_n % 4
                    e_n += 1
                    eh, el = GH[:, 14 + es, 0:n], GL[:, 14 + es, 0:n]
                    g4 = act.do(lambda e, T=T, eh=eh: e.activation(eh, T, ACT.Copy), g3, *e_free[es])
                    g5 = pool.do(lambda e, T=T, eh=eh, el=el: e.tensor_tensor(el, T, eh.bitcast(F32), ALU.subtract), g4, *e_free[es])
                    scr.give(m, g5)
                    va = (GH[:, 6 + c, h * 128:h * 128 + 128], GL[:, 6 + c, h * 128:h * 128 + 128])
                    mm3(NUM[d][:, lo_c:hi_c], *va, eh, el, c == 0, c == 5, g5, *v_ok)
                    pe.quiet(lambda e, d=d, eh=eh, lo_c=lo_c, hi_c=hi_c, c=c: e.matmul(DEN[d][:, lo_c:hi_c], ONR[:, :], eh, start=(c == 0), stop=False))
                    tok = pe.do(lambda e, d=d, el=el, lo_c=lo_c, hi_c=hi_c, c=c: e.matmul(DEN[d][:, lo_c:hi_c], ONR[:, :], el, start=False, stop=(c == 5)))
                    e_free[es] = (tok,)
                s_free[b] = (g3,)
            q_free = (q_read,)
            hs = []
            for d in range(2):
                m, T = take_scr(act)
                a = act.do(lambda e, T=T, d=d: e.activation(T, DEN[d][:, :], ACT.Abs), tok)
                acc_free[2 + d] = (a,)
                x1 = dve.do(lambda e, T=T, d=d: e.tensor_tensor(T, T, Z[:, 5 + 2 * d, :], ALU.max), a, mbs[2 * d + 1])
                x2 = dve.do(lambda e, T=T: e.reciprocal(T, T), x1)
                x3 = dve.do(lambda e, T=T, d=d: e.tensor_tensor(T, NUM[d][:, :], T, ALU.mult), x2)
                acc_free[d] = (x3,)
                hs.append((m, T, x3))
            mb_free = (x3,)
            (m0, A, _), (m1, B, kb) = hs
            hh = dve.do(lambda e, A=A, B=B: e.tensor_tensor(A, A, B, ALU.add), kb)
            scr.give(m1, hh)
            add_ssq(A, S, True, hh)
            r = rms(S, 2)
            y1 = dve.do(lambda e, A=A, h=h: e.scalar_tensor_tensor(out=A, in0=A, scalar=par("hn", h), in1=STAT[:, :], op0=ALU.mult, op1=ALU.mult), r, ssq["ok"])
            stat["free"] = (y1,)
            y2 = dve.do(lambda e, A=A, h=h: e.tensor_tensor(A, A, Z[:, h, :], ALU.mult), y1, so_ok[h])
            mix_ok[h] = split(A, HH[:, h, :], HL[:, h, :], y2, h_read)
            scr.give(m0, mix_ok[h])
        for i in range(4):
            banks.last[i] = acc_free[i]
        banks.last[4], banks.last[5] = s_free
        z_free = (y2,)
        state["g_free"] = (tok, q_read)
        for nn in range(8):
            i, p = take_bank()
            tok = lin(8, lambda k, nn=nn: ("w_out2", 0, k * 128, nn * 128), hx(), S, p[:, :], *mix_ok.values())
            ev = act.do(lambda e, nn=nn, p=p: e.activation(Z[:, nn, :], p[:, :], ACT.Copy), tok, *z_free)
            add_ssq(Z[:, nn, :], S, nn == 0, ev)
            banks.give(i, ssq["ok"])
        state["h_free"] = (tok,)
        x_tok = ada_out(1, 0, 1.0, zx, xx, S, ev, x_tok)
        h_ok = ada_norm(2, 0, xx, lambda t: (HH[:, t, :], HL[:, t, :]), S, x_tok, *state["h_free"])
        pe.wait(h_ok)
        z_ok = swiglu(1, S, zx, x_tok)
        x_tok = ada_out(2, 0, 0.5, zx, xx, S, z_ok, x_tok)
        sp.wait(x_tok)
        for t in range(DT):
            sp.ops.append(lambda e, t=t: e.dma_start(out[t], X[:, t, :]).then_inc(s_out, 16))
        sp.wait((s_out, 16 * DT))

        if dry:
            return
        block = ctx.enter_context(nc.Block())

        @block.sync
        def _(e):
            sp.run(e)

        @block.tensor
        def _(e):
            pe.run(e)

        @block.scalar
        def _(e):
            act.run(e)

        @block.vector
        def _(e):
            dve.run(e)

        @block.gpsimd
        def _(e):
            pool.run(e)


def constants():
    c = np.zeros((128, 5248), np.float32)
    c[:, 0:128] = np.eye(128)
    i = np.arange(128)
    ang = 2 * np.pi * ((i[:, None] * i[None, :]) % 128) / 128
    c[:, 128:256] = np.cos(ang) / 256
    c[:, 256:384] = np.sin(ang) / 256
    inv = np.float32(10000.0) ** (-np.arange(128, dtype=np.float32) / np.float32(128))
    ang = (np.arange(512, dtype=np.float32)[None, :] * inv.astype(np.float32)[:, None]).astype(np.float64)
    c[:, 384:896] = np.cos(ang)
    c[:, 896:1408] = np.sin(ang)
    d = np.arange(896)[None, :] - 384 - np.arange(128)[:, None]
    for h in range(4):
        gf = 1 - 2.0 ** -(5.0 + h)
        gb = 1 - 2.0 ** -(5.5 + h)
        c[:, 1408 + h * 896:1408 + (h + 1) * 896] = np.where(d >= 0, gf ** np.abs(d), gb ** np.abs(d)) / 16
    c[:, 4992:5120] = i[:, None] <= i[None, :]
    c[:, 5120:5248] = i[:, None] >= i[None, :]
    sel = np.zeros((GATE_ROWS, 8, 128), np.float32)
    for d2 in range(2):
        for h in range(4):
            sel[32 * d2 + h, d2 * 4 + h] = 1
    j = np.arange(512)
    ph = 2 * np.pi * ((j[:256, None] * j[None, :]) % 512) / 512
    dft = np.zeros((512, 512))
    dft[:256] = np.cos(ph)
    dft[256:] = -np.sin(ph)
    dft[256] = np.where(j % 2 == 0, 1, -1)
    poolm = np.zeros((4, 512, 512))
    for g, win in enumerate((2, 4, 8, 16)):
        def mean(n):
            m = np.zeros((n, n))
            lo, hi = win // 2, win - 1 - win // 2
            for t in range(n):
                a, b = max(t - lo, 0), min(t + hi, n - 1)
                m[t, a:b + 1] = 1.0 / (b - a + 1)
            return m
        poolm[g] = (np.kron(mean(8), mean(64)) - np.eye(512)).T
    return c, sel.reshape(GATE_ROWS, 1024), dft.astype(np.float32), poolm.astype(np.float32)


def kernel(x, c, norm1_g, norm2_g, ada_w, ada_b, w_in, w_fourier, w_ret, w_out, ffn_up, conv_w, conv_b,
           ffn_down, final_g, c_2, ctx_2, c_ctx_2, w_mod_2, b_mod_2, norm_pre_2, norm_post_2,
           ffn_w_in_2, ffn_w_out_2, w_in_2, w_out_2, conv_w_2, conv_b_2, w_q_2, w_k_2, i_bias_2,
           f_bias_2, head_norm_2, pool_w_2, pool_scale_2):
    import concourse.bacc as bacc
    from concourse.bass_utils import run_bass_kernel_spmd

    A = lambda a: np.ascontiguousarray(a)
    consts, sel, dft, poolm = constants()
    gate = np.zeros((1024, 128), np.float32)
    w2 = A(w_in_2)[0]
    for q in range(4):
        gate[:, 32 * q:32 * q + 4] = w2[:, 1536 + 4 * q:1540 + 4 * q]
    P = np.zeros((128, NP), np.float32)

    def put(name, a, at=0):
        a = A(a)
        P[:, PCOLS[name] + at:PCOLS[name] + at + a.shape[1]] = a

    cols = lambda a: A(a).reshape(-1, 128).T
    put("c", cols(c))
    put("c2", np.stack([cols(c_2), cols(c_ctx_2)], 2).reshape(128, 16))
    put("n1", cols(norm1_g))
    put("n2", cols(norm2_g))
    put("adab", cols(ada_b))
    put("fing", cols(final_g))
    put("bmod", np.repeat(cols(b_mod_2), 2, axis=1))
    put("npre", cols(norm_pre_2))
    put("npost", cols(norm_post_2))
    put("cw", cols(conv_w))
    put("cb", cols(conv_b))
    put("cw2", cols(conv_w_2))
    put("cb2", cols(conv_b_2))
    put("hn", cols(head_norm_2))
    put("ps", cols(pool_scale_2))
    for d in range(2):
        P[32 * d:32 * d + 4, PCOLS["ib"]] = A(i_bias_2)[0, d]
        P[32 * d:32 * d + 4, PCOLS["fb"]] = A(f_bias_2)[0, d]

    src = {"w_in": A(w_in), "w_fourier": A(w_fourier), "w_ret": A(w_ret), "w_out": A(w_out), "ffn_up": A(ffn_up),
           "ffn_down": A(ffn_down), "ada_w": A(ada_w), "w_mod": A(w_mod_2), "ffn_w_in": A(ffn_w_in_2)[0],
           "ffn_w_out": A(ffn_w_out_2)[0], "w_in2": A(w_in_2), "w_out2": A(w_out_2), "w_q": A(w_q_2)[0],
           "w_k": A(w_k_2)[0], "pool_w": A(pool_w_2)[0], "gate": gate[None], "dft": dft[None], "poolm": poolm}

    def build(chunks, dry):
        nc = bacc.Bacc("TRN2", target_bir_lowering=False, num_devices=1, dynamic_dma_scratch_size=1024)
        n = max(len(chunks), 1)
        ins = {"ws": (n, 128, 1024), "xT": (8, 128, S), "cT": (8, 128, C), "params": (128, NP),
               "consts": consts.shape, "sel": sel.shape}
        t = {k: nc.dram_tensor(k, v, F32, kind="ExternalInput").ap() for k, v in ins.items()}
        out = nc.dram_tensor("out", (8, 128, S), F32, kind="ExternalOutput").ap()
        program(nc, t["ws"], t["xT"], t["cT"], t["params"], t["consts"], t["sel"], out, chunks, dry)
        return nc

    chunks = []
    build(chunks, True)
    nc = build(chunks, False)
    ws = np.zeros((len(chunks), 128, 1024), np.float32)
    for i, (_, specs) in enumerate(chunks):
        for b, (name, l, r, q) in enumerate(specs):
            ws[i, :, b * 128:b * 128 + 128] = src[name][l, r:r + 128, q:q + 128]
    arrays = {"ws": ws, "xT": A(A(x)[0].T).reshape(8, 128, S), "cT": A(A(ctx_2)[0].T).reshape(8, 128, C),
              "params": P, "consts": consts, "sel": sel}
    r = run_bass_kernel_spmd(nc, [arrays], core_ids=[0])
    o = r.results[0]["out"]
    return A(o.reshape(D, S).T).reshape(1, S, D)
```

```python
from contextlib import ExitStack

import numpy as np

import concourse.bass as bass
from concourse import mybir

F32 = mybir.dt.float32
F32R = mybir.dt.float32r
ALU = mybir.AluOpType
ACT = mybir.ActivationFunctionType

S = 512
C = 256
D = 1024
DT = 8
FF = 2816
NH = 4
EPS = 1e-6
GATE_ROWS = 36
NS = 4
NW = 3
AHEAD = 2
NSLOT = 18


class Queue:

    def __init__(self, sem):
        self.sem = sem
        self.count = 0
        self.ops = []
        self.seen = {}

    def wait(self, *tokens):
        for token in tokens:
            if token is None:
                continue
            sem, value = token
            if self.seen.get(id(sem), 0) < value:
                self.seen[id(sem)] = value
                self.ops.append(lambda e, s=sem, v=value: e.wait_ge(s, v))

    def do(self, fn, *waits):
        self.wait(*waits)
        self.count += 1
        self.ops.append(lambda e, f=fn, s=self.sem: f(e).then_inc(s, 1))
        return (self.sem, self.count)

    def quiet(self, fn, *waits):
        self.wait(*waits)
        self.ops.append(fn)

    def run(self, e):
        for op in self.ops:
            op(e)


PCOLS = {}
_at = 0
for _name, _n in [("c", 8), ("c2", 16), ("n1", 16), ("n2", 16), ("adab", 96), ("fing", 8), ("bmod", 144),
                  ("npre", 24), ("npost", 24), ("cw", 264), ("cb", 88), ("cw2", 12), ("cb2", 4),
                  ("hn", 4), ("ps", 4), ("ib", 1), ("fb", 1)]:
    PCOLS[_name] = _at
    _at += _n
NP = _at


def program(nc, ws, wm, xT, cT, params, consts, sel_d, out, chunks, dry):
    nch = len(chunks)
    ctx = ExitStack()
    with ctx:
        def sem(name):
            return ctx.enter_context(nc.semaphore(name))

        def sb(name, shape, dt=F32, stack=None):
            return (stack or ctx).enter_context(nc.sbuf_tensor(name, shape, dt))

        pe, act, dve, pool, sp = (Queue(sem(f"s_{n}")) for n in ("pe", "act", "dve", "pool", "sp"))
        s_ws = [sem(f"s_ws{i}") for i in range(NS)]
        s_par, s_con, s_x, s_rope, s_out = (sem(n) for n in ("s_par", "s_con", "s_x", "s_rope", "s_out"))
        s_mk = sem("s_mk")

        stage = sb("stage", [128, NS, 1024])
        WH = sb("WH", [128, NW, 1024], F32R)
        WL = sb("WL", [128, NW, 1024], F32R)
        HH = sb("HH", [128, DT, S], F32R)
        HL = sb("HL", [128, DT, S], F32R)
        GH = sb("GH", [128, NSLOT, S], F32R)
        GL = sb("GL", [128, NSLOT, S], F32R)
        GHf = GH[:, :, :].rearrange("p a b -> p (a b)")
        GLf = GL[:, :, :].rearrange("p a b -> p (a b)")
        X = sb("X", [128, DT, S])
        Z = sb("Z", [128, DT, S])
        SCR = sb("SCR", [128, 6, S])
        SSQ = sb("SSQ", [128, S])
        DG = sb("DG", [128, S])
        PAR = sb("PAR", [128, NP])
        MOD = sb("MOD", [128, 2, 48])
        MOD2 = sb("MOD2", [128, 72, 2])
        CS = sb("CS", [128, 8])
        CS2 = sb("CS2", [128, 8, 2])
        AB = sb("AB", [128, 8])
        V4 = sb("V4", [128, 8])
        HM = sb("HM", [128, 4])
        OC = sb("OC", [128, 3])
        IDN = sb("IDN", [128, 128])
        ONE = sb("ONE", [128, 128])
        VM = sb("VM", [128, 8])
        ONR = sb("ONR", [128, 128], F32R)
        st1 = ctx.enter_context(ExitStack())
        ACC = sb("ACC", [128, 2, 512], stack=st1)
        MST = sb("MST", [128, 2, 1024], stack=st1)

        PS = [ctx.enter_context(nc.psum_tensor(f"ps{i}", [128, S], F32)) for i in range(8)]
        STAT, MODP = PS[6], PS[7]

        def par(name, i, n=1):
            return PAR[:, PCOLS[name] + i:PCOLS[name] + i + n]

        class Ring:

            def __init__(self, n):
                self.idle = list(range(n))
                self.last = [()] * n

            def take(self):
                i = self.idle.pop(0)
                return i, self.last[i]

            def give(self, i, *tokens):
                assert i not in self.idle
                self.last[i] = tokens
                self.idle.append(i)

        banks = Ring(6)
        scr = Ring(6)

        class Stream:
            def __init__(self):
                self.n = -1
                self.used = 8
                self.loaded = 0
                self.ready = {}
                self.slot_free = [()] * NW
                self.stage_free = {}
                self.next = 0

            def open(self):
                if not dry:
                    for i in range(min(NS, nch)):
                        self.load(i, ())

            def load(self, i, free):
                sp.wait(*free)
                sp.ops.append(lambda e, i=i: e.dma_start(stage[:, i % NS, :], ws[i]).then_inc(s_ws[i % NS], 16))
                self.loaded = i + 1

            def landed(self, i):
                return (s_ws[i % NS], 16 * (i // NS + 1))

            def freed(self, i, *tokens):
                self.stage_free[i] = tokens
                while self.loaded < nch and self.loaded - NS in self.stage_free:
                    self.load(self.loaded, self.stage_free.pop(self.loaded - NS))

            def prepare(self, upto):
                while self.next <= min(upto, nch - 1):
                    i = self.next
                    slot = i % NW
                    if self.slot_free[slot] is None:
                        assert i > self.n
                        break
                    self.next += 1
                    src = stage[:, i % NS, :]
                    free = self.slot_free[slot]
                    self.slot_free[slot] = None
                    hi = act.do(lambda e, o=WH[:, slot, :], s=src: e.activation(o, s, ACT.Copy),
                                self.landed(i), *free)
                    lo = dve.do(lambda e, o=WL[:, slot, :], s=src, h=WH[:, slot, :].bitcast(F32):
                                e.tensor_tensor(o, s, h, ALU.subtract), self.landed(i), hi, *free)
                    self.ready[i] = lo
                    self.freed(i, lo)

            def start(self):
                self.n += 1
                self.used = 0
                if dry:
                    chunks.append([])
                else:
                    self.prepare(self.n + AHEAD)
                    pe.wait(self.ready[self.n])

            def block(self, specs):
                if self.used + len(specs) > 8:
                    self.start()
                    self.cur = self.n
                if dry:
                    chunks[self.cur].extend(specs)
                a = self.used * 128
                self.used += len(specs)
                b = self.used * 128
                if dry:
                    return WH[:, 0, a:b], WL[:, 0, a:b]
                slot = self.cur % NW
                return WH[:, slot, a:b], WL[:, slot, a:b]

            def done(self, token):
                if not dry:
                    self.slot_free[self.cur % NW] = (token,)

            def close(self):
                self.used = 8

        st = Stream()

        def mm3(o, wh, wl, mh, ml, start, stop, *waits):
            pe.quiet(lambda e: e.matmul(o, wh, mh, start=start, stop=False), *waits)
            pe.quiet(lambda e: e.matmul(o, wh, ml, start=False, stop=False))
            return pe.do(lambda e: e.matmul(o, wl, mh, start=False, stop=stop))

        def col_specs(name, l, k, n):
            return (name, l, k * 128, n * 128)

        mod_tok = {}
        mod_jobs = [("ada", 0, v) for v in range(6)] + [("ada", 1, v) for v in range(6)] \
            + [("mod", 0, v) for v in range(9)]
        mod_state = {"free": (), "acc_free": (), "due": None}

        def mod_sum():
            which, l, v, half, tok = mod_state["due"]
            mod_state["due"] = None
            nv = 1 if which == "ada" else 2
            if half == 0:
                pe.wait(*mod_state["free"])
            for t in range(4):
                for d in range(nv):
                    o = MODP[:, (half * 4 + t) * nv + d:(half * 4 + t) * nv + d + 1]
                    fn = lambda e, o=o, t=t, d=d: e.matmul(o, ACC[:, d, t * 128:t * 128 + 128], ONE[:, 0:1],
                                                           start=True, stop=True)
                    if t < 3 or d < nv - 1:
                        pe.quiet(fn, tok)
                    else:
                        done = pe.do(fn, tok)
            mod_state["acc_free"] = (done,)
            if half == 1:
                if which == "ada":
                    ev = dve.do(lambda e: e.tensor_tensor(MOD[:, l, v * 8:v * 8 + 8], MODP[:, 0:8],
                                                          par("adab", l * 48 + v * 8, 8), ALU.add), done)
                else:
                    ev = dve.do(lambda e: e.tensor_tensor(
                        MOD2[:, v * 8:v * 8 + 8, :].rearrange("p a b -> p (a b)"), MODP[:, 0:16],
                        par("bmod", v * 16, 16), ALU.add), done)
                mod_state["free"] = (ev,)
                mod_tok[(which, l, v)] = ev

        mod_list = [(name, l, v, half, q) for name, l, v in mod_jobs for half in range(2) for q in range(4)]
        mod_at = {"n": 0, "loaded": 0, "user": {}, "acc": [None, None]}
        mod_sem = [sem(f"s_md{i}") for i in range(6)]
        mod_uses = [0] * 6
        mod_slot = {}

        def mod_buffer(b):
            return MST[:, b, :] if b < 2 else Z[:, 2 * (b - 2):2 * (b - 1), :].rearrange("p a b -> p (a b)")

        def mod_load(q):
            m = mod_at["loaded"]
            if m >= len(mod_list):
                return
            mod_at["loaded"] += 1
            b = m % 6 if m < 16 else m % 2
            mod_uses[b] += 1
            mod_slot[m] = (b, (mod_sem[b], 16 * mod_uses[b]))
            q.wait(mod_at["user"].get(b))
            q.ops.append(lambda e, b=b, m=m: e.dma_start(mod_buffer(b), wm[m]).then_inc(mod_sem[b], 16))

        def mod_step():
            if mod_state["due"]:
                mod_sum()
            m = mod_at["n"]
            if m >= len(mod_list):
                return
            mod_at["n"] += 1
            if m >= 16 and mod_at["loaded"] <= m + 1:
                mod_load(act)
            which, l, v, half, q = mod_list[m]
            b, landed = mod_slot[m]
            w = mod_buffer(b)
            for kk in range(2):
                k = 2 * q + kk
                src = w[:, kk * 512:kk * 512 + 512]
                for d in range(1 if which == "ada" else 2):
                    c = CS[:, k:k + 1] if which == "ada" else CS2[:, k, d:d + 1]
                    if k == 0:
                        tok = dve.do(lambda e, src=src, c=c, d=d: e.tensor_scalar(ACC[:, d, :], src, c, None, ALU.mult),
                                     landed, cs_tok, *mod_state["acc_free"])
                    else:
                        tok = dve.do(lambda e, src=src, c=c, d=d: e.scalar_tensor_tensor(
                            out=ACC[:, d, :], in0=src, scalar=c, in1=ACC[:, d, :], op0=ALU.mult, op1=ALU.add),
                            landed, mod_at["acc"][d])
                    mod_at["acc"][d] = tok
            mod_at["user"][b] = tok
            if mod_at["loaded"] < 16:
                mod_load(sp)
            elif m == 14:
                mod_load(act)
            if q == 3:
                mod_state["due"] = (which, l, v, half, tok)

        def need(*job):
            while job not in mod_tok:
                mod_step()
            return mod_tok[job]

        sp.ops.append(lambda e: e.dma_start(PAR[:, :], params).then_inc(s_par, 16))
        for _ in range(6):
            mod_load(sp)
        sp.ops.append(lambda e: e.dma_start(IDN[:, :], consts[:, 0:128]).then_inc(s_con, 16))
        for t in range(DT):
            act.ops.append(lambda e, t=t: e.dma_start(X[:, t, :], xT[t]).then_inc(s_x, 16))
        par_ok, con_ok, x_ok = (s_par, 16), (s_con, 16), (s_x, 16 * DT)
        dve.do(lambda e: e.memset(ONE[:, :], 1.0))
        dve.do(lambda e: e.memset(OC[:, 0:1], 1.0 / 1024))
        dve.do(lambda e: e.memset(OC[:, 1:2], 1.0 / 256))
        dve.do(lambda e: e.memset(OC[:, 2:3], 1.0 / 128))
        dve.do(lambda e: e.memset(HM[:, :], -0.5))
        one_ok = dve.do(lambda e: e.memset(ONR[:, :].bitcast(F32), 1.0))
        cs1 = act.do(lambda e: e.activation(CS[:, :], par("c", 0, 8), ACT.Silu), par_ok)
        cs_tok = act.do(lambda e: e.activation(CS2[:, :, :].rearrange("p a b -> p (a b)"), par("c2", 0, 16), ACT.Silu))
        dve.wait(par_ok)
        pe.wait(one_ok)
        while mod_at["n"] < 10:
            mod_step()

        stat = {"free": ()}
        ssq = {"free": (), "ok": None}

        def take_scr(*qs):
            i, free = scr.take()
            for q in qs:
                q.wait(*free)
            return i, SCR[:, i, :]

        def take_bank():
            i, free = banks.take()
            pe.wait(*free)
            return i, PS[i]

        def split(src, hi, lo, *waits, bias=None, scale=None):
            if bias is None and scale is None:
                a = act.do(lambda e: e.activation(hi, src, ACT.Copy), *waits)
                return dve.do(lambda e: e.tensor_tensor(lo, src, hi.bitcast(F32), ALU.subtract), a, *waits)
            if scale is not None:
                a = act.do(lambda e: e.activation(hi, src, ACT.Copy, scale=scale), *waits)
                return dve.do(lambda e: e.scalar_tensor_tensor(out=lo, in0=src, scalar=scale, in1=hi.bitcast(F32),
                                                               op0=ALU.mult, op1=ALU.subtract), a, *waits)
            a = act.do(lambda e: e.activation(hi, src, ACT.Identity, bias=bias), *waits)
            return dve.do(lambda e: e.scalar_tensor_tensor(out=lo, in0=src, scalar=bias, in1=hi.bitcast(F32),
                                                           op0=ALU.add, op1=ALU.subtract), a, *waits)

        def add_ssq(src, n, first, *waits):
            if first:
                ssq["ok"] = act.do(lambda e: e.activation(SSQ[:, 0:n], src, ACT.Square), *waits, *ssq["free"])
                return ssq["ok"]
            i, t = take_scr(act)
            sq = act.do(lambda e: e.activation(t[:, 0:n], src, ACT.Square), *waits)
            ssq["ok"] = dve.do(lambda e: e.tensor_tensor(SSQ[:, 0:n], SSQ[:, 0:n], t[:, 0:n], ALU.add), sq, ssq["ok"])
            scr.give(i, ssq["ok"])
            return sq

        def rms_first(n, oc, summed=None):
            nt = n // 128
            if summed is None:
                pe.wait(ssq["ok"], *stat["free"])
                for t in range(nt):
                    fn = lambda e, t=t: e.matmul(STAT[:, t:t + 1], SSQ[:, t * 128:t * 128 + 128], OC[:, oc:oc + 1],
                                                 start=True, stop=True)
                    if t < nt - 1:
                        pe.quiet(fn)
                    else:
                        summed = pe.do(fn)
                ssq["free"] = (summed,)
            e1 = dve.do(lambda e: e.tensor_scalar(V4[:, 0:nt], STAT[:, 0:nt], EPS, None, ALU.add), summed)
            r4 = pool.do(lambda e: e.tensor_tensor(V4[:, 4:4 + nt], V4[:, 0:nt], HM[:, 0:nt], ALU.pow), e1, one_ok)
            dve.wait(con_ok, *stat.get("dg_free", ()))
            for t in range(nt):
                dg = dve.do(lambda e, t=t: e.tensor_scalar(DG[:, t * 128:t * 128 + 128], IDN[:, :],
                                                           V4[:, 4 + t:5 + t], None, ALU.mult), r4)
            stat["dg"] = dg
            return n

        def rms_last(n):
            for t in range(n // 128):
                tok = pe.do(lambda e, t=t: e.matmul(STAT[:, t * 128:t * 128 + 128], ONE[:, :], DG[:, t * 128:t * 128 + 128],
                                                    start=True, stop=True), stat["dg"])
            stat["dg_free"] = (tok,)
            return tok

        def rms(n, oc, summed=None):
            return rms_last(rms_first(n, oc, summed))

        def sum_pe(src, n, t, last, *waits):
            i, sq = take_scr(act)
            a = act.do(lambda e: e.activation(sq[:, 0:n], src, ACT.Square), *waits)
            if t == 0:
                pe.wait(*stat["free"])
            for q in range(n // 128):
                tok = pe.do(lambda e, q=q: e.matmul(STAT[:, q:q + 1], sq[:, q * 128:q * 128 + 128], OC[:, 0:1],
                                                    start=(t == 0 and q == 0), stop=last, skip_group_check=True), a)
            scr.give(i, tok)
            return tok, a

        def affine(src, dst, a_col, b_col, n, rtok, *waits):
            held = []
            last = None

            def low(i, tmp, t, hi):
                tok = dve.do(lambda e: e.scalar_tensor_tensor(out=dst(t)[1], in0=tmp, scalar=b_col(t), in1=dst(t)[0].bitcast(F32),
                                                              op0=ALU.add, op1=ALU.subtract), hi)
                scr.give(i, tok)
                oks.append(tok)

            oks = []
            for t in range(DT):
                i, tmp = take_scr(dve)
                tmp = tmp[:, 0:n]
                m = dve.do(lambda e, t=t, tmp=tmp: e.scalar_tensor_tensor(out=tmp, in0=src(t), scalar=a_col(t), in1=STAT[:, 0:n],
                                                                          op0=ALU.mult, op1=ALU.mult), rtok, *waits)
                hi = act.do(lambda e, t=t, tmp=tmp: e.activation(dst(t)[0], tmp, ACT.Identity, bias=b_col(t)), m, *waits)
                if held:
                    low(*held.pop())
                held.append((i, tmp, t, hi))
            stat["free"] = (m,)
            low(*held.pop())
            return oks

        def lin(nk, spec, mov, n, o, oks=(), bg=True):
            for k in range(nk):
                pe.wait(*oks[k:k + 1])
                wh, wl = st.block([spec(k)])
                mh, ml = mov(k)
                tok = mm3(o, wh, wl, mh, ml, k == 0, k == nk - 1)
                st.done(tok)
            if bg:
                mod_step()
            return tok

        def lin2(specs, mov, outs, oks):
            st.close()
            for k in range(8):
                pe.wait(oks[k])
                mh, ml = mov(k)
                for spec, o in zip(specs, outs):
                    wh, wl = st.block([spec(k)])
                    tok = mm3(o, wh, wl, mh, ml, k == 0, k == 7)
                    st.done(tok)
            mod_step()
            return tok

        def slot(i, n=S):
            return GH[:, i, 0:n], GL[:, i, 0:n]

        def hx(n=S):
            return lambda k: (HH[:, k, 0:n], HL[:, k, 0:n])

        MASK = sb("MASK", [128, 896], stack=st1)
        ROPE = sb("ROPE", [128, 2, S], stack=st1)
        DFTF = SCR[:, 0, 0:256]
        CH = sb("CH", [128, 256], F32R, stack=st1)
        CL = sb("CL", [128, 256], F32R, stack=st1)
        SG = None

        state = {"x": x_ok, "h_free": (), "g_free": (), "z_free": (), "mask_n": 0}
        st.open()
        sp.ops.append(lambda e: e.dma_start(DFTF, consts[:, 128:384]).then_inc(s_con, 16))
        sp.ops.append(lambda e: e.dma_start(ROPE[:, :, :].rearrange("p a b -> p (a b)"), consts[:, 384:1408]).then_inc(s_rope, 16))
        i, _ = scr.take()
        dft_ok = split(DFTF, CH[:, :], CL[:, :], (s_con, 32))
        scr.give(i, dft_ok)
        mask_free = [None]

        def load_mask(h):
            state["mask_n"] += 1
            sp.wait(mask_free[0])
            sp.ops.append(lambda e: e.dma_start(MASK[:, :], consts[:, 1408 + h * 896:1408 + (h + 1) * 896]).then_inc(s_mk, 16))
            return (s_mk, 16 * state["mask_n"])

        def token_mix(l):
            need("ada", l, 0)
            mtok = need("ada", l, 1)
            ab = dve.do(lambda e: e.scalar_tensor_tensor(out=AB[:, :], in0=MOD[:, l, 8:16], scalar=1.0, in1=par("n1", l * 8, 8),
                                                         op0=ALU.add, op1=ALU.mult), mtok, *state.get("ab_free", ()))
            r = rms(S, 0, state.pop("summed", None))
            h_ok = affine(lambda t: X[:, t, :], lambda t: (HH[:, t, :], HL[:, t, :]), lambda t: AB[:, t:t + 1],
                          lambda t: MOD[:, l, t:t + 1], S, r, ab, state["x"], mtok, *state["h_free"])
            state["ab_free"] = (h_ok[-1],)
            x_ready = state["x"]

            uf = [slice(16 * S, 16 * S + 640)]
            uf_free = [tuple(state["g_free"])]
            zero = []
            for b in range(1):
                for T in (GHf, GLf):
                    z = T[:, uf[b]]
                    dve.do(lambda e, z=z: e.memset(z[:, 512:640].bitcast(F32), 0.0), *uf_free[b])
                    zero.append(dve.do(lambda e, z=z: e.memset(z[:, 256:257].bitcast(F32), 0.0)))
            folded = []
            dfts = []
            pend = []

            def channel_dft(g, b, tok):
                i, p = take_bank()
                pe.wait(tok, zero[-1], dft_ok)
                uh, ul = GHf[:, uf[b]], GLf[:, uf[b]]
                for t in range(4):
                    cc = slice(0, 128) if t < 2 else slice(128, 256)
                    o = p[:, t * 128:t * 128 + 128]
                    tok = mm3(o, uh[:, t * 128:t * 128 + 128], ul[:, t * 128:t * 128 + 128], CH[:, cc], CL[:, cc],
                              True, t != 2)
                    if t == 2:
                        tok = mm3(o, uh[:, 512:640], ul[:, 512:640], CH[:, 0:128], CL[:, 0:128], False, True)
                uf_free[b] = (tok,)
                ev = split(p[:, :], *slot(8 + g), tok, *state["g_free"])
                banks.give(i, ev)
                dfts.append(ev)

            pair = [take_bank(), take_bank()]
            tok2 = lin2([lambda k: ("w_in", l, k * 128, 0), lambda k: ("w_in", l, k * 128, 128)], hx(),
                        [q[1][:, :] for q in pair], h_ok)
            for g in range(8):
                if g < 2:
                    (i, p), tok = pair[g], tok2
                else:
                    i, p = take_bank()
                    tok = lin(8, lambda k, g=g: ("w_in", l, k * 128, g * 128), hx(), S, p[:, :])
                j, U = take_scr(act)
                cp = act.do(lambda e, U=U, p=p: e.activation(U, p[:, :], ACT.Copy), tok)
                banks.give(i, cp)
                b = 0
                m, W = take_scr(dve)
                dve.do(lambda e, U=U, W=W: e.tensor_tensor(W[:, 1:256], U[:, 1:256], U[:, 511:256:-1], ALU.add), cp)
                dve.do(lambda e, U=U, W=W: e.tensor_tensor(W[:, 257:512], U[:, 1:256], U[:, 511:256:-1], ALU.subtract))
                fo = dve.do(lambda e, U=U, W=W: e.tensor_copy(W[:, 0:512:256], U[:, 0:512:256]))
                if pend:
                    channel_dft(*pend.pop())
                uh, ul = GHf[:, uf[b]], GLf[:, uf[b]]

                def halves(dst, src, *w):
                    a = act.do(lambda e: e.activation(dst[0], src, ACT.Copy), *w)
                    return dve.do(lambda e: e.tensor_tensor(dst[1], src, dst[0].bitcast(F32), ALU.subtract), a)

                w = (fo, *uf_free[b], *zero)
                halves((uh[:, 0:256], ul[:, 0:256]), W[:, 0:256], *w)
                halves((uh[:, 257:512], ul[:, 257:512]), W[:, 257:512], *w)
                fd = halves((uh[:, 512:513], ul[:, 512:513]), W[:, 256:257], *w)
                scr.give(j, fo)
                scr.give(m, fd)
                pend.append((g, b, fd))
            st.close()
            gates = {}

            def gate(base, n):
                i, p = take_bank()
                tok = lin(8, lambda k: ("w_in", l, k * 128, (base + n) * 128), hx(), S, p[:, :])
                j, sg = take_scr(act)
                sk = act.do(lambda e: e.activation(sg, p[:, :], ACT.Sigmoid), tok)
                banks.give(i, sk)
                gates[n] = (j, sg, sk)

            channel_dft(*pend.pop())
            gate(40, 0)
            pe.wait(*dfts)
            st.close()
            tabs = []
            for q in range(2):
                a = st.block([("dft", 0, 2 * q * 128, c * 128) for c in range(4)])
                first = st.cur
                b = st.block([("dft", 0, (2 * q + 1) * 128, c * 128) for c in range(4)])
                tabs += [(a, st.cur), (b, st.cur)]
            f_ok = []
            for g in range(8):
                i, p = take_bank()
                for t in range(4):
                    (th, tl), _ = tabs[t]
                    tok = mm3(p[:, :], GH[:, 8 + g, t * 128:t * 128 + 128], GL[:, 8 + g, t * 128:t * 128 + 128], th, tl,
                              t == 0, t == 3)
                ev = split(p[:, :], *slot(g), tok, *state["g_free"])
                banks.give(i, ev)
                f_ok.append(ev)
            if not dry:
                for (_, cur) in tabs:
                    st.slot_free[cur % NW] = (tok,)
            st.close()
            m1_ok = []
            for n in range(8):
                if n:
                    gate(40, n)
                i, p = take_bank()
                tok = lin(8, lambda k, n=n: ("w_fourier", l, k * 128, n * 128), slot, S, p[:, :], f_ok)
                j, sg, sk = gates[n]
                ev = dve.do(lambda e, n=n, p=p, sg=sg: e.tensor_tensor(Z[:, n, :], p[:, :], sg, ALU.mult), tok, sk, *state["z_free"])
                banks.give(i, ev)
                scr.give(j, ev)
                m1_ok.append(ev)
            fourier_read = tok

            g_free = (fourier_read,)
            qk_free = g_free
            v_free = g_free
            s_free = g_free
            qk_ok, v_ok, s_ok, sg_ok, r_ok = {}, {}, {}, {}, []
            masks = {0: load_mask(0)}
            sg_slot = {}

            def part_a(h):
                nonlocal qk_free
                toks = []
                for w, base in ((0, 8 + 2 * h), (1, 16 + 2 * h)):
                    b = []
                    for t in range(2):
                        i, p = take_bank()
                        tok = lin(8, lambda k, c=base + t: ("w_in", l, k * 128, c * 128), hx(), S, p[:, :])
                        b.append((i, p, tok))
                    (i0, p0, k0), (i1, p1, k1) = b
                    dve.wait((s_rope, 16))
                    for half in range(2):
                        ja, A = take_scr(dve)
                        jb, B = take_scr(dve)
                        ca, cb = (0, 1) if half == 0 else (1, 0)
                        dve.do(lambda e, A=A, p0=p0, ca=ca: e.tensor_tensor(A, p0[:, :], ROPE[:, ca, :], ALU.mult), k0)
                        mb = dve.do(lambda e, B=B, p1=p1, cb=cb: e.tensor_tensor(B, p1[:, :], ROPE[:, cb, :], ALU.mult), k1)
                        rr = dve.do(lambda e, A=A, B=B, half=half: e.tensor_tensor(A, A, B, ALU.subtract if half == 0 else ALU.add), mb)
                        ok = split(A, *slot(2 * w + half), rr, *qk_free)
                        scr.give(ja, ok)
                        scr.give(jb, rr)
                        toks.append(ok)
                    banks.give(i0, mb)
                    banks.give(i1, mb)
                qk_ok[h] = toks

            def part_b(h, between=None):
                st.close()
                ch = []
                for q in range(2):
                    for kk in range(4):
                        ch.append(st.block([("w_in", l, (q * 4 + kk) * 128, (24 + 2 * h + c) * 128) for c in range(2)]))
                        cur = st.cur
                    ch[-1] = ch[-1]
                    if q == 0:
                        first = st.cur
                v = []
                for q in range(2):
                    i, p = take_bank()
                    for t in (2 * q, 2 * q + 1):
                        for k in range(8):
                            wh, wl = ch[k]
                            sl = slice(t * 128, t * 128 + 128)
                            tok = mm3(p[:, (t % 2) * 256:(t % 2) * 256 + 256], HH[:, k, sl], HL[:, k, sl], wh, wl, k == 0, k == 7)
                    v.append((i, p, tok))
                    if q == 0 and between:
                        between()
                if not dry:
                    st.slot_free[first % NW] = (tok,)
                    st.done(tok)
                st.close()
                toks = []
                for q in range(2):
                    i, p, tok = v[q]
                    j, junk = take_scr(act)
                    sms = []
                    for t in range(2):
                        sms.append(act.do(lambda e, p=p, t=t, q=q, junk=junk: e.activation(
                            junk[:, t * 256:t * 256 + 256], p[:, t * 256:t * 256 + 256], ACT.Copy,
                            accum_out=VM[:, 2 * q + t:2 * q + t + 1]), tok, *state.get("vm_free", ())))
                    nm = dve.do(lambda e, q=q: e.tensor_scalar(VM[:, 4 + 2 * q:6 + 2 * q], VM[:, 2 * q:2 * q + 2], -1.0 / 256, None, ALU.mult), sms[-1])
                    for t in range(2):
                        sl = slice(t * 256, t * 256 + 256)
                        hi = act.do(lambda e, p=p, q=q, t=t, sl=sl: e.activation(
                            GH[:, 4 + q, sl], p[:, sl], ACT.Identity, bias=VM[:, 4 + 2 * q + t:5 + 2 * q + t]), nm, *v_free)
                    for t in range(2):
                        sl = slice(t * 256, t * 256 + 256)
                        ok = dve.do(lambda e, p=p, q=q, t=t, sl=sl: e.scalar_tensor_tensor(
                            out=GL[:, 4 + q, sl], in0=p[:, sl], scalar=VM[:, 4 + 2 * q + t:5 + 2 * q + t],
                            in1=GH[:, 4 + q, sl].bitcast(F32), op0=ALU.add, op1=ALU.subtract), hi, *v_free)
                    banks.give(i, ok)
                    scr.give(j, ok)
                    toks.append(ok)
                state["vm_free"] = (ok,)
                v_ok[h] = toks
                mod_step()
                sg_ok[h] = []
                for t in range(2):
                    i, p = take_bank()
                    tok = lin(8, lambda k, t=t: ("w_in", l, k * 128, (32 + 2 * h + t) * 128), hx(), S, p[:, :])
                    j, sg = take_scr(act)
                    sk = act.do(lambda e, p=p, sg=sg: e.activation(sg, p[:, :], ACT.Silu), tok)
                    banks.give(i, sk)
                    sg_ok[h].append((j, sg, sk))

            def part_c(h):
                nonlocal s_free, qk_free
                mtok = masks[h]
                pe.wait(*qk_ok[h])
                s_ok[h] = []
                for jt in range(4):
                    i, p = take_bank()
                    for t in range(2):
                        sl = slice(jt * 128, jt * 128 + 128)
                        tok = mm3(p[:, :], GH[:, 2 + t, sl], GL[:, 2 + t, sl], GH[:, t, :], GL[:, t, :], t == 0, t == 1)
                    j, T = take_scr(dve)
                    m = dve.do(lambda e, T=T, p=p, jt=jt: e.tensor_tensor(
                        T, p[:, :], MASK[:, 384 - 128 * jt:896 - 128 * jt], ALU.mult), tok, mtok)
                    banks.give(i, m)
                    a = act.do(lambda e, T=T, jt=jt: e.activation(GH[:, 6 + jt, :], T, ACT.Copy), m, *s_free)
                    lo = pool.do(lambda e, T=T, jt=jt: e.tensor_tensor(GL[:, 6 + jt, :], T, GH[:, 6 + jt, :].bitcast(F32), ALU.subtract), m, a, *s_free)
                    scr.give(j, lo)
                    s_ok[h].append(lo)
                mask_free[0] = m
                if h + 1 < NH:
                    masks[h + 1] = load_mask(h + 1)
                qk_free = (tok,)

            def part_d(h):
                nonlocal v_free, s_free
                pe.wait(*v_ok[h])
                ys = []
                for t in range(2):
                    i, p = take_bank()
                    for jt in range(4):
                        a = (jt % 2) * 256 + t * 128
                        tok = mm3(p[:, :], GH[:, 4 + jt // 2, a:a + 128], GL[:, 4 + jt // 2, a:a + 128],
                                  GH[:, 6 + jt, :], GL[:, 6 + jt, :], jt == 0, jt == 3, s_ok[h][jt])
                    sq = add_ssq(p[:, :], S, t == 0, tok)
                    j, sg, sk = sg_ok[h][t]
                    yg = dve.do(lambda e, p=p, sg=sg: e.tensor_tensor(sg, p[:, :], sg, ALU.mult), sq, sk)
                    banks.give(i, yg)
                    ys.append((j, sg, yg))
                v_free = (tok,)
                s_free = (tok,)
                return h, ys

            def part_e(h, ys):
                r = rms_last(S)
                for t in range(2):
                    j, sg, yg = ys[t]
                    m = dve.do(lambda e, sg=sg: e.tensor_tensor(sg, STAT[:, :], sg, ALU.mult), r, yg)
                    ok = split(sg, *slot(10 + 2 * h + t), m, fourier_read)
                    scr.give(j, ok)
                    r_ok.append(ok)
                stat["free"] = (m,)

            part_a(0)
            part_b(0)
            part_c(0)
            for h in range(NH):
                if h + 1 < NH:
                    part_a(h + 1)
                d = part_d(h)
                rms_first(S, 1)
                if h + 1 == NH:
                    gates.clear()
                    gate(48, 0)
                    part_e(*d)
                else:
                    part_b(h + 1, lambda: part_e(*d))
                    part_c(h + 1)

            gread = v_free + qk_free + s_free
            mg_ok = []
            for n in range(8):
                i, p = take_bank()
                if n:
                    gate(48, n)
                tok = lin(8, lambda k, n=n: ("w_ret", l, k * 128, n * 128), lambda k: slot(10 + k), S, p[:, :], r_ok)
                j, sg, sk = gates[n]
                dve.do(lambda e, p=p, sg=sg: e.tensor_tensor(sg, p[:, :], sg, ALU.mult), tok, sk)
                ev = (dve.sem, dve.count)
                banks.give(i, ev)
                ad = dve.do(lambda e, sg=sg, n=n: e.tensor_tensor(sg, sg, Z[:, n, :], ALU.add), ev, m1_ok[n])
                ok = split(sg, *slot(n), ad, *gread)
                scr.give(j, ok)
                mg_ok.append(ok)
            state["h_free"] = (tok,)
            state["z_free"] = (ad,)
            gtok = need("ada", l, 2)
            for n in range(8):
                i, p = take_bank()
                tok = lin(8, lambda k, n=n: ("w_out", l, k * 128, n * 128), slot, S, p[:, :], mg_ok)
                ev = dve.do(lambda e, n=n, p=p: e.scalar_tensor_tensor(
                    out=X[:, n, :], in0=p[:, :], scalar=MOD[:, l, 16 + n:17 + n], in1=X[:, n, :], op0=ALU.mult, op1=ALU.add),
                    tok, gtok, x_ready)
                banks.give(i, ev)
                add_ssq(X[:, n, :], S, n == 0, ev)
            state["x"] = ev
            state["g_free"] = (tok,)

        def conv_ffn(l):
            need("ada", l, 3)
            mtok = need("ada", l, 4)
            ab = dve.do(lambda e: e.scalar_tensor_tensor(out=AB[:, :], in0=MOD[:, l, 32:40], scalar=1.0, in1=par("n2", l * 8, 8),
                                                         op0=ALU.add, op1=ALU.mult), mtok, *state["ab_free"])
            r = rms(S, 0)
            h_ok = affine(lambda t: X[:, t, :], lambda t: (HH[:, t, :], HL[:, t, :]), lambda t: AB[:, t:t + 1],
                          lambda t: MOD[:, l, 24 + t:25 + t], S, r, ab, state["x"], mtok, *state["h_free"])
            state["ab_free"] = (h_ok[-1],)
            for half in range(2):
                hid = []
                for jj in range(11):
                    j0 = half * 11 + jj
                    t2 = []
                    if j0 == 0:
                        pair = [take_bank(), take_bank()]
                        tok2 = lin2([lambda k, c=c: ("ffn_up", l, k * 128, c * 128) for c in (0, 22)], hx(),
                                    [q[1][:, :] for q in pair], h_ok)
                    for c in (j0, 22 + j0):
                        if j0 == 0:
                            (i, p), tok = pair[c // 22], tok2
                        else:
                            i, p = take_bank()
                            tok = lin(8, lambda k, c=c: ("ffn_up", l, k * 128, c * 128), hx(), S, p[:, :])
                        h_read = tok
                        m, T = take_scr(act)
                        cw = lambda tap, c=c: par("cw", (l * 3 + tap) * 44 + c)
                        a = act.do(lambda e, T=T, p=p, c=c, cw=cw: e.activation(T, p[:, :], ACT.Identity, scale=cw(1), bias=par("cb", l * 44 + c)), tok)
                        b1 = dve.do(lambda e, T=T, p=p, cw=cw: e.scalar_tensor_tensor(
                            out=T[:, 1:S], in0=p[:, 0:S - 1], scalar=cw(0), in1=T[:, 1:S], op0=ALU.mult, op1=ALU.add), a)
                        b2 = dve.do(lambda e, T=T, p=p, cw=cw: e.scalar_tensor_tensor(
                            out=T[:, 0:S - 1], in0=p[:, 1:S], scalar=cw(2), in1=T[:, 0:S - 1], op0=ALU.mult, op1=ALU.add), b1)
                        banks.give(i, b2)
                        if c == j0:
                            b2 = act.do(lambda e, T=T: e.activation(T, T, ACT.Gelu), b2)
                        t2.append((m, T, b2))
                    (m1, A, ka), (m2, B, kb) = t2
                    hm = dve.do(lambda e, A=A, B=B: e.tensor_tensor(B, A, B, ALU.mult), ka, kb)
                    ok = split(B, *slot(jj), hm, *state["g_free"])
                    scr.give(m1, hm)
                    scr.give(m2, ok)
                    hid.append(ok)
                if half == 1:
                    state["h_free"] = (h_read,)
                gtok = need("ada", l, 5)
                for n in range(8):
                    i, p = take_bank()
                    tok = lin(11, lambda k, n=n: ("ffn_down", l, (half * 11 + k) * 128, n * 128), slot, S, p[:, :], hid)
                    ev = dve.do(lambda e, n=n, p=p: e.scalar_tensor_tensor(
                        out=X[:, n, :], in0=p[:, :], scalar=MOD[:, l, 40 + n:41 + n], in1=X[:, n, :], op0=ALU.mult, op1=ALU.add),
                        tok, gtok, state["x"])
                    banks.give(i, ev)
                    if half:
                        add_ssq(X[:, n, :], S, n == 0, ev)
                state["x"] = ev
                state["g_free"] = (tok,)

        if not dry:
            pass
        for t in range(DT):
            state["summed"], _ = sum_pe(X[:, t, :], S, t, t == DT - 1, x_ok)
        st.prepare(AHEAD - 1)
        for l in range(2):
            token_mix(l)
            conv_ffn(l)
        r = rms(S, 0)
        for t in range(DT):
            ev = dve.do(lambda e, t=t: e.scalar_tensor_tensor(out=X[:, t, :], in0=X[:, t, :], scalar=par("fing", t), in1=STAT[:, :],
                                                              op0=ALU.mult, op1=ALU.mult), r, state["x"], ssq["ok"])
        stat["free"] = (ev,)
        state["x"] = ev
        need("mod", 0, 8)
        st1.close()

        GT = sb("GT", [GATE_ROWS, 4, 768])
        SEL = sb("SEL", [GATE_ROWS, 8, 128])
        TRI = sb("TRI", [128, 2, 128])
        GC = sb("GC", [128, 6, GATE_ROWS])
        RC = sb("RC", [128, 8])
        old = ((pe.sem, pe.count), (dve.sem, dve.count), (act.sem, act.count))
        sp.wait(*old)
        sp.ops.append(lambda e: e.dma_start(SEL[:, :, :].rearrange("p a b -> p (a b)"), sel_d).then_inc(s_rope, 16))
        sp.ops.append(lambda e: e.dma_start(TRI[:, :, :].rearrange("p a b -> p (a b)"), consts[:, 4992:5248]).then_inc(s_rope, 16))
        sp.wait(*state["z_free"])
        for t in range(DT):
            sp.ops.append(lambda e, t=t: e.dma_start(Z[:, t, 256:512], cT[t]).then_inc(s_x, 16))
        sel_ok = (s_rope, 48)
        xc_ok = (s_x, 32 * DT)

        def ada_norm(j, col, src, dst, n, *waits):
            need("mod", 0, 3 * j)
            mtok = need("mod", 0, 3 * j + 1)
            ab = dve.do(lambda e: e.scalar_tensor_tensor(out=AB[:, :], in0=MOD2[:, 24 * j + 8:24 * j + 16, col], scalar=1.0,
                                                         in1=par("npre", j * 8, 8), op0=ALU.add, op1=ALU.mult), mtok, *state["ab_free"])
            r = rms(n, 0, state.pop("summed", None))
            ok = affine(src, dst, lambda t: AB[:, t:t + 1], lambda t: MOD2[:, 24 * j + t, col:col + 1], n, r, ab, mtok, *waits)
            state["ab_free"] = (ok[-1],)
            return ok

        def swiglu(f, n, zt, h_ok, *waits):
            for half in range(2):
                hid = []
                for jj in range(11):
                    j0 = half * 11 + jj
                    i0, p0 = take_bank()
                    if j0 == 0:
                        i1, p1 = take_bank()
                        tok2 = tok = lin2([lambda k, c=c: ("ffn_w_in", f, k * 128, c * 128) for c in (0, 22)], hx(n),
                                          [p0[:, 0:n], p1[:, 0:n]], h_ok)
                    else:
                        tok = lin(8, lambda k: ("ffn_w_in", f, k * 128, j0 * 128), hx(n), n, p0[:, 0:n])
                    m, T = take_scr(act)
                    T = T[:, 0:n]
                    a = act.do(lambda e, T=T, p0=p0: e.activation(T, p0[:, 0:n], ACT.Silu), tok)
                    banks.give(i0, a)
                    if j0:
                        i1, p1 = take_bank()
                        tok = lin(8, lambda k: ("ffn_w_in", f, k * 128, (22 + j0) * 128), hx(n), n, p1[:, 0:n])
                    h_read = tok
                    hm = dve.do(lambda e, T=T, p1=p1: e.tensor_tensor(T, p1[:, 0:n], T, ALU.mult), tok, a)
                    banks.give(i1, hm)
                    ok = split(T, *slot(jj, n), hm, *state["g_free"])
                    scr.give(m, ok)
                    hid.append(ok)
                if half == 1:
                    state["h_free"] = (h_read,)
                for nn in range(8):
                    i, p = take_bank()
                    tok = lin(11, lambda k, nn=nn: ("ffn_w_out", f, (half * 11 + k) * 128, nn * 128), lambda k: slot(k, n), n,
                              p[:, 0:n], hid)
                    z = zt(nn)
                    if half == 0:
                        ev = act.do(lambda e, z=z, p=p: e.activation(z, p[:, 0:n], ACT.Copy), tok, *waits)
                    else:
                        ev = dve.do(lambda e, z=z, p=p: e.tensor_tensor(z, p[:, 0:n], z, ALU.add), tok, z_prev)
                        add_ssq(z, n, nn == 0, ev)
                    banks.give(i, ev)
                z_prev = ev
                state["g_free"] = (tok,)
            return ev

        def ada_out(j, col, res_w, zt, xt, n, z_ok, x_tok, more=True):
            mtok = need("mod", 0, 3 * j + 2)
            rc = dve.do(lambda e: e.scalar_tensor_tensor(out=RC[:, :], in0=MOD2[:, 24 * j + 16:24 * j + 24, col], scalar=res_w,
                                                         in1=par("npost", j * 8, 8), op0=ALU.mult, op1=ALU.mult), mtok)
            r = rms(n, 0)
            xs = []
            for t in range(DT):
                i, T = take_scr(dve)
                T = T[:, 0:n]
                m = dve.do(lambda e, t=t, T=T: e.scalar_tensor_tensor(out=T, in0=zt(t), scalar=RC[:, t:t + 1], in1=STAT[:, 0:n],
                                                                      op0=ALU.mult, op1=ALU.mult), r, rc, z_ok)
                ev = dve.do(lambda e, t=t, T=T: e.tensor_tensor(xt(t), xt(t), T, ALU.add), m, x_tok)
                scr.give(i, ev)
                if more:
                    xs.append(ev)
            stat["free"] = (m,)
            if more:
                for t in range(DT):
                    summed, _ = sum_pe(xt(t), n, t, t == DT - 1, xs[t], m)
                state["summed"] = summed
            return ev

        zc = lambda t: Z[:, t, 0:256]
        xc = lambda t: Z[:, t, 256:512]
        zx = lambda t: Z[:, t, :]
        xx = lambda t: X[:, t, :]
        hcs = lambda t: (GH[:, 14 + t // 2, (t % 2) * 256:(t % 2) * 256 + 256], GL[:, 14 + t // 2, (t % 2) * 256:(t % 2) * 256 + 256])

        x_ssq_first = state["x"]
        for t in range(DT):
            add_ssq(xc(t), C, t == 0, xc_ok)
        h_ok = ada_norm(0, 1, xc, lambda t: (HH[:, t, 0:C], HL[:, t, 0:C]), C, xc_ok, *state["h_free"])
        z_ok = swiglu(0, C, zc, h_ok, *state["z_free"])
        c_ok = ada_out(0, 1, 0.5, zc, xc, C, z_ok, xc_ok)
        hc_ok = ada_norm(1, 1, xc, hcs, C, c_ok, *state["g_free"])

        for t in range(DT):
            add_ssq(xx(t), S, t == 0, x_ssq_first)
        h_ok = ada_norm(0, 0, xx, lambda t: (HH[:, t, :], HL[:, t, :]), S, state["x"], *state["h_free"])
        z_ok = swiglu(0, S, zx, h_ok, hc_ok[-1])
        x_tok = ada_out(0, 0, 0.5, zx, xx, S, z_ok, state["x"])
        h_ok = ada_norm(1, 0, xx, lambda t: (HH[:, t, :], HL[:, t, :]), S, x_tok, *state["h_free"])
        pe.wait(h_ok[-1], hc_ok[-1])
        g_free = state["g_free"]
        UH, UL = GHf[:, 0:3072], GLf[:, 0:3072]
        lat, con = slice(256, 768), slice(0, 256)

        u_ok = []
        for h in range(NH):
            ix, px = take_bank()
            ic, pc = take_bank()
            for k in range(8):
                wh, wl = st.block([("w_in2", 0, k * 128, h * 128)])
                mm3(px[:, :], wh, wl, HH[:, k, :], HL[:, k, :], k == 0, k == 7)
                tok = mm3(pc[:, 0:C], wh, wl, *hcs(k), k == 0, k == 7)
                st.done(tok)
            mod_step()
            for p, i, n, cols in ((px, ix, S, lat), (pc, ic, C, con)):
                m, T = take_scr(act)
                cw = lambda tap, h=h: par("cw2", tap * 4 + h)
                a = act.do(lambda e, T=T, p=p, n=n, cw=cw, h=h: e.activation(
                    T[:, 0:n], p[:, 0:n], ACT.Identity, scale=cw(1), bias=par("cb2", h)), tok)
                b1 = dve.do(lambda e, T=T, p=p, n=n, cw=cw: e.scalar_tensor_tensor(
                    out=T[:, 1:n], in0=p[:, 0:n - 1], scalar=cw(0), in1=T[:, 1:n], op0=ALU.mult, op1=ALU.add), a)
                b2 = dve.do(lambda e, T=T, p=p, n=n, cw=cw: e.scalar_tensor_tensor(
                    out=T[:, 0:n - 1], in0=p[:, 1:n], scalar=cw(2), in1=T[:, 0:n - 1], op0=ALU.mult, op1=ALU.add), b1)
                banks.give(i, b2)
                sl = act.do(lambda e, T=T, n=n: e.activation(T[:, 0:n], T[:, 0:n], ACT.Silu), b2)
                a0 = h * 768 + cols.start
                ok = split(T[:, 0:n], UH[:, a0:a0 + n], UL[:, a0:a0 + n], sl, *g_free)
                scr.give(m, ok)
                u_ok.append(ok)

        st.close()
        bs = []
        for c in range(6):
            bs.append(take_bank())
        for k in range(8):
            wh, wl = st.block([("w_in2", 0, k * 128, 512 + q * 128) for q in range(4)])
            for c in range(6):
                if c < 2:
                    a, b = (x[:, c * 128:c * 128 + 128] for x in hcs(k))
                else:
                    a, b = HH[:, k, (c - 2) * 128:(c - 1) * 128], HL[:, k, (c - 2) * 128:(c - 1) * 128]
                tok = mm3(bs[c][1][:, :], a, b, wh, wl, k == 0, k == 7)
            st.done(tok)
        v_ok = []
        for c in range(6):
            i, p = bs[c]
            ok = split(p[:, :], *slot(6 + c), tok, *g_free)
            banks.give(i, ok)
            v_ok.append(ok)
        mod_step()

        ix, px = take_bank()
        ic, pc = take_bank()
        for k in range(8):
            wh, wl = st.block([("gate", 0, k * 128, 0)])
            mm3(px[:, :], wh, wl, HH[:, k, :], HL[:, k, :], k == 0, k == 7)
            tok = mm3(pc[:, 0:C], wh, wl, *hcs(k), k == 0, k == 7)
            st.done(tok)
        hc_read = tok
        T0, T1, T2, T3 = (GT[:, i, :] for i in range(4))
        for T, base in ((T0, 0), (T1, 64)):
            for p, c0, n in ((px, 256, S), (pc, 0, C)):
                dve.do(lambda e, T=T, p=p, c0=c0, n=n, base=base: e.tensor_copy(T[0:32, c0:c0 + n], p[base:base + 32, 0:n]), tok, *old)
                cpy = dve.do(lambda e, T=T, p=p, c0=c0, n=n, base=base: e.tensor_copy(
                    T[32:36, c0:c0 + n], p[base + 32:base + 36, n - 1::-1] if n == S else p[base + 32:base + 36, C - 1::-1]))
        banks.give(ix, cpy)
        banks.give(ic, cpy)
        ib, fb = PAR[0:36, PCOLS["ib"]:PCOLS["ib"] + 1], PAR[0:36, PCOLS["fb"]:PCOLS["fb"] + 1]
        dve.do(lambda e: e.tensor_scalar(T0, T0, ib, None, ALU.add), cpy)
        d1 = dve.do(lambda e: e.tensor_scalar(T1, T1, fb, None, ALU.add), cpy)
        d0 = dve.do(lambda e: e.memset(T3, 1.0))
        a1 = act.do(lambda e: e.activation(T2, T1, ACT.Abs), d1)
        a2 = act.do(lambda e: e.activation(T2, T2, ACT.Exp, scale=-1.0), a1)
        a3 = act.do(lambda e: e.activation(T2, T2, ACT.Ln, bias=1.0), a2)
        d2 = dve.do(lambda e: e.scalar_tensor_tensor(out=T1, in0=T1, scalar=0.0, in1=T2, op0=ALU.min, op1=ALU.subtract), a3)
        d3 = dve.do(lambda e: e.tensor_tensor_scan(T2, T3, T1, 0.0, ALU.mult, ALU.add), d2, d0)
        d4 = dve.do(lambda e: e.tensor_tensor(T0, T0, T2, ALU.subtract), d3)
        d5 = dve.do(lambda e: e.tensor_tensor_scan(T1, T3, T0, 0.0, ALU.mult, ALU.max), d4)
        d6 = dve.do(lambda e: e.tensor_tensor(T2, T2, T1, ALU.add), d5)
        dve.do(lambda e: e.tensor_copy(T3[0:32, :], T0[0:32, :]), d6)
        dve.do(lambda e: e.tensor_copy(T3[32:36, 0:256], T0[32:36, 255::-1]))
        d7 = dve.do(lambda e: e.tensor_copy(T3[32:36, 256:768], T0[32:36, 767:255:-1]))
        dve.do(lambda e: e.tensor_copy(T0[0:32, 256:768], T1[0:32, 256:768]), d7)
        d8 = dve.do(lambda e: e.tensor_copy(T0[32:36, 256:768], T1[32:36, 767:255:-1]), d7)
        dve.do(lambda e: e.tensor_copy(T1[0:32, 256:768], T2[0:32, 256:768]), d8)
        d9 = dve.do(lambda e: e.tensor_copy(T1[32:36, 256:768], T2[32:36, 767:255:-1]), d8)

        so_ok = []
        for h in range(NH):
            i, p = take_bank()
            tok = lin(8, lambda k: ("w_in2", 0, k * 128, 1024 + h * 128), hx(), S, p[:, :])
            ok = act.do(lambda e, p=p, h=h: e.activation(Z[:, h, :], p[:, :], ACT.Sigmoid), tok, x_tok)
            banks.give(i, ok)
            so_ok.append(ok)

        pe.wait(*stat["free"], d7, con_ok)
        for c in range(6):
            fn = lambda e, c=c: e.transpose(STAT[:, c * 36:c * 36 + 36], T3[:, c * 128:c * 128 + 128], IDN[0:36, 0:36])
            if c < 5:
                pe.quiet(fn)
            else:
                tok = pe.do(fn)
        gc_ok = dve.do(lambda e: e.tensor_copy(GC[:, :, :].rearrange("p a b -> p (a b)"), STAT[:, 0:216]), tok, *old)
        stat["free"] = (gc_ok,)

        st.close()
        bs = [take_bank() for _ in range(4)]
        for k in range(8):
            wh, wl = st.block([("w_in2", 0, k * 128, 1552 + q * 128) for q in range(4)])
            for c in range(4):
                tok = mm3(bs[c][1][:, :], HH[:, k, c * 128:c * 128 + 128], HL[:, k, c * 128:c * 128 + 128], wh, wl, k == 0, k == 7)
            st.done(tok)
        h_read = tok
        pu_ok = []
        for c in range(4):
            i, p = bs[c]
            ok = split(p[:, :], *slot(14 + c), tok, hc_read)
            banks.give(i, ok)
            pu_ok.append(ok)
        mod_step()
        st.close()
        d_free = [g_free, g_free]
        mix_ok = {}
        pend = []

        def pool_out(g, ok):
            i, p = take_bank()
            wh, wl = st.block([("pool_w", g, 0, 0)])
            tok = mm3(p[:, :], wh, wl, *slot(12 + g % 2), True, True, ok)
            st.done(tok)
            d_free[g % 2] = (tok,)
            mix_ok[4 + g] = split(p[:, :], HH[:, 4 + g, :], HL[:, 4 + g, :], tok, h_read, scale=par("ps", g))
            banks.give(i, mix_ok[4 + g])

        pe.wait(*pu_ok)
        for g in range(4):
            i, p = take_bank()
            for t in range(4):
                ph, pl = st.block([("poolm", g, t * 128, q * 128) for q in range(4)])
                tok = mm3(p[:, :], GH[:, 14 + t, g * 128:g * 128 + 128], GL[:, 14 + t, g * 128:g * 128 + 128], ph, pl, t == 0, t == 3)
                st.done(tok)
            pu_read = tok
            ok = split(p[:, :], *slot(12 + g % 2), tok, *d_free[g % 2])
            banks.give(i, ok)
            if pend:
                pool_out(*pend.pop())
            pend.append((g, ok))
            mod_step()
        pool_out(*pend.pop())
        st.close()

        q_free = d_free[0] + d_free[1]
        e_free = [(pu_read,)] * 4
        pe.wait(*u_ok, *v_ok)
        scale = 128.0 ** -0.5
        acc_free = [tuple(banks.last[i]) for i in range(4)]
        s_free = [tuple(banks.last[4]), tuple(banks.last[5])]
        pe.wait(sel_ok, d9)
        NUM, DEN = (PS[0], PS[1]), (PS[2], PS[3])
        cnt = {"s": 0, "e": 0, "q_free": q_free}
        mb_ok, mb_free, d_items, s_items, e_items = {}, {}, {}, {}, {}

        def span(c, d):
            j = c - 2
            return (0, S) if c < 2 else ((128 * j, S) if d == 0 else (0, 128 * (j + 1)))

        def kslot(h, c):
            a = h * 768 + c * 128
            return (UH[:, a:a + 128], UL[:, a:a + 128]) if c < 2 else \
                (GH[:, 13, (c - 2) * 128:(c - 1) * 128], GL[:, 13, (c - 2) * 128:(c - 1) * 128])

        def spread(row, d, h):
            pe.wait(*stat["free"])
            return pe.do(lambda e: e.matmul(STAT[:, :], SEL[:, d * 4 + h, :], row[:, 256:768], start=True, stop=True))

        def running_max(h):
            for d in range(2):
                tok = spread(T0, d, h)
                dst = Z[:, 4 + 2 * (h % 2) + d, :]
                mb_ok[h, d] = act.do(lambda e, dst=dst: e.activation(dst, STAT[:, :], ACT.Copy), tok, x_tok, *mb_free.get((h - 2, d), ()))
                stat["free"] = (mb_ok[h, d],)

        def q_and_k(h):
            a0 = h * 768
            st.close() if h == 0 else None
            wq = st.block([("w_q", h, 0, 0)])
            wk = st.block([("w_k", h, 0, 0)])
            for which, w, cols, dst in ((0, wq, slice(a0 + 256, a0 + 768), slot(12)),
                                        (1, wk, slice(a0 + 256, a0 + 768), slot(13)),
                                        (2, wk, slice(a0, a0 + 256), (UH[:, a0:a0 + 256], UL[:, a0:a0 + 256]))):
                b = cnt["s"] % 2
                cnt["s"] += 1
                n = cols.stop - cols.start
                P = PS[4 + b]
                tok = mm3(P[:, 0:n], w[0], w[1], UH[:, cols], UL[:, cols], True, True, *s_free[b])
                ok = split(P[:, 0:n], *dst, tok, *cnt["q_free"], scale=None if which == 0 else scale)
                s_free[b] = (ok,)
            st.done(tok)
            pe.wait(ok)

        def scores(h, c):
            b = cnt["s"] % 2
            cnt["s"] += 1
            tok = mm3(PS[4 + b][:, :], *kslot(h, c), *slot(12), True, True, *s_free[b])
            cnt["q_free"] = (tok,)
            s_items[h, c] = (b, tok)

        def weights(h, c):
            for d in range(2):
                lo, hi = span(c, d)
                n = hi - lo
                m, T = take_scr(dve)
                T = T[:, 0:n]
                src = Z[:, 4 + 2 * (h % 2) + d, lo:hi]
                g = GC[:, c, 32 * d + h:32 * d + h + 1]
                g1 = dve.do(lambda e, T=T, src=src, g=g: e.tensor_scalar(T, src, g, 0.0, ALU.subtract, ALU.max), mb_ok[h, d], gc_ok)
                mb_free[h, d] = (g1,)
                g2 = act.do(lambda e, T=T: e.activation(T, T, ACT.Exp, scale=-1.0), g1)
                if c >= 2:
                    dd = slice(0, 128) if d == 0 else slice(n - 128, n)
                    g2 = pool.do(lambda e, T=T, dd=dd, d=d: e.tensor_tensor(T[:, dd], T[:, dd], TRI[:, d, :], ALU.mult), g2, sel_ok)
                d_items[h, c, d] = (m, T, g2)

        def weigh(h, c):
            b, stok = s_items[h, c]
            mid = []
            for d in range(2):
                lo, hi = span(c, d)
                m, T, g2 = d_items[h, c, d]
                P = PS[4 + b]
                g3 = dve.do(lambda e, T=T, P=P, lo=lo, hi=hi: e.tensor_tensor(T, P[:, lo:hi], T, ALU.mult), g2, stok)
                mid.append(g3)
            s_free[b] = (g3,)
            for d in range(2):
                lo, hi = span(c, d)
                m, T, _ = d_items[h, c, d]
                es = cnt["e"] % 4
                cnt["e"] += 1
                eh, el = GH[:, 14 + es, 0:hi - lo], GL[:, 14 + es, 0:hi - lo]
                g4 = act.do(lambda e, T=T, eh=eh: e.activation(eh, T, ACT.Copy), mid[d], *e_free[es])
                g5 = pool.do(lambda e, T=T, eh=eh, el=el: e.tensor_tensor(el, T, eh.bitcast(F32), ALU.subtract), g4, *e_free[es])
                scr.give(m, g5)
                e_items[h, c, d] = (es, eh, el, g5)

        def sums(h, c):
            if c == 0:
                for i in range(4):
                    pe.wait(*acc_free[i])
            for d in range(2):
                lo, hi = span(c, d)
                es, eh, el, g5 = e_items[h, c, d]
                va = (GH[:, 6 + c, h * 128:h * 128 + 128], GL[:, 6 + c, h * 128:h * 128 + 128])
                mm3(NUM[d][:, lo:hi], *va, eh, el, c == 0, c == 5, g5)
                pe.quiet(lambda e, o=DEN[d][:, lo:hi], eh=eh: e.matmul(o, ONR[:, :], eh, start=(c == 0), stop=False))
                tok = pe.do(lambda e, o=DEN[d][:, lo:hi], el=el: e.matmul(o, ONR[:, :], el, start=False, stop=(c == 5)))
                e_free[es] = (tok,)
            cnt["sums"] = tok

        def normalize(h):
            tok = cnt["sums"]
            hs = []
            for d in range(2):
                mf, Fl = take_scr(act)
                em = act.do(lambda e, Fl=Fl: e.activation(Fl, STAT[:, :], ACT.Exp, scale=-1.0), spread(T1, d, h))
                stat["free"] = (em,)
                m, T = take_scr(act)
                a = act.do(lambda e, T=T, d=d: e.activation(T, DEN[d][:, :], ACT.Abs), tok)
                acc_free[2 + d] = (a,)
                x1 = dve.do(lambda e, T=T, Fl=Fl: e.tensor_tensor(T, T, Fl, ALU.max), a)
                scr.give(mf, x1)
                x2 = dve.do(lambda e, T=T: e.reciprocal(T, T), x1)
                x3 = dve.do(lambda e, T=T, d=d: e.tensor_tensor(T, NUM[d][:, :], T, ALU.mult), x2)
                acc_free[d] = (x3,)
                hs.append((m, T, x3))
            (m0, A, _), (m1, B, kb) = hs
            hh = dve.do(lambda e: e.tensor_tensor(A, A, B, ALU.add), kb)
            scr.give(m1, hh)
            return m0, A, hh

        def head_norm(h, m0, A, hh):
            add_ssq(A, S, True, hh)
            r = rms(S, 2)
            y1 = dve.do(lambda e: e.scalar_tensor_tensor(out=A, in0=A, scalar=par("hn", h), in1=STAT[:, :], op0=ALU.mult, op1=ALU.mult), r, ssq["ok"])
            stat["free"] = (y1,)
            y2 = dve.do(lambda e: e.tensor_tensor(A, A, Z[:, h, :], ALU.mult), y1, so_ok[h])
            mix_ok[h] = split(A, HH[:, h, :], HL[:, h, :], y2, h_read)
            scr.give(m0, mix_ok[h])
            return y2

        steps = [(h, c) for h in range(NH) for c in range(6)]
        running_max(0)
        q_and_k(0)
        weights(0, 0)
        scores(0, 0)
        for i, (h, c) in enumerate(steps):
            if c == 5:
                weigh(h, c)
                sums(*steps[i - 1])
            if i + 1 < len(steps):
                if c == 5:
                    q_and_k(h + 1)
                elif c == 3 and h + 1 < NH:
                    running_max(h + 1)
                scores(*steps[i + 1])
                weights(*steps[i + 1])
            if c < 5:
                weigh(h, c)
            if i and c < 5:
                sums(*steps[i - 1])
                if c == 0:
                    y2 = head_norm(h - 1, *normalize(h - 1))
        sums(*steps[-1])
        y2 = head_norm(NH - 1, *normalize(NH - 1))
        tok = cnt["sums"]
        q_read = cnt["q_free"][0]
        for i in range(4):
            banks.last[i] = acc_free[i]
        banks.last[4], banks.last[5] = s_free
        z_free = (y2,)
        state["g_free"] = (tok, q_read)
        for nn in range(8):
            i, p = take_bank()
            tok = lin(8, lambda k, nn=nn: ("w_out2", 0, k * 128, nn * 128), hx(), S, p[:, :], [mix_ok[q] for q in range(8)])
            ev = act.do(lambda e, nn=nn, p=p: e.activation(Z[:, nn, :], p[:, :], ACT.Copy), tok, *z_free)
            add_ssq(Z[:, nn, :], S, nn == 0, ev)
            banks.give(i, ssq["ok"])
        state["h_free"] = (tok,)
        x_tok = ada_out(1, 0, 1.0, zx, xx, S, ev, x_tok)
        h_ok = ada_norm(2, 0, xx, lambda t: (HH[:, t, :], HL[:, t, :]), S, x_tok, *state["h_free"])
        z_ok = swiglu(1, S, zx, h_ok, x_tok)
        x_tok = ada_out(2, 0, 0.5, zx, xx, S, z_ok, x_tok, more=False)
        sp.wait(x_tok)
        for t in range(DT):
            sp.ops.append(lambda e, t=t: e.dma_start(out[t], X[:, t, :]).then_inc(s_out, 16))
        sp.wait((s_out, 16 * DT))

        if dry:
            return
        block = ctx.enter_context(nc.Block())

        @block.sync
        def _(e):
            sp.run(e)

        @block.tensor
        def _(e):
            pe.run(e)

        @block.scalar
        def _(e):
            act.run(e)

        @block.vector
        def _(e):
            dve.run(e)

        @block.gpsimd
        def _(e):
            pool.run(e)


def constants():
    c = np.zeros((128, 5248), np.float32)
    c[:, 0:128] = np.eye(128)
    i = np.arange(128)
    ang = 2 * np.pi * ((i[:, None] * i[None, :]) % 128) / 128
    c[:, 128:256] = np.cos(ang) / 256
    c[:, 256:384] = np.sin(ang) / 256
    inv = np.float32(10000.0) ** (-np.arange(128, dtype=np.float32) / np.float32(128))
    ang = (np.arange(512, dtype=np.float32)[None, :] * inv.astype(np.float32)[:, None]).astype(np.float64)
    c[:, 384:896] = np.cos(ang)
    c[:, 896:1408] = np.sin(ang)
    d = np.arange(896)[None, :] - 384 - np.arange(128)[:, None]
    for h in range(4):
        gf = 1 - 2.0 ** -(5.0 + h)
        gb = 1 - 2.0 ** -(5.5 + h)
        c[:, 1408 + h * 896:1408 + (h + 1) * 896] = np.where(d >= 0, gf ** np.abs(d), gb ** np.abs(d)) / 16
    c[:, 4992:5120] = i[:, None] <= i[None, :]
    c[:, 5120:5248] = i[:, None] >= i[None, :]
    sel = np.zeros((GATE_ROWS, 8, 128), np.float32)
    for d2 in range(2):
        for h in range(4):
            sel[32 * d2 + h, d2 * 4 + h] = 1
    j = np.arange(512)
    ph = 2 * np.pi * ((j[:256, None] * j[None, :]) % 512) / 512
    dft = np.zeros((512, 512))
    dft[:256] = np.cos(ph)
    dft[256:] = -np.sin(ph)
    dft[256] = np.where(j % 2 == 0, 1, -1)
    poolm = np.zeros((4, 512, 512))
    for g, win in enumerate((2, 4, 8, 16)):
        def mean(n):
            m = np.zeros((n, n))
            lo, hi = win // 2, win - 1 - win // 2
            for t in range(n):
                a, b = max(t - lo, 0), min(t + hi, n - 1)
                m[t, a:b + 1] = 1.0 / (b - a + 1)
            return m
        poolm[g] = (np.kron(mean(8), mean(64)) - np.eye(512)).T
    return c, sel.reshape(GATE_ROWS, 1024), dft.astype(np.float32), poolm.astype(np.float32)


def kernel(x, c, norm1_g, norm2_g, ada_w, ada_b, w_in, w_fourier, w_ret, w_out, ffn_up, conv_w, conv_b,
           ffn_down, final_g, c_2, ctx_2, c_ctx_2, w_mod_2, b_mod_2, norm_pre_2, norm_post_2,
           ffn_w_in_2, ffn_w_out_2, w_in_2, w_out_2, conv_w_2, conv_b_2, w_q_2, w_k_2, i_bias_2,
           f_bias_2, head_norm_2, pool_w_2, pool_scale_2):
    import concourse.bacc as bacc
    from concourse.bass_utils import run_bass_kernel_spmd

    A = lambda a: np.ascontiguousarray(a)
    consts, sel, dft, poolm = constants()
    gate = np.zeros((1024, 128), np.float32)
    w2 = A(w_in_2)[0]
    for q in range(4):
        gate[:, 32 * q:32 * q + 4] = w2[:, 1536 + 4 * q:1540 + 4 * q]
    P = np.zeros((128, NP), np.float32)

    def put(name, a, at=0):
        a = A(a)
        P[:, PCOLS[name] + at:PCOLS[name] + at + a.shape[1]] = a

    cols = lambda a: A(a).reshape(-1, 128).T
    put("c", cols(c))
    put("c2", np.stack([cols(c_2), cols(c_ctx_2)], 2).reshape(128, 16))
    put("n1", cols(norm1_g))
    put("n2", cols(norm2_g))
    put("adab", cols(ada_b))
    put("fing", cols(final_g))
    put("bmod", np.repeat(cols(b_mod_2), 2, axis=1))
    put("npre", cols(norm_pre_2))
    put("npost", cols(norm_post_2))
    put("cw", cols(conv_w))
    put("cb", cols(conv_b))
    put("cw2", cols(conv_w_2))
    put("cb2", cols(conv_b_2))
    put("hn", cols(head_norm_2))
    put("ps", cols(pool_scale_2))
    for d in range(2):
        P[32 * d:32 * d + 4, PCOLS["ib"]] = A(i_bias_2)[0, d]
        P[32 * d:32 * d + 4, PCOLS["fb"]] = A(f_bias_2)[0, d]

    src = {"w_in": A(w_in), "w_fourier": A(w_fourier), "w_ret": A(w_ret), "w_out": A(w_out), "ffn_up": A(ffn_up),
           "ffn_down": A(ffn_down), "ada_w": A(ada_w), "w_mod": A(w_mod_2), "ffn_w_in": A(ffn_w_in_2)[0],
           "ffn_w_out": A(ffn_w_out_2)[0], "w_in2": A(w_in_2), "w_out2": A(w_out_2), "w_q": A(w_q_2)[0],
           "w_k": A(w_k_2)[0], "pool_w": A(pool_w_2)[0], "gate": gate[None], "dft": dft[None], "poolm": poolm}

    mods = [("ada_w", l, v) for l in range(2) for v in range(6)] + [("w_mod", 0, v) for v in range(9)]

    def build(chunks, dry):
        nc = bacc.Bacc("TRN2", target_bir_lowering=False, num_devices=1, dynamic_dma_scratch_size=1024)
        n = max(len(chunks), 1)
        ins = {"ws": (n, 128, 1024), "wm": (len(mods) * 8, 128, 1024), "xT": (8, 128, S), "cT": (8, 128, C), "params": (128, NP),
               "consts": consts.shape, "sel": sel.shape}
        t = {k: nc.dram_tensor(k, v, F32, kind="ExternalInput").ap() for k, v in ins.items()}
        out = nc.dram_tensor("out", (8, 128, S), F32, kind="ExternalOutput").ap()
        program(nc, t["ws"], t["wm"], t["xT"], t["cT"], t["params"], t["consts"], t["sel"], out, chunks, dry)
        return nc

    chunks = []
    build(chunks, True)
    nc = build(chunks, False)
    ws = np.zeros((len(chunks), 128, 1024), np.float32)
    for i, specs in enumerate(chunks):
        for b, (name, l, r, q) in enumerate(specs):
            ws[i, :, b * 128:b * 128 + 128] = src[name][l, r:r + 128, q:q + 128]
    wm = np.empty((len(mods), 2, 4, 128, 2, 512), np.float32)
    for i, (name, l, v) in enumerate(mods):
        w = src[name][l, :, v * 1024:(v + 1) * 1024].reshape(4, 2, 128, 2, 512)
        wm[i] = w.transpose(3, 0, 2, 1, 4)
    wm = wm.reshape(len(mods) * 8, 128, 1024)
    arrays = {"ws": ws, "wm": wm, "xT": A(A(x)[0].T).reshape(8, 128, S), "cT": A(A(ctx_2)[0].T).reshape(8, 128, C),
              "params": P, "consts": consts, "sel": sel}
    r = run_bass_kernel_spmd(nc, [arrays], core_ids=[0])
    o = r.results[0]["out"]
    return A(o.reshape(D, S).T).reshape(1, S, D)
```

```python
from contextlib import ExitStack

import numpy as np

import concourse.bass as bass
from concourse import mybir

F32 = mybir.dt.float32
F32R = mybir.dt.float32r
ALU = mybir.AluOpType
ACT = mybir.ActivationFunctionType

S = 512
C = 256
D = 1024
DT = 8
FF = 2816
NH = 4
EPS = 1e-6
GATE_ROWS = 36
NS = 4
NW = 3
AHEAD = 2
NSLOT = 18


class Queue:

    def __init__(self, sem):
        self.sem = sem
        self.count = 0
        self.ops = []
        self.seen = {}

    def wait(self, *tokens):
        for token in tokens:
            if token is None:
                continue
            sem, value = token
            if self.seen.get(id(sem), 0) < value:
                self.seen[id(sem)] = value
                self.ops.append(lambda e, s=sem, v=value: e.wait_ge(s, v))

    def do(self, fn, *waits):
        self.wait(*waits)
        self.count += 1
        self.ops.append(lambda e, f=fn, s=self.sem: f(e).then_inc(s, 1))
        return (self.sem, self.count)

    def quiet(self, fn, *waits):
        self.wait(*waits)
        self.ops.append(fn)

    def run(self, e):
        for op in self.ops:
            op(e)


PCOLS = {}
_at = 0
for _name, _n in [("c", 8), ("c2", 16), ("n1", 16), ("n2", 16), ("adab", 96), ("fing", 8), ("bmod", 144),
                  ("npre", 24), ("npost", 24), ("cw", 264), ("cb", 88), ("cw2", 12), ("cb2", 4),
                  ("hn", 4), ("ps", 4), ("ib", 1), ("fb", 1)]:
    PCOLS[_name] = _at
    _at += _n
NP = _at


def program(nc, ws, wm, xT, cT, params, consts, sel_d, out, chunks, dry):
    nch = len(chunks)
    ctx = ExitStack()
    with ctx:
        def sem(name):
            return ctx.enter_context(nc.semaphore(name))

        def sb(name, shape, dt=F32, stack=None):
            return (stack or ctx).enter_context(nc.sbuf_tensor(name, shape, dt))

        pe, act, dve, pool, sp = (Queue(sem(f"s_{n}")) for n in ("pe", "act", "dve", "pool", "sp"))
        s_ws = [sem(f"s_ws{i}") for i in range(NS)]
        s_par, s_con, s_x, s_rope, s_out = (sem(n) for n in ("s_par", "s_con", "s_x", "s_rope", "s_out"))
        s_mk = sem("s_mk")

        stage = sb("stage", [128, NS, 1024])
        WH = sb("WH", [128, NW, 1024], F32R)
        WL = sb("WL", [128, NW, 1024], F32R)
        HH = sb("HH", [128, DT, S], F32R)
        HL = sb("HL", [128, DT, S], F32R)
        GH = sb("GH", [128, NSLOT, S], F32R)
        GL = sb("GL", [128, NSLOT, S], F32R)
        GHf = GH[:, :, :].rearrange("p a b -> p (a b)")
        GLf = GL[:, :, :].rearrange("p a b -> p (a b)")
        X = sb("X", [128, DT, S])
        Z = sb("Z", [128, DT, S])
        SCR = sb("SCR", [128, 6, S])
        SSQ = sb("SSQ", [128, S])
        DG = sb("DG", [128, S])
        PAR = sb("PAR", [128, NP])
        MOD = sb("MOD", [128, 2, 48])
        MOD2 = sb("MOD2", [128, 72, 2])
        CS = sb("CS", [128, 8])
        CS2 = sb("CS2", [128, 8, 2])
        AB = sb("AB", [128, 8])
        V4 = sb("V4", [128, 8])
        HM = sb("HM", [128, 4])
        OC = sb("OC", [128, 3])
        IDN = sb("IDN", [128, 128])
        ONE = sb("ONE", [128, 128])
        VM = sb("VM", [128, 8])
        ONR = sb("ONR", [128, 128], F32R)
        RC = sb("RC", [128, 8])
        TAB = sb("TAB", [128, 2176])
        MASK = TAB[:, 0:896]
        ROPE = [TAB[:, 896:1408], TAB[:, 1408:1920]]
        DFTF = TAB[:, 1920:2176]
        SEL = TAB[0:GATE_ROWS, 0:1024]
        TRI = [TAB[:, 1024:1152], TAB[:, 1152:1280]]
        st1 = ctx.enter_context(ExitStack())
        ACC = sb("ACC", [128, 2, 512], stack=st1)
        MST = sb("MST", [128, 2, 1024], stack=st1)

        PS = [ctx.enter_context(nc.psum_tensor(f"ps{i}", [128, S], F32)) for i in range(8)]
        STAT, MODP = PS[6], PS[7]

        def par(name, i, n=1):
            return PAR[:, PCOLS[name] + i:PCOLS[name] + i + n]

        class Ring:

            def __init__(self, n):
                self.idle = list(range(n))
                self.last = [()] * n

            def take(self):
                i = self.idle.pop(0)
                return i, self.last[i]

            def give(self, i, *tokens):
                assert i not in self.idle
                self.last[i] = tokens
                self.idle.append(i)

        banks = Ring(6)
        scr = Ring(6)

        class Stream:
            def __init__(self):
                self.n = -1
                self.used = 8
                self.loaded = 0
                self.ready = {}
                self.slot_free = [()] * NW
                self.stage_free = {}
                self.next = 0

            def open(self):
                if not dry:
                    for i in range(min(NS, nch)):
                        self.load(i, ())

            def load(self, i, free):
                sp.wait(*free)
                sp.ops.append(lambda e, i=i: e.dma_start(stage[:, i % NS, :], ws[i]).then_inc(s_ws[i % NS], 16))
                self.loaded = i + 1

            def landed(self, i):
                return (s_ws[i % NS], 16 * (i // NS + 1))

            def freed(self, i, *tokens):
                self.stage_free[i] = tokens
                while self.loaded < nch and self.loaded - NS in self.stage_free:
                    self.load(self.loaded, self.stage_free.pop(self.loaded - NS))

            def prepare(self, upto):
                while self.next <= min(upto, nch - 1):
                    i = self.next
                    slot = i % NW
                    if self.slot_free[slot] is None:
                        assert i > self.n
                        break
                    self.next += 1
                    src = stage[:, i % NS, :]
                    free = self.slot_free[slot]
                    self.slot_free[slot] = None
                    hi = act.do(lambda e, o=WH[:, slot, :], s=src: e.activation(o, s, ACT.Copy),
                                self.landed(i), *free)
                    lo = dve.do(lambda e, o=WL[:, slot, :], s=src, h=WH[:, slot, :].bitcast(F32):
                                e.tensor_tensor(o, s, h, ALU.subtract), self.landed(i), hi, *free)
                    self.ready[i] = lo
                    self.freed(i, lo)

            def start(self):
                self.n += 1
                self.used = 0
                if dry:
                    chunks.append([])
                else:
                    self.prepare(self.n + AHEAD)
                    pe.wait(self.ready[self.n])

            def block(self, specs):
                if self.used + len(specs) > 8:
                    self.start()
                    self.cur = self.n
                if dry:
                    chunks[self.cur].extend(specs)
                a = self.used * 128
                self.used += len(specs)
                b = self.used * 128
                if dry:
                    return WH[:, 0, a:b], WL[:, 0, a:b]
                slot = self.cur % NW
                return WH[:, slot, a:b], WL[:, slot, a:b]

            def done(self, token):
                if not dry:
                    self.slot_free[self.cur % NW] = (token,)

            def close(self):
                self.used = 8

        st = Stream()

        def mm3(o, wh, wl, mh, ml, start, stop, *waits):
            pe.quiet(lambda e: e.matmul(o, wh, mh, start=start, stop=False), *waits)
            pe.quiet(lambda e: e.matmul(o, wh, ml, start=False, stop=False))
            return pe.do(lambda e: e.matmul(o, wl, mh, start=False, stop=stop))

        mod_tok = {}
        mod_jobs = [("ada", 0, v) for v in range(6)] + [("ada", 1, v) for v in range(6)] \
            + [("mod", 0, v) for v in range(9)]
        mod_state = {"free": (), "acc_free": (), "due": None}

        def mod_sum():
            which, l, v, half, tok = mod_state["due"]
            mod_state["due"] = None
            nv = 1 if which == "ada" else 2
            if half == 0:
                pe.wait(*mod_state["free"])
            for t in range(4):
                for d in range(nv):
                    o = MODP[:, (half * 4 + t) * nv + d:(half * 4 + t) * nv + d + 1]
                    fn = lambda e, o=o, t=t, d=d: e.matmul(o, ACC[:, d, t * 128:t * 128 + 128], ONE[:, 0:1],
                                                           start=True, stop=True)
                    if t < 3 or d < nv - 1:
                        pe.quiet(fn, tok)
                    else:
                        done = pe.do(fn, tok)
            mod_state["acc_free"] = (done,)
            if half == 1:
                if which == "ada":
                    ev = dve.do(lambda e: e.tensor_tensor(MOD[:, l, v * 8:v * 8 + 8], MODP[:, 0:8],
                                                          par("adab", l * 48 + v * 8, 8), ALU.add), done)
                else:
                    ev = dve.do(lambda e: e.tensor_tensor(
                        MOD2[:, v * 8:v * 8 + 8, :].rearrange("p a b -> p (a b)"), MODP[:, 0:16],
                        par("bmod", v * 16, 16), ALU.add), done)
                mod_state["free"] = (ev,)
                mod_tok[(which, l, v)] = ev

        mod_list = [(name, l, v, half, q) for name, l, v in mod_jobs for half in range(2) for q in range(4)]
        mod_at = {"n": 0, "kk": 0, "loaded": 0, "user": {}, "acc": [None, None]}
        mod_sem = [sem(f"s_md{i}") for i in range(6)]
        mod_uses = [0] * 6
        mod_slot = {}

        def mod_buffer(b):
            return MST[:, b, :] if b < 2 else Z[:, 2 * (b - 2):2 * (b - 1), :].rearrange("p a b -> p (a b)")

        def mod_load(q):
            m = mod_at["loaded"]
            if m >= len(mod_list):
                return
            mod_at["loaded"] += 1
            b = m % 6 if m < 16 else m % 2
            mod_uses[b] += 1
            mod_slot[m] = (b, (mod_sem[b], 16 * mod_uses[b]))
            q.wait(mod_at["user"].get(b))
            q.ops.append(lambda e, b=b, m=m: e.dma_start(mod_buffer(b), wm[m]).then_inc(mod_sem[b], 16))

        def mod_step():
            for _ in range(2 if mod_at["kk"] == 0 else 1):
                mod_half_step()

        def mod_half_step():
            if mod_state["due"]:
                mod_sum()
            m, kk = mod_at["n"], mod_at["kk"]
            if m >= len(mod_list):
                return
            if kk == 0 and m >= 16 and mod_at["loaded"] <= m + 1:
                mod_load(act)
            which, l, v, half, q = mod_list[m]
            b, landed = mod_slot[m]
            w = mod_buffer(b)
            k = 2 * q + kk
            src = w[:, kk * 512:kk * 512 + 512]
            for d in range(1 if which == "ada" else 2):
                c = CS[:, k:k + 1] if which == "ada" else CS2[:, k, d:d + 1]
                if k == 0:
                    tok = dve.do(lambda e, src=src, c=c, d=d: e.tensor_scalar(ACC[:, d, :], src, c, None, ALU.mult),
                                 landed, cs_tok, *mod_state["acc_free"])
                else:
                    tok = dve.do(lambda e, src=src, c=c, d=d: e.scalar_tensor_tensor(
                        out=ACC[:, d, :], in0=src, scalar=c, in1=ACC[:, d, :], op0=ALU.mult, op1=ALU.add),
                        landed, mod_at["acc"][d])
                mod_at["acc"][d] = tok
            mod_at["kk"] = 1 - kk
            if kk == 0:
                return
            mod_at["n"] += 1
            mod_at["user"][b] = tok
            if mod_at["loaded"] < 16:
                mod_load(sp)
            elif m == 14:
                mod_load(act)
            if q == 3:
                mod_state["due"] = (which, l, v, half, tok)

        def need(*job):
            while job not in mod_tok:
                mod_step()
            return mod_tok[job]

        sp.ops.append(lambda e: e.dma_start(PAR[:, :], params).then_inc(s_par, 16))
        for _ in range(6):
            mod_load(sp)
        sp.ops.append(lambda e: e.dma_start(IDN[:, :], consts[:, 0:128]).then_inc(s_con, 16))
        for t in range(DT):
            act.ops.append(lambda e, t=t: e.dma_start(X[:, t, :], xT[t]).then_inc(s_x, 16))
        par_ok, con_ok, x_ok = (s_par, 16), (s_con, 16), (s_x, 16 * DT)
        dve.do(lambda e: e.memset(ONE[:, :], 1.0))
        dve.do(lambda e: e.memset(OC[:, 0:1], 1.0 / 1024))
        dve.do(lambda e: e.memset(OC[:, 1:2], 1.0 / 256))
        dve.do(lambda e: e.memset(OC[:, 2:3], 1.0 / 128))
        dve.do(lambda e: e.memset(HM[:, :], -0.5))
        one_ok = dve.do(lambda e: e.memset(ONR[:, :].bitcast(F32), 1.0))
        cs1 = act.do(lambda e: e.activation(CS[:, :], par("c", 0, 8), ACT.Silu), par_ok)
        cs_tok = act.do(lambda e: e.activation(CS2[:, :, :].rearrange("p a b -> p (a b)"), par("c2", 0, 16), ACT.Silu))
        dve.wait(par_ok)
        pe.wait(one_ok)
        while mod_at["n"] < 10:
            mod_step()

        stat = {"free": ()}
        ssq = {"free": (), "ok": None}

        def take_scr(*qs):
            i, free = scr.take()
            for q in qs:
                q.wait(*free)
            return i, SCR[:, i, :]

        def take_bank():
            i, free = banks.take()
            pe.wait(*free)
            return i, PS[i]

        def split(src, hi, lo, *waits, bias=None, scale=None):
            if bias is None and scale is None:
                a = act.do(lambda e: e.activation(hi, src, ACT.Copy), *waits)
                return dve.do(lambda e: e.tensor_tensor(lo, src, hi.bitcast(F32), ALU.subtract), a, *waits)
            if scale is not None:
                a = act.do(lambda e: e.activation(hi, src, ACT.Copy, scale=scale), *waits)
                return dve.do(lambda e: e.scalar_tensor_tensor(out=lo, in0=src, scalar=scale, in1=hi.bitcast(F32),
                                                               op0=ALU.mult, op1=ALU.subtract), a, *waits)
            a = act.do(lambda e: e.activation(hi, src, ACT.Identity, bias=bias), *waits)
            return dve.do(lambda e: e.scalar_tensor_tensor(out=lo, in0=src, scalar=bias, in1=hi.bitcast(F32),
                                                           op0=ALU.add, op1=ALU.subtract), a, *waits)

        def add_ssq(src, n, first, *waits, q=dve):
            if first:
                ssq["ok"] = act.do(lambda e: e.activation(SSQ[:, 0:n], src, ACT.Square), *waits, *ssq["free"])
                return ssq["ok"]
            i, t = take_scr(act)
            sq = act.do(lambda e: e.activation(t[:, 0:n], src, ACT.Square), *waits)
            ssq["ok"] = q.do(lambda e: e.tensor_tensor(SSQ[:, 0:n], SSQ[:, 0:n], t[:, 0:n], ALU.add), sq, ssq["ok"])
            scr.give(i, ssq["ok"])
            return sq

        def rms_first(n, oc):
            nt = n // 128
            pe.wait(ssq["ok"], *stat["free"])
            for t in range(nt):
                fn = lambda e, t=t: e.matmul(STAT[:, t:t + 1], SSQ[:, t * 128:t * 128 + 128], OC[:, oc:oc + 1],
                                             start=True, stop=True)
                if t < nt - 1:
                    pe.quiet(fn)
                else:
                    summed = pe.do(fn)
            ssq["free"] = (summed,)
            e1 = dve.do(lambda e: e.tensor_scalar(V4[:, 0:nt], STAT[:, 0:nt], EPS, None, ALU.add), summed)
            r4 = pool.do(lambda e: e.tensor_tensor(V4[:, 4:4 + nt], V4[:, 0:nt], HM[:, 0:nt], ALU.pow), e1, one_ok)
            dve.wait(con_ok, *stat.get("dg_free", ()))
            for t in range(nt):
                dg = dve.do(lambda e, t=t: e.tensor_scalar(DG[:, t * 128:t * 128 + 128], IDN[:, :],
                                                           V4[:, 4 + t:5 + t], None, ALU.mult), r4)
            stat["dg"] = dg
            return n

        def rms_last(n):
            for t in range(n // 128):
                tok = pe.do(lambda e, t=t: e.matmul(STAT[:, t * 128:t * 128 + 128], ONE[:, :], DG[:, t * 128:t * 128 + 128],
                                                    start=True, stop=True), stat["dg"])
            stat["dg_free"] = (tok,)
            return tok

        def rms(n, oc):
            return rms_last(rms_first(n, oc))

        def affine_steps(src, dst, a_col, b_col, n, rtok, oks, *waits):
            held = []

            def low(i, tmp, t, hi):
                tok = dve.do(lambda e: e.scalar_tensor_tensor(out=dst(t)[1], in0=tmp, scalar=b_col(t), in1=dst(t)[0].bitcast(F32),
                                                              op0=ALU.add, op1=ALU.subtract), hi)
                scr.give(i, tok)
                oks.append(tok)

            for t in range(DT):
                i, tmp = take_scr(dve)
                tmp = tmp[:, 0:n]
                m = dve.do(lambda e, t=t, tmp=tmp: e.scalar_tensor_tensor(out=tmp, in0=src(t), scalar=a_col(t), in1=STAT[:, 0:n],
                                                                          op0=ALU.mult, op1=ALU.mult), rtok, *waits)
                hi = act.do(lambda e, t=t, tmp=tmp: e.activation(dst(t)[0], tmp, ACT.Identity, bias=b_col(t)), m, *waits)
                if held:
                    low(*held.pop())
                held.append((i, tmp, t, hi))
                if t == DT - 1:
                    stat["free"] = (m,)
                    low(*held.pop())
                yield

        def affine(*args):
            oks = []
            for _ in affine_steps(*args[:6], oks, *args[6:]):
                pass
            return oks

        background = []

        def tick():
            if mod_at["n"] < 48:
                mod_step()
            else:
                mod_half_step()
            if background and next(background[0], background) is background:
                background.pop()

        def drain():
            while background:
                if next(background[0], background) is background:
                    background.pop()

        def lin(nk, spec, mov, n, o, oks=(), bg=True):
            for k in range(nk):
                pe.wait(*oks[k:k + 1])
                wh, wl = st.block([spec(k)])
                mh, ml = mov(k)
                tok = mm3(o, wh, wl, mh, ml, k == 0, k == nk - 1)
                st.done(tok)
            if bg:
                tick()
            return tok

        def lin2(specs, mov, outs, oks):
            st.close()
            for k in range(8):
                pe.wait(oks[k])
                mh, ml = mov(k)
                for spec, o in zip(specs, outs):
                    wh, wl = st.block([spec(k)])
                    tok = mm3(o, wh, wl, mh, ml, k == 0, k == 7)
                    st.done(tok)
            tick()
            return tok

        def slot(i, n=S):
            return GH[:, i, 0:n], GL[:, i, 0:n]

        def hx(n=S):
            return lambda k: (HH[:, k, 0:n], HL[:, k, 0:n])

        CH = sb("CH", [128, 256], F32R, stack=st1)
        CL = sb("CL", [128, 256], F32R, stack=st1)

        state = {"x": x_ok, "h_free": (), "g_free": (), "z_free": (), "mask_n": 0}
        st.open()
        sp.ops.append(lambda e: e.dma_start(DFTF, consts[:, 128:384]).then_inc(s_con, 16))
        sp.ops.append(lambda e: e.dma_start(TAB[:, 896:1920], consts[:, 384:1408]).then_inc(s_rope, 16))
        mask_free = [None]

        def load_mask(h):
            state["mask_n"] += 1
            sp.wait(mask_free[0])
            sp.ops.append(lambda e: e.dma_start(MASK, consts[:, 1408 + h * 896:1408 + (h + 1) * 896]).then_inc(s_mk, 16))
            return (s_mk, 16 * state["mask_n"])

        def token_mix(l):
            need("ada", l, 0)
            mtok = need("ada", l, 1)
            ab = dve.do(lambda e: e.scalar_tensor_tensor(out=AB[:, :], in0=MOD[:, l, 8:16], scalar=1.0, in1=par("n1", l * 8, 8),
                                                         op0=ALU.add, op1=ALU.mult), mtok, *state.get("ab_free", ()))
            rms_first(S, 0)
            if l == 0:
                st.prepare(AHEAD - 1)
            r = rms_last(S)
            h_ok = affine(lambda t: X[:, t, :], lambda t: (HH[:, t, :], HL[:, t, :]), lambda t: AB[:, t:t + 1],
                          lambda t: MOD[:, l, t:t + 1], S, r, ab, state["x"], mtok, *state["h_free"])
            state["ab_free"] = (h_ok[-1],)
            x_ready = state["x"]
            if l == 0:
                state["dft"] = split(DFTF, CH[:, :], CL[:, :], (s_con, 32))
            dft_ok = state["dft"]

            uf = [slice(16 * S, 16 * S + 640)]
            uf_free = [tuple(state["g_free"])]
            zero = []
            for b in range(1):
                for T in (GHf, GLf):
                    z = T[:, uf[b]]
                    dve.do(lambda e, z=z: e.memset(z[:, 512:640].bitcast(F32), 0.0), *uf_free[b])
                    zero.append(dve.do(lambda e, z=z: e.memset(z[:, 256:257].bitcast(F32), 0.0)))
            dfts = []
            pend = []

            def channel_dft(g, b, tok):
                i, p = take_bank()
                pe.wait(tok, zero[-1], dft_ok)
                uh, ul = GHf[:, uf[b]], GLf[:, uf[b]]
                for t in range(4):
                    cc = slice(0, 128) if t < 2 else slice(128, 256)
                    o = p[:, t * 128:t * 128 + 128]
                    tok = mm3(o, uh[:, t * 128:t * 128 + 128], ul[:, t * 128:t * 128 + 128], CH[:, cc], CL[:, cc],
                              True, t != 2)
                    if t == 2:
                        tok = mm3(o, uh[:, 512:640], ul[:, 512:640], CH[:, 0:128], CL[:, 0:128], False, True)
                uf_free[b] = (tok,)
                ev = split(p[:, :], *slot(8 + g), tok, *state["g_free"])
                banks.give(i, ev)
                dfts.append(ev)

            pair = [take_bank(), take_bank()]
            tok2 = lin2([lambda k: ("w_in", l, k * 128, 0), lambda k: ("w_in", l, k * 128, 128)], hx(),
                        [q[1][:, :] for q in pair], h_ok)
            for g in range(8):
                if g < 2:
                    (i, p), tok = pair[g], tok2
                else:
                    i, p = take_bank()
                    tok = lin(8, lambda k, g=g: ("w_in", l, k * 128, g * 128), hx(), S, p[:, :])
                j, U = take_scr(act)
                cp = act.do(lambda e, U=U, p=p: e.activation(U, p[:, :], ACT.Copy), tok)
                banks.give(i, cp)
                b = 0
                m, W = take_scr(dve)
                dve.do(lambda e, U=U, W=W: e.tensor_tensor(W[:, 1:256], U[:, 1:256], U[:, 511:256:-1], ALU.add), cp)
                dve.do(lambda e, U=U, W=W: e.tensor_tensor(W[:, 257:512], U[:, 1:256], U[:, 511:256:-1], ALU.subtract))
                fo = dve.do(lambda e, U=U, W=W: e.tensor_copy(W[:, 0:512:256], U[:, 0:512:256]))
                if pend:
                    channel_dft(*pend.pop())
                uh, ul = GHf[:, uf[b]], GLf[:, uf[b]]

                def halves(dst, src, *w):
                    a = act.do(lambda e: e.activation(dst[0], src, ACT.Copy), *w)
                    return dve.do(lambda e: e.tensor_tensor(dst[1], src, dst[0].bitcast(F32), ALU.subtract), a)

                w = (fo, *uf_free[b], *zero)
                halves((uh[:, 0:256], ul[:, 0:256]), W[:, 0:256], *w)
                halves((uh[:, 257:512], ul[:, 257:512]), W[:, 257:512], *w)
                fd = halves((uh[:, 512:513], ul[:, 512:513]), W[:, 256:257], *w)
                scr.give(j, fo)
                scr.give(m, fd)
                pend.append((g, b, fd))
            st.close()
            gates = {}

            def gate(base, n):
                i, p = take_bank()
                tok = lin(8, lambda k: ("w_in", l, k * 128, (base + n) * 128), hx(), S, p[:, :])
                j, sg = take_scr(act)
                sk = act.do(lambda e: e.activation(sg, p[:, :], ACT.Sigmoid), tok)
                banks.give(i, sk)
                gates[n] = (j, sg, sk)

            channel_dft(*pend.pop())
            gate(40, 0)
            pe.wait(*dfts)
            st.close()
            tabs = []
            for q in range(2):
                a = st.block([("dft", 0, 2 * q * 128, c * 128) for c in range(4)])
                b = st.block([("dft", 0, (2 * q + 1) * 128, c * 128) for c in range(4)])
                tabs += [(a, st.cur), (b, st.cur)]
            f_ok = []
            for g in range(8):
                i, p = take_bank()
                for t in range(4):
                    (th, tl), _ = tabs[t]
                    tok = mm3(p[:, :], GH[:, 8 + g, t * 128:t * 128 + 128], GL[:, 8 + g, t * 128:t * 128 + 128], th, tl,
                              t == 0, t == 3)
                ev = split(p[:, :], *slot(g), tok, *state["g_free"])
                banks.give(i, ev)
                f_ok.append(ev)
            if not dry:
                for (_, cur) in tabs:
                    st.slot_free[cur % NW] = (tok,)
            st.close()
            m1_ok = []
            for n in range(8):
                if n:
                    gate(40, n)
                i, p = take_bank()
                tok = lin(8, lambda k, n=n: ("w_fourier", l, k * 128, n * 128), slot, S, p[:, :], f_ok)
                j, sg, sk = gates[n]
                ev = dve.do(lambda e, n=n, p=p, sg=sg: e.tensor_tensor(Z[:, n, :], p[:, :], sg, ALU.mult), tok, sk, *state["z_free"])
                banks.give(i, ev)
                scr.give(j, ev)
                m1_ok.append(ev)
            fourier_read = tok

            g_free = (fourier_read,)
            qk_free = g_free
            v_free = g_free
            s_free = g_free
            qk_ok, v_ok, s_ok, sg_ok, r_ok = {}, {}, {}, {}, []
            masks = {0: load_mask(0)}
            sg_slot = {}

            def part_a(h):
                nonlocal qk_free
                toks = []
                for w, base in ((0, 8 + 2 * h), (1, 16 + 2 * h)):
                    b = []
                    for t in range(2):
                        i, p = take_bank()
                        tok = lin(8, lambda k, c=base + t: ("w_in", l, k * 128, c * 128), hx(), S, p[:, :])
                        b.append((i, p, tok))
                    (i0, p0, k0), (i1, p1, k1) = b
                    dve.wait((s_rope, 16))
                    for half in range(2):
                        ja, A = take_scr(dve)
                        jb, B = take_scr(dve)
                        ca, cb = (0, 1) if half == 0 else (1, 0)
                        dve.do(lambda e, A=A, p0=p0, ca=ca: e.tensor_tensor(A, p0[:, :], ROPE[ca], ALU.mult), k0)
                        mb = dve.do(lambda e, B=B, p1=p1, cb=cb: e.tensor_tensor(B, p1[:, :], ROPE[cb], ALU.mult), k1)
                        rr = dve.do(lambda e, A=A, B=B, half=half: e.tensor_tensor(A, A, B, ALU.subtract if half == 0 else ALU.add), mb)
                        ok = split(A, *slot(2 * w + half), rr, *qk_free)
                        scr.give(ja, ok)
                        scr.give(jb, rr)
                        toks.append(ok)
                    banks.give(i0, mb)
                    banks.give(i1, mb)
                qk_ok[h] = toks

            def part_b(h, between=None):
                st.close()
                v = [take_bank() for _ in range(4)]
                for k in range(8):
                    wh, wl = st.block([("w_in", l, k * 128, (24 + 2 * h + c) * 128) for c in range(2)])
                    for t in range(4):
                        sl = slice(t * 128, t * 128 + 128)
                        tok = mm3(v[t][1][:, 0:256], HH[:, k, sl], HL[:, k, sl], wh, wl, k == 0, k == 7)
                    st.done(tok)
                    if between and k in (3, 7):
                        between[k // 4]()
                st.close()
                if not dry:
                    st.prepare(st.n + AHEAD)
                toks = []
                for q in range(2):
                    j, junk = take_scr(act)
                    sms = []
                    for t in range(2):
                        sms.append(act.do(lambda e, p=v[2 * q + t][1], t=t, q=q, junk=junk: e.activation(
                            junk[:, t * 256:t * 256 + 256], p[:, 0:256], ACT.Copy,
                            accum_out=VM[:, 2 * q + t:2 * q + t + 1]), tok, *state.get("vm_free", ())))
                    nm = dve.do(lambda e, q=q: e.tensor_scalar(VM[:, 4 + 2 * q:6 + 2 * q], VM[:, 2 * q:2 * q + 2], -1.0 / 256, None, ALU.mult), sms[-1])
                    for t in range(2):
                        sl = slice(t * 256, t * 256 + 256)
                        hi = act.do(lambda e, p=v[2 * q + t][1], q=q, t=t, sl=sl: e.activation(
                            GH[:, 4 + q, sl], p[:, 0:256], ACT.Identity, bias=VM[:, 4 + 2 * q + t:5 + 2 * q + t]), nm, *v_free)
                    for t in range(2):
                        sl = slice(t * 256, t * 256 + 256)
                        ok = dve.do(lambda e, p=v[2 * q + t][1], q=q, t=t, sl=sl: e.scalar_tensor_tensor(
                            out=GL[:, 4 + q, sl], in0=p[:, 0:256], scalar=VM[:, 4 + 2 * q + t:5 + 2 * q + t],
                            in1=GH[:, 4 + q, sl].bitcast(F32), op0=ALU.add, op1=ALU.subtract), hi, *v_free)
                        banks.give(v[2 * q + t][0], ok)
                    scr.give(j, ok)
                    toks.append(ok)
                state["vm_free"] = (ok,)
                v_ok[h] = toks
                mod_step()
                sg_ok[h] = []
                for t in range(2):
                    i, p = take_bank()
                    tok = lin(8, lambda k, t=t: ("w_in", l, k * 128, (32 + 2 * h + t) * 128), hx(), S, p[:, :])
                    j, sg = take_scr(act)
                    sk = act.do(lambda e, p=p, sg=sg: e.activation(sg, p[:, :], ACT.Silu), tok)
                    banks.give(i, sk)
                    sg_ok[h].append((j, sg, sk))

            def part_c(h):
                nonlocal s_free, qk_free
                mtok = masks[h]
                pe.wait(*qk_ok[h])
                s_ok[h] = []
                for jt in range(4):
                    i, p = take_bank()
                    for t in range(2):
                        sl = slice(jt * 128, jt * 128 + 128)
                        tok = mm3(p[:, :], GH[:, 2 + t, sl], GL[:, 2 + t, sl], GH[:, t, :], GL[:, t, :], t == 0, t == 1)
                    j, T = take_scr(dve)
                    m = dve.do(lambda e, T=T, p=p, jt=jt: e.tensor_tensor(
                        T, p[:, :], MASK[:, 384 - 128 * jt:896 - 128 * jt], ALU.mult), tok, mtok)
                    banks.give(i, m)
                    a = act.do(lambda e, T=T, jt=jt: e.activation(GH[:, 6 + jt, :], T, ACT.Copy), m, *s_free)
                    lo = pool.do(lambda e, T=T, jt=jt: e.tensor_tensor(GL[:, 6 + jt, :], T, GH[:, 6 + jt, :].bitcast(F32), ALU.subtract), m, a, *s_free)
                    scr.give(j, lo)
                    s_ok[h].append(lo)
                mask_free[0] = m
                if h + 1 < NH:
                    masks[h + 1] = load_mask(h + 1)
                qk_free = (tok,)

            def part_d(h):
                nonlocal v_free, s_free
                pe.wait(*v_ok[h])
                ys = []
                for t in range(2):
                    i, p = take_bank()
                    for jt in range(4):
                        a = (jt % 2) * 256 + t * 128
                        tok = mm3(p[:, :], GH[:, 4 + jt // 2, a:a + 128], GL[:, 4 + jt // 2, a:a + 128],
                                  GH[:, 6 + jt, :], GL[:, 6 + jt, :], jt == 0, jt == 3, s_ok[h][jt])
                    sq = add_ssq(p[:, :], S, t == 0, tok)
                    j, sg, sk = sg_ok[h][t]
                    yg = dve.do(lambda e, p=p, sg=sg: e.tensor_tensor(sg, p[:, :], sg, ALU.mult), sq, sk)
                    banks.give(i, yg)
                    ys.append((j, sg, yg))
                v_free = (tok,)
                s_free = (tok,)
                return h, ys

            def part_e(h, ys):
                r = rms_last(S)
                for t in range(2):
                    j, sg, yg = ys[t]
                    m = dve.do(lambda e, sg=sg: e.tensor_tensor(sg, STAT[:, :], sg, ALU.mult), r, yg)
                    ok = split(sg, *slot(10 + 2 * h + t), m, fourier_read)
                    scr.give(j, ok)
                    r_ok.append(ok)
                stat["free"] = (m,)

            part_a(0)
            part_b(0)
            part_c(0)
            for h in range(NH):
                if h + 1 < NH:
                    part_a(h + 1)
                d = part_d(h)
                if h + 1 == NH:
                    rms_first(S, 1)
                    gates.clear()
                    gate(48, 0)
                    part_e(*d)
                else:
                    part_b(h + 1, (lambda: rms_first(S, 1), lambda: part_e(*d)))
                    part_c(h + 1)

            gread = v_free + qk_free + s_free
            mg_ok = []
            for n in range(8):
                i, p = take_bank()
                if n:
                    gate(48, n)
                tok = lin(8, lambda k, n=n: ("w_ret", l, k * 128, n * 128), lambda k: slot(10 + k), S, p[:, :], r_ok)
                j, sg, sk = gates[n]
                dve.do(lambda e, p=p, sg=sg: e.tensor_tensor(sg, p[:, :], sg, ALU.mult), tok, sk)
                ev = (dve.sem, dve.count)
                banks.give(i, ev)
                ad = dve.do(lambda e, sg=sg, n=n: e.tensor_tensor(sg, sg, Z[:, n, :], ALU.add), ev, m1_ok[n])
                ok = split(sg, *slot(n), ad, *gread)
                scr.give(j, ok)
                mg_ok.append(ok)
            state["h_free"] = (tok,)
            state["z_free"] = (ad,)
            gtok = need("ada", l, 2)
            for n in range(8):
                i, p = take_bank()
                tok = lin(8, lambda k, n=n: ("w_out", l, k * 128, n * 128), slot, S, p[:, :], mg_ok)
                ev = dve.do(lambda e, n=n, p=p: e.scalar_tensor_tensor(
                    out=X[:, n, :], in0=p[:, :], scalar=MOD[:, l, 16 + n:17 + n], in1=X[:, n, :], op0=ALU.mult, op1=ALU.add),
                    tok, gtok, x_ready)
                banks.give(i, ev)
                add_ssq(X[:, n, :], S, n == 0, ev)
            state["x"] = ev
            state["g_free"] = (tok,)

        def conv_ffn(l, behind=None):
            need("ada", l, 3)
            mtok = need("ada", l, 4)
            ab = dve.do(lambda e: e.scalar_tensor_tensor(out=AB[:, :], in0=MOD[:, l, 32:40], scalar=1.0, in1=par("n2", l * 8, 8),
                                                         op0=ALU.add, op1=ALU.mult), mtok, *state["ab_free"])
            r = rms(S, 0)
            h_ok = affine(lambda t: X[:, t, :], lambda t: (HH[:, t, :], HL[:, t, :]), lambda t: AB[:, t:t + 1],
                          lambda t: MOD[:, l, 24 + t:25 + t], S, r, ab, state["x"], mtok, *state["h_free"])
            state["ab_free"] = (h_ok[-1],)
            if behind:
                background.append(behind)
            for half in range(2):
                hid = []
                for jj in range(11):
                    j0 = half * 11 + jj
                    t2 = []
                    if j0 == 0:
                        pair = [take_bank(), take_bank()]
                        tok2 = lin2([lambda k, c=c: ("ffn_up", l, k * 128, c * 128) for c in (0, 22)], hx(),
                                    [q[1][:, :] for q in pair], h_ok)
                    for c in (j0, 22 + j0):
                        if j0 == 0:
                            (i, p), tok = pair[c // 22], tok2
                        else:
                            i, p = take_bank()
                            tok = lin(8, lambda k, c=c: ("ffn_up", l, k * 128, c * 128), hx(), S, p[:, :])
                        h_read = tok
                        m, T = take_scr(act)
                        cw = lambda tap, c=c: par("cw", (l * 3 + tap) * 44 + c)
                        a = act.do(lambda e, T=T, p=p, c=c, cw=cw: e.activation(T, p[:, :], ACT.Identity, scale=cw(1), bias=par("cb", l * 44 + c)), tok)
                        b1 = dve.do(lambda e, T=T, p=p, cw=cw: e.scalar_tensor_tensor(
                            out=T[:, 1:S], in0=p[:, 0:S - 1], scalar=cw(0), in1=T[:, 1:S], op0=ALU.mult, op1=ALU.add), a)
                        b2 = dve.do(lambda e, T=T, p=p, cw=cw: e.scalar_tensor_tensor(
                            out=T[:, 0:S - 1], in0=p[:, 1:S], scalar=cw(2), in1=T[:, 0:S - 1], op0=ALU.mult, op1=ALU.add), b1)
                        banks.give(i, b2)
                        if c == j0:
                            b2 = act.do(lambda e, T=T: e.activation(T, T, ACT.Gelu), b2)
                        t2.append((m, T, b2))
                    (m1, A, ka), (m2, B, kb) = t2
                    hm = dve.do(lambda e, A=A, B=B: e.tensor_tensor(B, A, B, ALU.mult), ka, kb)
                    ok = split(B, *slot(jj), hm, *state["g_free"])
                    scr.give(m1, hm)
                    scr.give(m2, ok)
                    hid.append(ok)
                if half == 1:
                    state["h_free"] = (h_read,)
                if half:
                    drain()
                gtok = need("ada", l, 5)
                for n in range(8):
                    i, p = take_bank()
                    tok = lin(11, lambda k, n=n: ("ffn_down", l, (half * 11 + k) * 128, n * 128), slot, S, p[:, :], hid)
                    ev = dve.do(lambda e, n=n, p=p: e.scalar_tensor_tensor(
                        out=X[:, n, :], in0=p[:, :], scalar=MOD[:, l, 40 + n:41 + n], in1=X[:, n, :], op0=ALU.mult, op1=ALU.add),
                        tok, gtok, state["x"])
                    banks.give(i, ev)
                    if half:
                        add_ssq(X[:, n, :], S, n == 0, ev)
                state["x"] = ev
                state["g_free"] = (tok,)

        for t in range(DT):
            i, sq = (0, SSQ[:, :]) if t == 0 else take_scr(act)
            a = act.do(lambda e, t=t, sq=sq: e.activation(sq, X[:, t, :], ACT.Square), x_ok)
            if t:
                ssq["ok"] = pool.do(lambda e, sq=sq: e.tensor_tensor(SSQ[:, :], SSQ[:, :], sq, ALU.add), a, ssq["ok"])
                scr.give(i, ssq["ok"])
            else:
                ssq["ok"] = a
        xc = lambda t: TAB[:, t * 256:t * 256 + 256]
        xx = lambda t: X[:, t, :]
        zx = lambda t: Z[:, t, :]
        hx_to = lambda t: (HH[:, t, :], HL[:, t, :])
        hcs = lambda t: (GH[:, 14 + t // 2, (t % 2) * 256:(t % 2) * 256 + 256], GL[:, 14 + t // 2, (t % 2) * 256:(t % 2) * 256 + 256])

        def ada_norm(j, col, src, dst, n, oks, *waits):
            need("mod", 0, 3 * j)
            mtok = need("mod", 0, 3 * j + 1)
            ab = dve.do(lambda e: e.scalar_tensor_tensor(out=AB[:, :], in0=MOD2[:, 24 * j + 8:24 * j + 16, col], scalar=1.0,
                                                         in1=par("npre", j * 8, 8), op0=ALU.add, op1=ALU.mult), mtok, *state["ab_free"])
            rms_first(n, 0)
            yield
            r = rms_last(n)
            yield
            yield from affine_steps(src, dst, lambda t: AB[:, t:t + 1], lambda t: MOD2[:, 24 * j + t, col:col + 1], n, r, oks,
                                    ab, mtok, *waits)
            state["ab_free"] = (oks[-1],)

        def ada_out(j, col, res_w, zt, xt, n, z_ok, x_toks, oks, more=True):
            mtok = need("mod", 0, 3 * j + 2)
            rc = dve.do(lambda e: e.scalar_tensor_tensor(out=RC[:, :], in0=MOD2[:, 24 * j + 16:24 * j + 24, col], scalar=res_w,
                                                         in1=par("npost", j * 8, 8), op0=ALU.mult, op1=ALU.mult),
                        mtok, *state.get("rc_free", ()))
            rms_first(n, 0)
            yield
            r = rms_last(n)
            yield
            for t in range(DT):
                i, T = take_scr(dve)
                T = T[:, 0:n]
                m = dve.do(lambda e, t=t, T=T: e.scalar_tensor_tensor(out=T, in0=zt(t), scalar=RC[:, t:t + 1], in1=STAT[:, 0:n],
                                                                      op0=ALU.mult, op1=ALU.mult), r, rc, z_ok)
                q = pool if t % 2 == 0 else dve
                ev = q.do(lambda e, t=t, T=T: e.tensor_tensor(xt(t), xt(t), T, ALU.add), m, *x_toks)
                scr.give(i, ev)
                oks.append(ev)
                if more and t:
                    add_ssq(xt(t - 1), n, t == 1, oks[t - 1])
                if t == DT - 1:
                    stat["free"] = (m,)
                    state["rc_free"] = (m,)
                    if more:
                        add_ssq(xt(t), n, False, ev)
                yield

        def context_norm(g_free, oks):
            sp.wait(*g_free)
            for t in range(DT):
                sp.ops.append(lambda e, t=t: e.dma_start(xc(t), cT[t]).then_inc(s_x, 16))
            xc_ok = (s_x, 32 * DT)
            yield
            yield
            for t in range(DT):
                add_ssq(xc(t), C, t == 0, xc_ok)
                if t % 2:
                    yield
            yield from ada_norm(0, 1, xc, hcs, C, oks, xc_ok, *g_free)

        def closing_norm(oks):
            rms_first(S, 0)
            yield
            r = rms_last(S)
            yield
            for t in range(DT):
                ev = dve.do(lambda e, t=t: e.scalar_tensor_tensor(out=X[:, t, :], in0=X[:, t, :], scalar=par("fing", t), in1=STAT[:, :],
                                                                  op0=ALU.mult, op1=ALU.mult), r, *x_free)
                if t == DT - 1:
                    stat["free"] = (ev,)
                    state["x"] = ev
                add_ssq(xx(t), S, t == 0, ev, q=pool if t % 2 else dve)
                yield
            yield from ada_norm(0, 0, xx, hx_to, S, oks, state["x"], *state["h_free"])

        hc_ok = []
        for l in range(2):
            token_mix(l)
            conv_ffn(l, context_norm(state["g_free"], hc_ok) if l else None)
        x_free = (state["x"], ssq["ok"])
        need("mod", 0, 8)
        st1.close()

        GC = sb("GC", [128, 10, GATE_ROWS])
        DV = sb("DV", [128, 8])
        st2 = ctx.enter_context(ExitStack())
        ZC = sb("ZC", [128, DT, C], stack=st2)
        zc = lambda t: ZC[:, t, :]
        old = ((pe.sem, pe.count), (dve.sem, dve.count), (act.sem, act.count))

        def swiglu(f, half, n, zt, mov, h_ok, *waits):
            hid = []
            for jj in range(11):
                j0 = half * 11 + jj
                i0, p0 = take_bank()
                if h_ok:
                    i1, p1 = take_bank()
                    tok2 = tok = lin2([lambda k, c=c: ("ffn_w_in", f, k * 128, c * 128) for c in (j0, 22 + j0)], mov,
                                      [p0[:, 0:n], p1[:, 0:n]], h_ok)
                else:
                    tok = lin(8, lambda k: ("ffn_w_in", f, k * 128, j0 * 128), mov, n, p0[:, 0:n])
                m, T = take_scr(act)
                T = T[:, 0:n]
                a = act.do(lambda e, T=T, p0=p0: e.activation(T, p0[:, 0:n], ACT.Silu), tok)
                banks.give(i0, a)
                if not h_ok:
                    i1, p1 = take_bank()
                    tok = lin(8, lambda k: ("ffn_w_in", f, k * 128, (22 + j0) * 128), mov, n, p1[:, 0:n])
                h_ok = None
                h_read = tok
                hm = dve.do(lambda e, T=T, p1=p1: e.tensor_tensor(T, p1[:, 0:n], T, ALU.mult), tok, a)
                banks.give(i1, hm)
                ok = split(T, *slot(jj, n), hm, *state["g_free"])
                scr.give(m, ok)
                hid.append(ok)
            if half:
                drain()
            for nn in range(8):
                i, p = take_bank()
                tok = lin(11, lambda k, nn=nn: ("ffn_w_out", f, (half * 11 + k) * 128, nn * 128), lambda k: slot(k, n), n,
                          p[:, 0:n], hid)
                z = zt(nn)
                if half == 0:
                    ev = act.do(lambda e, z=z, p=p: e.activation(z, p[:, 0:n], ACT.Copy), tok, *waits)
                else:
                    ev = dve.do(lambda e, z=z, p=p: e.tensor_tensor(z, p[:, 0:n], z, ALU.add), tok, *waits)
                    add_ssq(z, n, nn == 0, ev)
                banks.give(i, ev)
            state["g_free"] = (tok,)
            return ev, h_read

        def swiglu_x(f, h_ok, *waits):
            z_ok, _ = swiglu(f, 0, S, zx, hx(), h_ok, *waits)
            z_ok, h_read = swiglu(f, 1, S, zx, hx(), None, z_ok)
            state["h_free"] = (h_read,)
            return z_ok

        h_ok = []
        background.append(closing_norm(h_ok))
        zc_ok, _ = swiglu(0, 0, C, zc, hcs, hc_ok, *old)
        drain()
        z_ok = swiglu_x(0, h_ok, *state["z_free"])
        h_ok, x_oks = [], []

        def x_norms():
            yield from ada_out(0, 0, 0.5, zx, xx, S, z_ok, (state["x"],), x_oks)
            yield from ada_norm(1, 0, xx, hx_to, S, h_ok, *x_oks[-2:], *state["h_free"])

        background.append(x_norms())
        zc_ok, hc_read = swiglu(0, 1, C, zc, hcs, None, zc_ok)
        x_toks = tuple(x_oks[-2:])
        hc_ok, c_oks = [], []

        def context_norms():
            yield from ada_out(0, 1, 0.5, zc, xc, C, zc_ok, (), c_oks)
            yield from ada_norm(1, 1, xc, hcs, C, hc_ok, *c_oks[-2:], hc_read)

        background.append(context_norms())
        so_ok = []
        pe.wait(h_ok[-1])
        for h in range(NH):
            i, p = take_bank()
            tok = lin(8, lambda k: ("w_in2", 0, k * 128, 1024 + h * 128), hx(), S, p[:, :])
            for _ in range(5):
                tick()
            ok = act.do(lambda e, p=p, h=h: e.activation(Z[:, h, :], p[:, :], ACT.Sigmoid), tok, *x_toks)
            banks.give(i, ok)
            so_ok.append(ok)
        drain()
        sp.wait(hc_ok[-1])
        sp.ops.append(lambda e: e.dma_start(SEL, sel_d).then_inc(s_rope, 16))
        sp.ops.append(lambda e: e.dma_start(TAB[:, 1024:1280], consts[:, 4992:5248]).then_inc(s_rope, 16))
        sel_ok = (s_rope, 48)
        st2.close()
        GT = sb("GT", [GATE_ROWS, 4, 768])
        old = old + ((pe.sem, pe.count), (dve.sem, dve.count), (act.sem, act.count), (pool.sem, pool.count))
        pe.wait(h_ok[-1], hc_ok[-1])
        g_free = state["g_free"]
        UH, UL = GHf[:, 0:3072], GLf[:, 0:3072]
        lat, con = slice(256, 768), slice(0, 256)

        u_ok = []
        for h in range(NH):
            ix, px = take_bank()
            ic, pc = take_bank()
            for k in range(8):
                wh, wl = st.block([("w_in2", 0, k * 128, h * 128)])
                mm3(px[:, :], wh, wl, HH[:, k, :], HL[:, k, :], k == 0, k == 7)
                tok = mm3(pc[:, 0:C], wh, wl, *hcs(k), k == 0, k == 7)
                st.done(tok)
            for p, i, n, cols in ((px, ix, S, lat), (pc, ic, C, con)):
                m, T = take_scr(act)
                cw = lambda tap, h=h: par("cw2", tap * 4 + h)
                a = act.do(lambda e, T=T, p=p, n=n, cw=cw, h=h: e.activation(
                    T[:, 0:n], p[:, 0:n], ACT.Identity, scale=cw(1), bias=par("cb2", h)), tok)
                b1 = dve.do(lambda e, T=T, p=p, n=n, cw=cw: e.scalar_tensor_tensor(
                    out=T[:, 1:n], in0=p[:, 0:n - 1], scalar=cw(0), in1=T[:, 1:n], op0=ALU.mult, op1=ALU.add), a)
                b2 = dve.do(lambda e, T=T, p=p, n=n, cw=cw: e.scalar_tensor_tensor(
                    out=T[:, 0:n - 1], in0=p[:, 1:n], scalar=cw(2), in1=T[:, 0:n - 1], op0=ALU.mult, op1=ALU.add), b1)
                banks.give(i, b2)
                sl = act.do(lambda e, T=T, n=n: e.activation(T[:, 0:n], T[:, 0:n], ACT.Silu), b2)
                a0 = h * 768 + cols.start
                ok = split(T[:, 0:n], UH[:, a0:a0 + n], UL[:, a0:a0 + n], sl, *g_free)
                scr.give(m, ok)
                u_ok.append(ok)

        st.close()
        bs = [(i, PS[i]) for i in banks.idle]
        banks.idle.clear()
        for k in range(8):
            wh, wl = st.block([("w_in2", 0, k * 128, 512 + q * 128) for q in range(4)])
            for c in range(6):
                if c < 2:
                    a, b = (x[:, c * 128:c * 128 + 128] for x in hcs(k))
                else:
                    a, b = HH[:, k, (c - 2) * 128:(c - 1) * 128], HL[:, k, (c - 2) * 128:(c - 1) * 128]
                if k == 0:
                    pe.wait(*banks.last[bs[c][0]])
                tok = mm3(bs[c][1][:, :], a, b, wh, wl, k == 0, k == 7)
            st.done(tok)
        v_ok = []
        for c in range(6):
            i, p = bs[c]
            ok = split(p[:, :], *slot(6 + c), tok, *g_free)
            banks.give(i, ok)
            v_ok.append(ok)
        mod_step()

        ix, px = take_bank()
        ic, pc = take_bank()
        for k in range(8):
            wh, wl = st.block([("gate", 0, k * 128, 0)])
            mm3(px[:, :], wh, wl, HH[:, k, :], HL[:, k, :], k == 0, k == 7)
            tok = mm3(pc[:, 0:C], wh, wl, *hcs(k), k == 0, k == 7)
            st.done(tok)
        hc_read = tok
        T0, T1, T2, T3 = (GT[:, i, :] for i in range(4))
        for T, base in ((T0, 0), (T1, 64)):
            for p, c0, n in ((px, 256, S), (pc, 0, C)):
                dve.do(lambda e, T=T, p=p, c0=c0, n=n, base=base: e.tensor_copy(T[0:32, c0:c0 + n], p[base:base + 32, 0:n]), tok, *old)
                cpy = dve.do(lambda e, T=T, p=p, c0=c0, n=n, base=base: e.tensor_copy(
                    T[32:36, c0:c0 + n], p[base + 32:base + 36, n - 1::-1] if n == S else p[base + 32:base + 36, C - 1::-1]))
        banks.give(ix, cpy)
        banks.give(ic, cpy)
        ib, fb = PAR[0:36, PCOLS["ib"]:PCOLS["ib"] + 1], PAR[0:36, PCOLS["fb"]:PCOLS["fb"] + 1]

        def gate_scans():
            dve.do(lambda e: e.tensor_scalar(T0, T0, ib, None, ALU.add), cpy)
            d1 = dve.do(lambda e: e.tensor_scalar(T1, T1, fb, None, ALU.add), cpy)
            d0 = dve.do(lambda e: e.memset(T3, 1.0))
            yield
            a1 = act.do(lambda e: e.activation(T2, T1, ACT.Abs), d1)
            a2 = act.do(lambda e: e.activation(T2, T2, ACT.Exp, scale=-1.0), a1)
            a3 = act.do(lambda e: e.activation(T2, T2, ACT.Ln, bias=1.0), a2)
            yield
            d2 = dve.do(lambda e: e.scalar_tensor_tensor(out=T1, in0=T1, scalar=0.0, in1=T2, op0=ALU.min, op1=ALU.subtract), a3)
            d3 = dve.do(lambda e: e.tensor_tensor_scan(T2, T3, T1, 0.0, ALU.mult, ALU.add), d2, d0)
            yield
            d4 = dve.do(lambda e: e.tensor_tensor(T0, T0, T2, ALU.subtract), d3)
            d5 = dve.do(lambda e: e.tensor_tensor_scan(T1, T3, T0, 0.0, ALU.mult, ALU.max), d4)
            yield
            d6 = dve.do(lambda e: e.tensor_tensor(T2, T2, T1, ALU.add), d5)
            yield
            dve.do(lambda e: e.tensor_copy(T3[0:32, :], T0[0:32, :]), d6)
            dve.do(lambda e: e.tensor_copy(T3[32:36, 0:256], T0[32:36, 255::-1]))
            d7 = dve.do(lambda e: e.tensor_copy(T3[32:36, 256:768], T0[32:36, 767:255:-1]))
            dve.do(lambda e: e.tensor_copy(T0[0:32, 256:768], T1[0:32, 256:768]), d7)
            d8 = dve.do(lambda e: e.tensor_copy(T0[32:36, 256:768], T1[32:36, 767:255:-1]), d7)
            yield
            dve.do(lambda e: e.tensor_copy(T1[0:32, 256:768], T2[0:32, 256:768]), d8)
            d9 = dve.do(lambda e: e.tensor_copy(T1[32:36, 256:768], T2[32:36, 767:255:-1]), d8)
            state["gates"] = (d7, d8, d9)
            yield

        st.close()
        bs = [take_bank() for _ in range(4)]
        scans = gate_scans()
        for k in range(8):
            next(scans, None)
            wh, wl = st.block([("w_in2", 0, k * 128, 1552 + q * 128) for q in range(4)])
            for c in range(4):
                tok = mm3(bs[c][1][:, :], HH[:, k, c * 128:c * 128 + 128], HL[:, k, c * 128:c * 128 + 128], wh, wl, k == 0, k == 7)
            st.done(tok)
        h_read = tok
        for _ in scans:
            pass
        d9 = state["gates"][2]
        pu_ok = []
        for c in range(4):
            i, p = bs[c]
            ok = split(p[:, :], *slot(14 + c), tok, hc_read)
            banks.give(i, ok)
            pu_ok.append(ok)
        st.close()
        pe.wait(*stat["free"], d9, con_ok)
        for c in range(10):
            src = T3[:, c * 128:c * 128 + 128] if c < 6 else T1[:, (c - 4) * 128:(c - 3) * 128]
            fn = lambda e, c=c, src=src: e.transpose(STAT[:, c * 36:c * 36 + 36], src, IDN[0:36, 0:36])
            if c < 9:
                pe.quiet(fn)
            else:
                tok = pe.do(fn)
        gc_ok = dve.do(lambda e: e.tensor_copy(GC[:, 0:6, :].rearrange("p a b -> p (a b)"), STAT[:, 0:216]), tok, *old)
        fc_ok = act.do(lambda e: e.activation(GC[:, 6:10, :].rearrange("p a b -> p (a b)"), STAT[:, 216:360], ACT.Exp, scale=-1.0),
                       gc_ok)
        stat["free"] = (fc_ok,)

        d_free = [(*g_free, hc_ok[-1])] * 2
        mix_ok = {}
        pend = []

        def pool_out(g, ok):
            i, p = take_bank()
            wh, wl = st.block([("pool_w", g, 0, 0)])
            tok = mm3(p[:, :], wh, wl, *slot(12 + g % 2), True, True, ok)
            st.done(tok)
            d_free[g % 2] = (tok,)
            mix_ok[4 + g] = split(p[:, :], HH[:, 4 + g, :], HL[:, 4 + g, :], tok, h_read, scale=par("ps", g))
            banks.give(i, mix_ok[4 + g])

        pe.wait(*pu_ok)
        for g in range(4):
            i, p = take_bank()
            for t in range(4):
                ph, pl = st.block([("poolm", g, t * 128, q * 128) for q in range(4)])
                tok = mm3(p[:, :], GH[:, 14 + t, g * 128:g * 128 + 128], GL[:, 14 + t, g * 128:g * 128 + 128], ph, pl, t == 0, t == 3)
                st.done(tok)
            pu_read = tok
            ok = split(p[:, :], *slot(12 + g % 2), tok, *d_free[g % 2])
            banks.give(i, ok)
            if pend:
                pool_out(*pend.pop())
            pend.append((g, ok))
            mod_step()
        pool_out(*pend.pop())
        st.close()

        q_free = d_free[0] + d_free[1]
        e_free = [(pu_read,)] * 4
        pe.wait(*u_ok, *v_ok)
        scale = 128.0 ** -0.5
        acc_free = [tuple(banks.last[i]) for i in range(4)]
        s_free = [tuple(banks.last[4]), tuple(banks.last[5])]
        pe.wait(sel_ok)
        DEN = PS[7]
        den_free = (pe.sem, pe.count), *mod_state["free"]
        cnt = {"s": 0, "e": 0, "q_free": q_free, "den_free": den_free, "dv_free": old, "sums_of": {}}
        mb_ok, mb_free, d_items, s_items, e_items = {}, {}, {}, {}, {}

        def span(c, d):
            j = c - 2
            return (0, S) if c < 2 else ((128 * j, S) if d == 0 else (0, 128 * (j + 1)))

        def kslot(h, c):
            a = h * 768 + c * 128
            return (UH[:, a:a + 128], UL[:, a:a + 128]) if c < 2 else \
                (GH[:, 13, (c - 2) * 128:(c - 1) * 128], GL[:, 13, (c - 2) * 128:(c - 1) * 128])

        def spread(row, d, h):
            pe.wait(*stat["free"])
            return pe.do(lambda e: e.matmul(STAT[:, :], SEL[:, (d * 4 + h) * 128:(d * 4 + h) * 128 + 128], row[:, 256:768], start=True, stop=True))

        def running_max(h, d):
            tok = spread(T0, d, h)
            dst = Z[:, 4 + 2 * (h % 2) + d, :]

            def rest():
                mb_ok[h, d] = act.do(lambda e: e.activation(dst, STAT[:, :], ACT.Copy), tok, *x_toks, *mb_free.get((h - 2, d), ()))
                stat["free"] = (mb_ok[h, d],)
            return rest

        def q_and_k(h, which, P, free):
            a0 = h * 768
            if which == 0:
                cnt["wq"] = st.block([("w_q", h, 0, 0)])
                w, n, cols, dst = cnt["wq"], S, slice(a0 + 256, a0 + 768), slot(12)
            elif which == 1:
                cnt["wk"] = st.block([("w_k", h, 0, 0)])
                w, n, cols, dst = cnt["wk"], S, slice(a0 + 256, a0 + 768), slot(13)
            else:
                w, n, cols = cnt["wk"], C, slice(a0, a0 + 256)
                dst = (UH[:, a0:a0 + 256], UL[:, a0:a0 + 256])
            tok = mm3(P[:, 0:n], w[0], w[1], UH[:, cols], UL[:, cols], True, True, *free)
            st.done(tok)
            return split(P[:, 0:n], *dst, tok, *cnt["q_free"], scale=None if which == 0 else scale)

        def q_and_k_in_scores(h, which):
            b = cnt["s"] % 2
            cnt["s"] += 1
            s_free[b] = (q_and_k(h, which, PS[4 + b], s_free[b]),)
            return s_free[b]

        def scores(h, c):
            b = cnt["s"] % 2
            cnt["s"] += 1
            tok = mm3(PS[4 + b][:, :], *kslot(h, c), *slot(12), True, True, *s_free[b])
            cnt["q_free"] = (tok,)
            s_items[h, c] = (b, tok)

        def weights(h, c):
            for d in range(2):
                lo, hi = span(c, d)
                n = hi - lo
                m, T = take_scr(dve)
                act.wait(*scr.last[m])
                T = T[:, 0:n]
                src = Z[:, 4 + 2 * (h % 2) + d, lo:hi]
                g = GC[:, c, 32 * d + h:32 * d + h + 1]
                rest = slice(0, n)
                if c >= 2:
                    dd, rest = (slice(0, 128), slice(128, n)) if d == 0 else (slice(n - 128, n), slice(0, n - 128))
                    g1 = dve.do(lambda e, T=T, src=src, g=g, dd=dd, d=d: e.scalar_tensor_tensor(
                        out=T[:, dd], in0=src[:, dd], scalar=g, in1=TRI[d], op0=ALU.subtract, op1=ALU.max),
                        mb_ok[h, d], gc_ok, sel_ok)
                if rest.stop > rest.start:
                    g2 = act.do(lambda e, T=T, src=src, g=g, rest=rest: e.activation(
                        T[:, rest], src[:, rest], ACT.Exp, scale=-1.0, bias=g), mb_ok[h, d], gc_ok)
                if c >= 2:
                    g2 = act.do(lambda e, T=T, dd=dd: e.activation(T[:, dd], T[:, dd], ACT.Exp, scale=-1.0), g1)
                mb_free[h, d] = (g2,)
                d_items[h, c, d] = (m, T, g2)

        def weigh(h, c):
            b, stok = s_items[h, c]
            mid = []
            for d in range(2):
                lo, hi = span(c, d)
                m, T, g2 = d_items[h, c, d]
                P = PS[4 + b]
                g3 = dve.do(lambda e, T=T, P=P, lo=lo, hi=hi: e.tensor_tensor(T, P[:, lo:hi], T, ALU.mult), g2, stok)
                mid.append(g3)
            s_free[b] = (g3,)
            for d in range(2):
                lo, hi = span(c, d)
                m, T, _ = d_items[h, c, d]
                es = cnt["e"] % 4
                cnt["e"] += 1
                eh, el = GH[:, 14 + es, 0:hi - lo], GL[:, 14 + es, 0:hi - lo]
                g4 = act.do(lambda e, T=T, eh=eh: e.activation(eh, T, ACT.Copy), mid[d], *e_free[es])
                g5 = pool.do(lambda e, T=T, eh=eh, el=el: e.tensor_tensor(el, T, eh.bitcast(F32), ALU.subtract), g4, *e_free[es])
                scr.give(m, g5)
                e_items[h, c, d] = (es, eh, el, g5)

        def sums(h, c):
            if c == 0:
                pe.wait(*acc_free[2 * (h % 2)], *acc_free[2 * (h % 2) + 1], *cnt["den_free"])
            for d in range(2):
                lo, hi = span(c, d)
                es, eh, el, g5 = e_items[h, c, d]
                va = (GH[:, 6 + c, h * 128:h * 128 + 128], GL[:, 6 + c, h * 128:h * 128 + 128])
                tok = mm3(PS[2 * (h % 2) + d][:, lo:hi], *va, eh, el, c == 0, c == 5, g5)
                for q in range(lo // 128, hi // 128):
                    o = DEN[:, 2 * (d * 4 + q):2 * (d * 4 + q) + 2]
                    a = q * 128 - lo
                    first = c == 0 and d == 0 and q == 0
                    pe.quiet(lambda e, o=o, w=eh[:, a:a + 128], f=first: e.matmul(
                        o, w, ONR[:, 0:2], start=f, stop=False, skip_group_check=True))
                    tok = pe.do(lambda e, o=o, w=el[:, a:a + 128]: e.matmul(
                        o, w, ONR[:, 0:2], start=False, stop=(c == 5), skip_group_check=True))
                e_free[es] = (tok,)
            cnt["sums"] = cnt["sums_of"][h] = tok

        def denominators(h):
            tok = cnt["sums"]
            a = act.do(lambda e: e.activation(DV[:, :], DEN[:, 0:16:2], ACT.Abs), tok, *cnt["dv_free"])
            cnt["den_free"] = (a,)
            dve.wait(fc_ok, con_ok)
            for d in range(2):
                x1 = dve.do(lambda e, d=d: e.tensor_tensor(DV[:, 4 * d:4 * d + 4], DV[:, 4 * d:4 * d + 4],
                                                           GC[:, 6:10, 32 * d + h], ALU.max), a)
            x2 = dve.do(lambda e: e.reciprocal(DV[:, :], DV[:, :]), x1)
            ds = []
            for d in range(2):
                m, T = take_scr(dve)
                for t in range(4):
                    dg = dve.do(lambda e, d=d, t=t, T=T: e.tensor_scalar(
                        T[:, t * 128:t * 128 + 128], IDN[:, :], DV[:, 4 * d + t:4 * d + t + 1], None, ALU.mult), x2)
                ds.append((m, T, dg))
            cnt["dv_free"] = (dg,)
            return ds

        def normalize(h, ds, d):
            m, T, dg = ds[d]
            pe.wait(*stat["free"])
            for t in range(4):
                bc = pe.do(lambda e, t=t: e.matmul(STAT[:, t * 128:t * 128 + 128], ONE[:, :], T[:, t * 128:t * 128 + 128],
                                                   start=True, stop=True), dg)

            def rest():
                r = act.do(lambda e: e.activation(T, STAT[:, :], ACT.Copy), bc)
                stat["free"] = (r,)
                b = 2 * (h % 2) + d
                x3 = dve.do(lambda e: e.tensor_tensor(T, PS[b][:, :], T, ALU.mult), r, cnt["sums_of"][h])
                acc_free[b] = (x3,)
                if d:
                    A = ds[0][1]
                    hh = dve.do(lambda e: e.tensor_tensor(A, A, T, ALU.add), x3)
                    scr.give(m, hh)
                    add_ssq(A, S, True, hh)
            return rest

        def head_norm(h, m0, A):
            r = rms_last(S)
            y1 = dve.do(lambda e: e.scalar_tensor_tensor(out=A, in0=A, scalar=par("hn", h), in1=STAT[:, :], op0=ALU.mult, op1=ALU.mult), r, ssq["ok"])
            stat["free"] = (y1,)
            y2 = dve.do(lambda e: e.tensor_tensor(A, A, Z[:, h, :], ALU.mult), y1, so_ok[h])
            mix_ok[h] = split(A, HH[:, h, :], HL[:, h, :], y2, h_read)
            scr.give(m0, mix_ok[h])
            return y2

        for d in range(2):
            running_max(0, d)()
        st.close()
        for part in range(3):
            qk_ok = q_and_k_in_scores(0, part)
        weights(0, 0)
        pe.wait(*qk_ok)
        scores(0, 0)
        for h in range(NH):
            more = h + 1 < NH
            for c in range(5):
                scores(h, c + 1)
                rest = None
                if c < 2 and h:
                    rest = normalize(h - 1, pending, c)
                elif 2 <= c < 4 and more:
                    rest = running_max(h + 1, c - 2)
                weights(h, c + 1)
                weigh(h, c)
                if rest:
                    rest()
                if c:
                    sums(h, c - 1)
                if c == 3 and h:
                    rms_first(S, 2)
                elif c == 4 and h:
                    y2 = head_norm(h - 1, *pending[0][0:2])
            weigh(h, 5)
            if more:
                stat["free"] = (q_and_k(h + 1, 0, STAT, stat["free"]),)
            sums(h, 4)
            if more:
                q_and_k_in_scores(h + 1, 1)
                qk_ok = q_and_k_in_scores(h + 1, 2)
                weights(h + 1, 0)
            sums(h, 5)
            pending = denominators(h)
            if more:
                pe.wait(*qk_ok)
                scores(h + 1, 0)
        tok = cnt["sums"]
        q_read = cnt["q_free"][0]
        state["g_free"] = (tok, q_read)
        banks.idle[:] = [0, 1, 4, 5, 2, 3]
        banks.last[0], banks.last[1] = acc_free[0:2]
        banks.last[4], banks.last[5] = s_free
        others = (0, 1, 2, 4, 5, 6, 7)
        early = []

        def early_tile(nn):
            i, p = take_bank()
            for k in others:
                pe.wait(mix_ok[k])
                wh, wl = st.block([("w_out2", 0, k * 128, nn * 128)])
                st.done(mm3(p[:, :], wh, wl, HH[:, k, :], HL[:, k, :], k == 0, False))
            early.append((nn, i, p))

        def finish(nn, i, p, tok, *waits):
            ev = act.do(lambda e: e.activation(Z[:, nn, :], p[:, :], ACT.Copy), tok, *waits)
            add_ssq(Z[:, nn, :], S, nn == 0, ev)
            banks.give(i, ssq["ok"])
            return ev

        early_tile(0)
        for d in range(2):
            rest = normalize(NH - 1, pending, d)
            rest()
            early_tile(1 + d)
        banks.last[2], banks.last[3] = acc_free[2:4]
        rms_first(S, 2)
        early_tile(3)
        y2 = head_norm(NH - 1, *pending[0][0:2])
        for nn, i, p in early:
            wh, wl = st.block([("w_out2", 0, 3 * 128, nn * 128)])
            tok = mm3(p[:, :], wh, wl, HH[:, 3, :], HL[:, 3, :], False, True, mix_ok[3])
            st.done(tok)
            ev = finish(nn, i, p, tok, y2)
        for nn in range(4, 8):
            i, p = take_bank()
            tok = lin(8, lambda k, nn=nn: ("w_out2", 0, k * 128, nn * 128), hx(), S, p[:, :])
            ev = finish(nn, i, p, tok)
        state["h_free"] = (tok,)
        h_ok, x_oks = [], []
        for _ in ada_out(1, 0, 1.0, zx, xx, S, ev, x_toks, x_oks):
            pass
        x_toks = x_oks[-2:]
        for _ in ada_norm(2, 0, xx, hx_to, S, h_ok, *x_toks, *state["h_free"]):
            pass
        z_ok = swiglu_x(1, h_ok, *x_toks)
        x_oks = []
        for _ in ada_out(2, 0, 0.5, zx, xx, S, z_ok, x_toks, x_oks, more=False):
            pass
        for t in range(DT):
            sp.wait(x_oks[t])
            sp.ops.append(lambda e, t=t: e.dma_start(out[t], X[:, t, :]).then_inc(s_out, 16))
        sp.wait((s_out, 16 * DT))

        if dry:
            return
        block = ctx.enter_context(nc.Block())

        @block.sync
        def _(e):
            sp.run(e)

        @block.tensor
        def _(e):
            pe.run(e)

        @block.scalar
        def _(e):
            act.run(e)

        @block.vector
        def _(e):
            dve.run(e)

        @block.gpsimd
        def _(e):
            pool.run(e)


def constants():
    c = np.zeros((128, 5248), np.float32)
    c[:, 0:128] = np.eye(128)
    i = np.arange(128)
    ang = 2 * np.pi * ((i[:, None] * i[None, :]) % 128) / 128
    c[:, 128:256] = np.cos(ang) / 256
    c[:, 256:384] = np.sin(ang) / 256
    inv = np.float32(10000.0) ** (-np.arange(128, dtype=np.float32) / np.float32(128))
    ang = (np.arange(512, dtype=np.float32)[None, :] * inv.astype(np.float32)[:, None]).astype(np.float64)
    c[:, 384:896] = np.cos(ang)
    c[:, 896:1408] = np.sin(ang)
    d = np.arange(896)[None, :] - 384 - np.arange(128)[:, None]
    for h in range(4):
        gf = 1 - 2.0 ** -(5.0 + h)
        gb = 1 - 2.0 ** -(5.5 + h)
        c[:, 1408 + h * 896:1408 + (h + 1) * 896] = np.where(d >= 0, gf ** np.abs(d), gb ** np.abs(d)) / 16
    c[:, 4992:5120] = np.where(i[:, None] <= i[None, :], 0, 1e4)
    c[:, 5120:5248] = np.where(i[:, None] >= i[None, :], 0, 1e4)
    sel = np.zeros((GATE_ROWS, 8, 128), np.float32)
    for d2 in range(2):
        for h in range(4):
            sel[32 * d2 + h, d2 * 4 + h] = 1
    j = np.arange(512)
    ph = 2 * np.pi * ((j[:256, None] * j[None, :]) % 512) / 512
    dft = np.zeros((512, 512))
    dft[:256] = np.cos(ph)
    dft[256:] = -np.sin(ph)
    dft[256] = np.where(j % 2 == 0, 1, -1)
    poolm = np.zeros((4, 512, 512))
    for g, win in enumerate((2, 4, 8, 16)):
        def mean(n):
            m = np.zeros((n, n))
            lo, hi = win // 2, win - 1 - win // 2
            for t in range(n):
                a, b = max(t - lo, 0), min(t + hi, n - 1)
                m[t, a:b + 1] = 1.0 / (b - a + 1)
            return m
        poolm[g] = (np.kron(mean(8), mean(64)) - np.eye(512)).T
    return c, sel.reshape(GATE_ROWS, 1024), dft.astype(np.float32), poolm.astype(np.float32)


def kernel(x, c, norm1_g, norm2_g, ada_w, ada_b, w_in, w_fourier, w_ret, w_out, ffn_up, conv_w, conv_b,
           ffn_down, final_g, c_2, ctx_2, c_ctx_2, w_mod_2, b_mod_2, norm_pre_2, norm_post_2,
           ffn_w_in_2, ffn_w_out_2, w_in_2, w_out_2, conv_w_2, conv_b_2, w_q_2, w_k_2, i_bias_2,
           f_bias_2, head_norm_2, pool_w_2, pool_scale_2):
    import concourse.bacc as bacc
    from concourse.bass_utils import run_bass_kernel_spmd

    A = lambda a: np.ascontiguousarray(a)
    consts, sel, dft, poolm = constants()
    gate = np.zeros((1024, 128), np.float32)
    w2 = A(w_in_2)[0]
    for q in range(4):
        gate[:, 32 * q:32 * q + 4] = w2[:, 1536 + 4 * q:1540 + 4 * q]
    P = np.zeros((128, NP), np.float32)

    def put(name, a, at=0):
        a = A(a)
        P[:, PCOLS[name] + at:PCOLS[name] + at + a.shape[1]] = a

    cols = lambda a: A(a).reshape(-1, 128).T
    put("c", cols(c))
    put("c2", np.stack([cols(c_2), cols(c_ctx_2)], 2).reshape(128, 16))
    put("n1", cols(norm1_g))
    put("n2", cols(norm2_g))
    put("adab", cols(ada_b))
    put("fing", cols(final_g))
    put("bmod", np.repeat(cols(b_mod_2), 2, axis=1))
    put("npre", cols(norm_pre_2))
    put("npost", cols(norm_post_2))
    put("cw", cols(conv_w))
    put("cb", cols(conv_b))
    put("cw2", cols(conv_w_2))
    put("cb2", cols(conv_b_2))
    put("hn", cols(head_norm_2))
    put("ps", cols(pool_scale_2))
    for d in range(2):
        P[32 * d:32 * d + 4, PCOLS["ib"]] = A(i_bias_2)[0, d]
        P[32 * d:32 * d + 4, PCOLS["fb"]] = A(f_bias_2)[0, d]

    src = {"w_in": A(w_in), "w_fourier": A(w_fourier), "w_ret": A(w_ret), "w_out": A(w_out), "ffn_up": A(ffn_up),
           "ffn_down": A(ffn_down), "ada_w": A(ada_w), "w_mod": A(w_mod_2), "ffn_w_in": A(ffn_w_in_2)[0],
           "ffn_w_out": A(ffn_w_out_2)[0], "w_in2": A(w_in_2), "w_out2": A(w_out_2), "w_q": A(w_q_2)[0],
           "w_k": A(w_k_2)[0], "pool_w": A(pool_w_2)[0], "gate": gate[None], "dft": dft[None], "poolm": poolm}

    mods = [("ada_w", l, v) for l in range(2) for v in range(6)] + [("w_mod", 0, v) for v in range(9)]

    def build(chunks, dry):
        nc = bacc.Bacc("TRN2", target_bir_lowering=False, num_devices=1, dynamic_dma_scratch_size=1024)
        n = max(len(chunks), 1)
        ins = {"ws": (n, 128, 1024), "wm": (len(mods) * 8, 128, 1024), "xT": (8, 128, S), "cT": (8, 128, C), "params": (128, NP),
               "consts": consts.shape, "sel": sel.shape}
        t = {k: nc.dram_tensor(k, v, F32, kind="ExternalInput").ap() for k, v in ins.items()}
        out = nc.dram_tensor("out", (8, 128, S), F32, kind="ExternalOutput").ap()
        program(nc, t["ws"], t["wm"], t["xT"], t["cT"], t["params"], t["consts"], t["sel"], out, chunks, dry)
        return nc

    chunks = []
    build(chunks, True)
    nc = build(chunks, False)
    ws = np.zeros((len(chunks), 128, 1024), np.float32)
    for i, specs in enumerate(chunks):
        for b, (name, l, r, q) in enumerate(specs):
            ws[i, :, b * 128:b * 128 + 128] = src[name][l, r:r + 128, q:q + 128]
    wm = np.empty((len(mods), 2, 4, 128, 2, 512), np.float32)
    for i, (name, l, v) in enumerate(mods):
        w = src[name][l, :, v * 1024:(v + 1) * 1024].reshape(4, 2, 128, 2, 512)
        wm[i] = w.transpose(3, 0, 2, 1, 4)
    wm = wm.reshape(len(mods) * 8, 128, 1024)
    arrays = {"ws": ws, "wm": wm, "xT": A(A(x)[0].T).reshape(8, 128, S), "cT": A(A(ctx_2)[0].T).reshape(8, 128, C),
              "params": P, "consts": consts, "sel": sel}
    r = run_bass_kernel_spmd(nc, [arrays], core_ids=[0])
    o = r.results[0]["out"]
    return A(o.reshape(D, S).T).reshape(1, S, D)
```
